# Optimizing a Trainium2 kernel written in Bass

```python
import math
import jax, jax.numpy as jnp
from jax import lax
import numpy as np

D_MODEL = 1024
BATCH = 1
SEQ = 128
DEPTH = 2
DEC_BATCH = 1
DEC_SEQ = 256
PAST_LEN = 128

GRID_W = 64
EPS = 1e-6
ROPE_BASE = 10000.0
N_EVEN = (DEPTH + 1) // 2
N_ODD = DEPTH // 2
DA_HEADS = 4
DA_DIM = 64
DA_WIDTH = DA_HEADS * 2 * DA_DIM
Q_BLOCK = 128
GLA_HEADS = 4
GLA_DK = 64
GLA_DV = 128
GLA_WIDTH = GLA_HEADS * GLA_DV
GLA_GATE_RANK = 16
GLA_TAU = 16.0
GLA_CHUNK = 64
MIX_WIDTH = DA_WIDTH + GLA_WIDTH
IN0_WIDTHS = (2 * DA_HEADS * DA_DIM, 2 * DA_HEADS * DA_DIM, DA_HEADS * 2 * DA_DIM,
              GLA_HEADS * GLA_DK, GLA_HEADS * GLA_DK, GLA_HEADS * GLA_DV, GLA_HEADS * GLA_DV,
              2 * GLA_GATE_RANK)
IN0_WIDTH = sum(IN0_WIDTHS)
S5_GROUP_CH = 16
S5_GROUPS = D_MODEL // S5_GROUP_CH
S5_P = 64
PEER_HEADS = 8
PEER_NKEYS = 128
PEER_N = PEER_NKEYS * PEER_NKEYS
PEER_QDIM = 256
PEER_TOPK = 16
PEER_TOKEN_BLOCK = 128

kernel_name = "hybrid_diffusion_prefix_step"

F32 = jnp.float32

def rms_norm(x, g):
    xf = x.astype(F32)
    y = xf * lax.rsqrt(jnp.mean(xf * xf, axis=-1, keepdims=True) + EPS)
    return (y * g.astype(F32)).astype(x.dtype)

def split_cols(x, widths):
    out, start = [], 0
    for w in widths:
        out.append(x[..., start:start + w])
        start += w
    return out

def lambda_init(layer):
    return 0.8 - 0.6 * math.exp(-0.3 * layer)

def axial_rope(length, dim):
    rows = length // GRID_W
    row_id = jnp.repeat(jnp.arange(rows), GRID_W).astype(F32)
    col_id = jnp.tile(jnp.arange(GRID_W), rows).astype(F32)
    quarter = dim // 4
    inv = ROPE_BASE ** (-jnp.arange(quarter, dtype=F32) / quarter)
    ang_r = row_id[:, None] * inv
    ang_c = col_id[:, None] * inv
    ang = jnp.concatenate([ang_r, ang_r, ang_c, ang_c], axis=-1)
    return jnp.cos(ang), jnp.sin(ang)

def apply_rope(x, cos, sin):
    xf = x.astype(F32)
    xr = xf.reshape(xf.shape[:-1] + (2, 2, xf.shape[-1] // 4))
    rot = jnp.concatenate([-xr[..., 1:, :], xr[..., :1, :]], axis=-2).reshape(xf.shape)
    return (xf * cos[:, None] + rot * sin[:, None]).astype(x.dtype)

def diff_attention(q, k, v, lam, lam_init, subln_g):
    B, Lq = q.shape[:2]
    Lk = k.shape[1]
    qb = q.reshape(B, Lq // Q_BLOCK, Q_BLOCK, DA_HEADS, 2, DA_DIM)
    qb = jnp.moveaxis(qb, 1, 0)
    kk = k.reshape(B, Lk, DA_HEADS, 2, DA_DIM)
    scale = DA_DIM ** -0.5

    def block(qblk):
        s = jnp.einsum('bqhmd,bkhmd->bhmqk', qblk, kk).astype(F32) * scale
        p = jax.nn.softmax(s, axis=-1)
        a = p[:, :, 0] - lam * p[:, :, 1]
        return jnp.einsum('bhqk,bkhe->bqhe', a.astype(v.dtype), v)

    o = lax.map(block, qb)
    o = jnp.moveaxis(o, 0, 1).reshape(B, Lq, DA_HEADS, 2 * DA_DIM)
    o = rms_norm(o, subln_g) * (1.0 - lam_init)
    return o.reshape(B, Lq, DA_WIDTH)

def gla_chunked(q, k, v, log_a, s0):
    B, L = q.shape[:2]
    n = L // GLA_CHUNK

    def to_chunks(t):
        return jnp.moveaxis(t.reshape((B, n, GLA_CHUNK) + t.shape[2:]), 1, 0)

    qc, kc, vc, gc = to_chunks(q), to_chunks(k), to_chunks(v), to_chunks(log_a)
    mask = jnp.tril(jnp.ones((GLA_CHUNK, GLA_CHUNK), dtype=bool))

    def step(s, inp):
        qi, ki, vi, gi = inp
        b = jnp.cumsum(gi, axis=1)
        kf = ki.astype(F32)
        vf = vi.astype(F32)
        q_dec = qi.astype(F32) * jnp.exp(b)
        k_inv = kf * jnp.exp(-b)
        inter = jnp.einsum('bchk,bhkv->bchv', q_dec, s)
        att = jnp.where(mask, jnp.einsum('bchk,bshk->bhcs', q_dec, k_inv), 0.0)
        intra = jnp.einsum('bhcs,bshv->bchv', att, vf)
        b_last = b[:, -1]
        k_end = kf * jnp.exp(b_last[:, None] - b)
        s_new = jnp.exp(b_last)[..., None] * s + jnp.einsum('bchk,bchv->bhkv', k_end, vf)
        return s_new, inter + intra

    s_final, o = lax.scan(step, s0, (qc, kc, vc, gc))
    o = jnp.moveaxis(o, 0, 1).reshape(B, L, GLA_HEADS, GLA_DV)
    return o, s_final

def even_mixer(h, w_in, w_out, da_lam, lam_init, subln_g, gate_up, gate_bias, gla_norm_g, rope, ctx):
    B, L, _ = h.shape
    q_da, k_da, v_da, q_g, k_g, v_g, r_g, g_low = split_cols(h @ w_in, IN0_WIDTHS)
    q_da = q_da.reshape(B, L, 2 * DA_HEADS, DA_DIM)
    k_da = k_da.reshape(B, L, 2 * DA_HEADS, DA_DIM)
    v_da = v_da.reshape(B, L, DA_HEADS, 2 * DA_DIM)
    if rope is not None:
        q_da = apply_rope(q_da, *rope)
        k_da = apply_rope(k_da, *rope)
    lf = da_lam.astype(F32)
    lam = jnp.exp(jnp.sum(lf[0] * lf[1])) - jnp.exp(jnp.sum(lf[2] * lf[3])) + lam_init
    if ctx is None:
        k_keys, v_keys = k_da, v_da
        s0 = jnp.zeros((2, B, GLA_HEADS, GLA_DK, GLA_DV), F32)
    else:
        k_ctx, v_ctx, s_ctx = ctx
        k_keys = jnp.concatenate([k_da, k_ctx.astype(k_da.dtype)], axis=1)
        v_keys = jnp.concatenate([v_da, v_ctx.astype(v_da.dtype)], axis=1)
        s0 = jnp.moveaxis(s_ctx.astype(F32), 1, 0)
    o_da = diff_attention(q_da, k_keys, v_keys, lam, lam_init, subln_g)

    q_g = q_g.reshape(B, L, GLA_HEADS, GLA_DK) * (GLA_DK ** -0.5)
    k_g = k_g.reshape(B, L, GLA_HEADS, GLA_DK)
    v_g = v_g.reshape(B, L, GLA_HEADS, GLA_DV)
    low = g_low.reshape(B, L, 2, GLA_GATE_RANK)
    z = (jnp.einsum('bldr,drk->bldk', low, gate_up) + gate_bias).astype(F32)
    log_a = (jax.nn.log_sigmoid(z) / GLA_TAU).reshape(B, L, 2, GLA_HEADS, GLA_DK)
    o_f, s_f = gla_chunked(q_g, k_g, v_g, log_a[:, :, 0], s0[0])
    flip = lambda t: jnp.flip(t, axis=1)
    o_b, s_b = gla_chunked(flip(q_g), flip(k_g), flip(v_g), flip(log_a[:, :, 1]), s0[1])
    o_g = rms_norm(o_f + flip(o_b), gla_norm_g).astype(h.dtype)
    o_g = o_g * jax.nn.silu(r_g.reshape(B, L, GLA_HEADS, GLA_DV))
    out = jnp.concatenate([o_da, o_g.reshape(B, L, GLA_WIDTH)], axis=-1) @ w_out
    return out, (k_da, v_da, jnp.stack([s_f, s_b], axis=1))

def s5_scan(u, lam_bar, b_bar, h0):
    bu = jnp.einsum('gpc,blgc->blgp', b_bar, u.astype(jnp.complex64))
    bu = bu.at[:, 0].add(lam_bar * h0)
    a = jnp.broadcast_to(lam_bar, bu.shape)

    def combine(x, y):
        a1, b1 = x
        a2, b2 = y
        return a1 * a2, a2 * b1 + b2

    _, states = lax.associative_scan(combine, (a, bu), axis=1)
    return states

def s5_mixer(h, w_in, a_re, a_im, log_dt, b_re, b_im, c_re, c_im, d_skip, w_out, h0):
    B, L, _ = h.shape
    u = (h @ w_in).astype(F32)
    ug = u.reshape(B, L, S5_GROUPS, S5_GROUP_CH)
    if h0 is None:
        h0c = jnp.zeros((B, 2, S5_GROUPS, S5_P), jnp.complex64)
    else:
        hf = h0.astype(F32)
        h0c = lax.complex(hf[..., 0], hf[..., 1])
    y = u * d_skip.astype(F32)
    finals = []
    for dirn in range(2):
        lam = lax.complex(a_re[dirn].astype(F32), a_im[dirn].astype(F32))
        dt = jnp.exp(log_dt[dirn].astype(F32))[:, None]
        lam_bar = jnp.exp(lam * dt)
        b_mat = lax.complex(b_re[dirn].astype(F32), b_im[dirn].astype(F32))
        b_bar = ((lam_bar - 1.0) / lam)[..., None] * b_mat
        c_mat = lax.complex(c_re[dirn].astype(F32), c_im[dirn].astype(F32))
        u_dir = ug if dirn == 0 else jnp.flip(ug, axis=1)
        states = s5_scan(u_dir, lam_bar, b_bar, h0c[:, dirn])
        y_dir = jnp.real(jnp.einsum('gcp,blgp->blgc', c_mat, states))
        if dirn == 1:
            y_dir = jnp.flip(y_dir, axis=1)
        y = y + y_dir.reshape(B, L, D_MODEL)
        finals.append(states[:, -1])
    zz = jax.nn.gelu(y).astype(h.dtype) @ w_out
    za, zb = jnp.split(zz, 2, axis=-1)
    fin = jnp.stack(finals, axis=1)
    return za * jax.nn.sigmoid(zb), jnp.stack([jnp.real(fin), jnp.imag(fin)], axis=-1)

def peer_ffn(h, w_query, sub_keys, u_tab, v_tab):
    B, L, D = h.shape
    q = (h @ w_query).reshape(B, L, PEER_HEADS, 2, PEER_QDIM // 2)
    s = jnp.einsum('blhtd,htnd->blhtn', q, sub_keys).astype(F32)
    s1, i1 = lax.top_k(s[..., 0, :], PEER_TOPK)
    s2, i2 = lax.top_k(s[..., 1, :], PEER_TOPK)
    cand = (s1[..., :, None] + s2[..., None, :]).reshape(B, L, PEER_HEADS, PEER_TOPK * PEER_TOPK)
    cidx = (i1[..., :, None] * PEER_NKEYS + i2[..., None, :]).reshape(B, L, PEER_HEADS, PEER_TOPK * PEER_TOPK)
    top, pos = lax.top_k(cand, PEER_TOPK)
    idx = jnp.take_along_axis(cidx, pos, axis=-1)
    g = jax.nn.softmax(top, axis=-1).astype(h.dtype)
    nb = (B * L) // PEER_TOKEN_BLOCK
    hb = h.reshape(nb, PEER_TOKEN_BLOCK, D)
    ib = idx.reshape(nb, PEER_TOKEN_BLOCK, PEER_HEADS * PEER_TOPK)
    gb = g.reshape(nb, PEER_TOKEN_BLOCK, PEER_HEADS * PEER_TOPK)

    def block(args):
        hx, ix, gx = args
        act = jax.nn.gelu(jnp.einsum('td,tkd->tk', hx, u_tab[ix]))
        return jnp.einsum('tk,tkd->td', gx * act, v_tab[ix])

    return lax.map(block, (hb, ib, gb)).reshape(B, L, D)

def setup_inputs(seed: int = 0) -> dict:
    key = jax.random.key(seed)
    ks = iter(jax.random.split(key, 48))

    def nrm(shape, scale):
        return scale * jax.random.normal(next(ks), shape, F32)

    D = D_MODEL
    n_idx = jnp.arange(S5_P, dtype=F32)
    return {
        "x_prompt": nrm((BATCH, SEQ, D), 1.0),
        "x_sample": nrm((DEC_BATCH, DEC_SEQ, D), 1.0),
        "cache_da_k": nrm((DEC_BATCH, N_EVEN, PAST_LEN, 2 * DA_HEADS, DA_DIM), 1.0),
        "cache_da_v": nrm((DEC_BATCH, N_EVEN, PAST_LEN, DA_HEADS, 2 * DA_DIM), 1.0),
        "state_gla": nrm((DEC_BATCH, N_EVEN, 2, GLA_HEADS, GLA_DK, GLA_DV), 1.0),
        "state_s5": nrm((DEC_BATCH, N_ODD, 2, S5_GROUPS, S5_P, 2), 0.3),
        "c": nrm((DEC_BATCH, D), 1.0),
        "c_ctx": nrm((D,), 1.0),
        "ada_w": nrm((DEPTH, D, 6 * D), 0.5 * D ** -0.5),
        "ada_b": nrm((DEPTH, 6 * D), 0.02),
        "norm_g": 1.0 + nrm((DEPTH, 2, D), 0.05),
        "final_norm_g": 1.0 + nrm((D,), 0.05),
        "mix0_w_in": nrm((N_EVEN, D, IN0_WIDTH), D ** -0.5),
        "mix0_w_out": nrm((N_EVEN, MIX_WIDTH, D), MIX_WIDTH ** -0.5),
        "da_lam": nrm((N_EVEN, 4, DA_DIM), 0.1),
        "da_subln_g": 1.0 + nrm((N_EVEN, 2 * DA_DIM), 0.05),
        "gla_gate_up": nrm((N_EVEN, 2, GLA_GATE_RANK, GLA_HEADS * GLA_DK), GLA_GATE_RANK ** -0.5),
        "gla_gate_bias": nrm((N_EVEN, 2, GLA_HEADS * GLA_DK), 0.1),
        "gla_norm_g": 1.0 + nrm((N_EVEN, GLA_DV), 0.05),
        "s5_w_in": nrm((N_ODD, D, D), D ** -0.5),
        "s5_a_re": -0.5 + nrm((N_ODD, 2, S5_GROUPS, S5_P), 0.01),
        "s5_a_im": jnp.pi * n_idx + nrm((N_ODD, 2, S5_GROUPS, S5_P), 0.01),
        "s5_log_dt": jax.random.uniform(next(ks), (N_ODD, 2, S5_GROUPS), F32,
                                        minval=math.log(1e-3), maxval=math.log(1e-1)),
        "s5_b_re": nrm((N_ODD, 2, S5_GROUPS, S5_P, S5_GROUP_CH), (2 * S5_GROUP_CH) ** -0.5),
        "s5_b_im": nrm((N_ODD, 2, S5_GROUPS, S5_P, S5_GROUP_CH), (2 * S5_GROUP_CH) ** -0.5),
        "s5_c_re": nrm((N_ODD, 2, S5_GROUPS, S5_GROUP_CH, S5_P), (2 * S5_P) ** -0.5),
        "s5_c_im": nrm((N_ODD, 2, S5_GROUPS, S5_GROUP_CH, S5_P), (2 * S5_P) ** -0.5),
        "s5_d": nrm((N_ODD, D), 0.5),
        "s5_w_out": nrm((N_ODD, D, 2 * D), D ** -0.5),
        "peer_w_query": nrm((DEPTH, D, PEER_HEADS * PEER_QDIM), D ** -0.5),
        "peer_sub_keys": nrm((DEPTH, PEER_HEADS, 2, PEER_NKEYS, PEER_QDIM // 2), (PEER_QDIM // 2) ** -0.5),
        "peer_u": nrm((DEPTH, PEER_N, D), D ** -0.5),
        "peer_v": nrm((DEPTH, PEER_N, D), PEER_HEADS ** -0.5),
    }

def reference(x_prompt, x_sample, cache_da_k, cache_da_v, state_gla, state_s5, c, c_ctx,
              ada_w, ada_b, norm_g, final_norm_g, mix0_w_in, mix0_w_out, da_lam, da_subln_g,
              gla_gate_up, gla_gate_bias, gla_norm_g, s5_w_in, s5_a_re, s5_a_im, s5_log_dt,
              s5_b_re, s5_b_im, s5_c_re, s5_c_im, s5_d, s5_w_out,
              peer_w_query, peer_sub_keys, peer_u, peer_v):

    def trunk(x, cond, rope, caches):
        new_k, new_v, new_gla, new_s5 = [], [], [], []
        for layer in range(DEPTH):
            mod = jax.nn.silu(cond) @ ada_w[layer] + ada_b[layer]
            sh1, sc1, g1, sh2, sc2, g2 = jnp.split(mod[..., None, :], 6, axis=-1)
            h = rms_norm(x, norm_g[layer, 0]) * (1.0 + sc1) + sh1
            j = layer // 2
            if layer % 2 == 0:
                ctx = None if caches is None else (caches[0][:, j], caches[1][:, j], caches[2][:, j])
                m, (k_c, v_c, s_c) = even_mixer(h, mix0_w_in[j], mix0_w_out[j], da_lam[j],
                                                lambda_init(layer), da_subln_g[j], gla_gate_up[j],
                                                gla_gate_bias[j], gla_norm_g[j], rope, ctx)
                if caches is None:
                    new_k.append(k_c)
                    new_v.append(v_c)
                    new_gla.append(s_c)
            else:
                h0 = None if caches is None else caches[3][:, j]
                m, s_c = s5_mixer(h, s5_w_in[j], s5_a_re[j], s5_a_im[j], s5_log_dt[j], s5_b_re[j],
                                  s5_b_im[j], s5_c_re[j], s5_c_im[j], s5_d[j], s5_w_out[j], h0)
                if caches is None:
                    new_s5.append(s_c)
            x = x + g1 * m
            h = rms_norm(x, norm_g[layer, 1]) * (1.0 + sc2) + sh2
            x = x + g2 * peer_ffn(h, peer_w_query[layer], peer_sub_keys[layer], peer_u[layer], peer_v[layer])
        return rms_norm(x, final_norm_g), new_k, new_v, new_gla, new_s5

    y_prompt, k_list, v_list, gla_list, s5_list = trunk(x_prompt, c_ctx, None, None)
    rope = axial_rope(x_sample.shape[1], DA_DIM)
    y_sample = trunk(x_sample, c, rope, (cache_da_k, cache_da_v, state_gla, state_s5))[0]

    dt = x_prompt.dtype
    new_cache_da_k = jnp.stack(k_list, axis=1).astype(dt)
    new_cache_da_v = jnp.stack(v_list, axis=1).astype(dt)
    new_state_gla = jnp.stack(gla_list, axis=1).astype(dt)
    new_state_s5 = jnp.stack(s5_list, axis=1).astype(dt)
    return (y_prompt, y_sample, new_cache_da_k, new_cache_da_v, new_state_gla, new_state_s5)


_drawn_inputs = setup_inputs


def setup_inputs(seed=0):
    import zlib

    import numpy as np

    out = dict(_drawn_inputs(seed))
    spreads = {}
    factors = {'state_gla': 6.178,
     'da_lam': 3.084,
     'da_subln_g': 4.91,
     'gla_norm_g': 6.193,
     's5_a_re': 4.756,
     's5_c_re': 2.961,
     's5_c_im': 2.961}
    for name, (base, spread) in spreads.items():
        noise = np.random.default_rng([zlib.crc32(name.encode()), seed]).standard_normal(out[name].shape)
        drawn = base * np.exp(spread * noise) if base else spread * noise
        out[name] = __import__('jax').numpy.asarray(drawn.astype(out[name].dtype))
    for name, factor in factors.items():
        out[name] = (out[name] * factor).astype(out[name].dtype)
    return out
```

```python
import math
from contextlib import ExitStack

import numpy as np
import concourse.bass as bass
from concourse import mybir
from concourse.alu_op_type import AluOpType as ALU

ACT = mybir.ActivationFunctionType
F32 = mybir.dt.float32
F32R = mybir.dt.float32r
F16 = mybir.dt.float16
I32 = mybir.dt.int32
U32 = mybir.dt.uint32
X_AXIS = mybir.AxisListType.X

P = 128
D = 1024
KC = D // P
T = 384
TP = 128
NT = T // P
SEGS = ((0, 0, TP), (1, TP, T))
EPS = 1e-6
HEADS = 4
CHUNK = 64
NCH = T // CHUNK
PH = 8
TOPK = 16
NKEYS = 128
NEG = -3.0e38
GATE_SCALE = 1024.0
MODS = 6 * KC

CAND_LEN = [TOPK // (a + 1) for a in range(TOPK)]
CAND_START = [sum(CAND_LEN[:a]) for a in range(TOPK)]
NCAND = sum(CAND_LEN)

C_ID, C_ST, C_LEN, C_I16, C_IOTA = 0, 128, 144, 160, 176
C_KEEP = 304
C_ROT, C_MF, C_MB, C_CH, C_COS, C_SIN = 304, 432, 560, 688, 1072, 1328
C_ALL = 1584


def constants():
    c = np.zeros((P, C_ALL), np.float32)
    c[:, C_ID:C_ID + P] = np.eye(P)
    r = np.zeros((P, P), np.float32)
    for d in range(P):
        if d % 32 < 16:
            r[d, d + 16] = -1.0
        else:
            r[d, d - 16] = 1.0
    c[:, C_ROT:C_ROT + P] = r.T
    c[:, C_IOTA:C_IOTA + P] = np.arange(P)
    s, t = np.meshgrid(np.arange(P), np.arange(P), indexing="ij")
    same = s // CHUNK == t // CHUNK
    c[:, C_MF:C_MF + P] = same & (s <= t)
    c[:, C_MB:C_MB + P] = same & (s >= t)
    c[:, C_CH:C_CH + T] = np.arange(T) % CHUNK != 0
    c[:, C_ST:C_ST + 16] = CAND_START
    c[:, C_LEN + 1:C_LEN + 16] = CAND_LEN[:15]
    c[:, C_I16:C_I16 + 16] = np.arange(16)
    pos = np.arange(256)
    inv = 10000.0 ** (-np.arange(16, dtype=np.float32) / 16)
    row = (pos // 64).astype(np.float32)[:, None] * inv
    col = (pos % 64).astype(np.float32)[:, None] * inv
    ang = np.concatenate([row, row, col, col], 1).T
    c[:, C_COS:C_COS + 256] = np.tile(np.cos(ang), (2, 1))
    c[:, C_SIN:C_SIN + 256] = np.tile(np.sin(ang), (2, 1))
    return c


class Stage:

    def __init__(self, nc, sems, name):
        self.nc, self.sems, self.name, self.mem = nc, sems, name, ExitStack()

    def __enter__(self):
        return self

    def __exit__(self, *e):
        return self.mem.__exit__(*e)

    def sb(self, name, shape, dt=F32):
        return self.mem.enter_context(self.nc.sbuf_tensor(f"{self.name}_{name}", shape, dt))

    def ps(self, name, shape):
        return self.mem.enter_context(self.nc.psum_tensor(f"{self.name}_{name}", shape, F32))

    def sem(self, name):
        return self.sems.new(f"{self.name}_{name}")


class Semaphores:

    def __init__(self, nc):
        self.nc, self.taken = nc, []

    def new(self, name):
        self.taken.append(self.nc.alloc_semaphore(name))
        return self.taken[-1]

    def clear(self):
        self.nc.clear_and_free_semaphores(self.taken)
        self.nc.all_engine_barrier()
        self.taken = []


class Steps:

    def __init__(self, eng, sem, base=0):
        self.eng, self.sem, self.base, self.n = eng, sem, base, 0

    def done(self, ins):
        self.n += 1
        ins.then_inc(self.sem, 1)
        return ins

    def settle(self):
        self.eng.wait_ge(self.sem, self.base + self.n)


def r32(ap):
    return ap.bitcast(F32R)


def hi_part(nc, out, x):
    return nc.vector.tensor_copy(r32(out), x)


def lo_part(nc, out, x, hi):
    return nc.vector.tensor_tensor(r32(out), x, hi, ALU.subtract)


def modulation(nc, sems, cx, d):
    NW = 3
    N = 2 * 12
    with Stage(nc, sems, "mod") as s:
        w = s.sb("w", [P, NW, KC, 512])
        bias, cond, sg, row = s.sb("bias", [P, 2, MODS]), s.sb("cond", [P, KC, 2]), s.sb("sg", [P, KC, 2]), s.sb("row", [P, NW, 512])
        normg = s.sb("normg", [P, 4, KC])
        one = s.sb("one", [P, 2, 2, KC, 2])
        acc, tr = s.ps("acc", [P, NW, 512]), s.ps("tr", [P, NW, 512])
        small, loaded = s.sem("small"), [s.sem(f"w{i}_loaded") for i in range(NW)]
        sig, silu = s.sem("sigmoid"), s.sem("silu")
        summed, copied, turned, stored = s.sem("summed"), s.sem("copied"), s.sem("turned"), s.sem("stored")
        own, cleared = s.sem("dve"), s.sem("rows_cleared")
        with nc.Block() as block:
            @block.sync
            def _(sp):
                sp.dma_start(cond[:], d["cond"]).then_inc(small, 16)
                sp.dma_start(cx.const[:], d["consts"][:, 0:C_KEEP]).then_inc(small, 16)
                sp.dma_start(bias[:], d["ada_b"]).then_inc(small, 16)
                sp.dma_start(normg[:], d["norm_g"]).then_inc(small, 16)
                sp.dma_start(cx.x[:], d["x"]).then_inc(small, 16)
                sp.dma_start(cx.finalg[:], d["final_g"]).then_inc(small, 16)
                with sp.Fori(0, N // NW) as i:
                    for u in range(NW):
                        sp.wait_ge(summed, i * NW + u + 1)
                        sp.dma_start(w[:, u], d["ada_w"][bass.ds(i * NW + u, 1)].rearrange("a p k n -> p (a k) n")).then_inc(loaded[u], 16)

            @block.tensor
            def _(pe):
                pe.sem_inc(summed, NW)
                pe.sem_inc(turned, NW)
                pe.wait_ge(silu, 1)
                with pe.Fori(0, N // NW) as i:
                    for u in range(NW):
                        pe.wait_ge(loaded[u], i * 16 + 16)
                        pe.wait_ge(copied, i * NW + u + 1)
                        for k in range(KC):
                            mm = pe.matmul(acc[0:2, u, :], sg[:, k, :], w[:, u, k, :], start=k == 0, stop=k == KC - 1)
                        mm.then_inc(summed, 1)
                    for u in range(NW):
                        pe.wait_ge(copied, i * NW + u + 1 + NW)
                        pe.wait_ge(stored, i * NW + u + 1)
                        for b in range(4):
                            mm = pe.transpose(tr[:, u, b * P:(b + 1) * P], row[:, u, b * P:(b + 1) * P], cx.ident)
                        mm.then_inc(turned, 1)

            @block.scalar
            def _(act):
                act.sem_inc(copied, NW)
                act.wait_ge(cleared, 1)
                act.wait_ge(small, 96)
                nc.scalar.activation(sg[:], cond[:], ACT.Sigmoid).then_inc(sig, 1)
                with act.Fori(0, N // NW) as i:
                    for u in range(NW):
                        act.wait_ge(summed, i * NW + u + 1 + NW)
                        act.wait_ge(turned, i * NW + u + 1)
                        nc.scalar.activation(row[0:2, u], acc[0:2, u, :], ACT.Copy).then_inc(copied, 1)

            @block.vector
            def _(dve):
                dve.sem_inc(stored, NW)
                st = Steps(dve, own)
                nc.vector.memset(row[:], 0.0).then_inc(cleared, 1)
                st.done(nc.vector.memset(cx.ones[:], 1.0))
                st.done(nc.vector.memset(cx.eps[:], EPS))
                dve.wait_ge(small, 96)
                st.done(nc.vector.tensor_copy(cx.iota[:], cx.const[:, C_IOTA:C_IOTA + P]))
                dve.wait_ge(sig, 1)
                nc.vector.tensor_tensor(sg[:], sg[:], cond[:], ALU.mult).then_inc(silu, 1)
                with dve.Fori(0, N // NW) as i:
                    for u in range(NW):
                        dve.wait_ge(turned, i * NW + u + 1 + NW)
                        nc.vector.tensor_copy(cx.modT[:, bass.ds((i * NW + u) * 4, 4), :],
                                              tr[:, u].rearrange("p (b c) -> p b c", b=4)[:, :, 0:2]).then_inc(stored, 1)
                dve.wait_ge(stored, N + NW)
                m = cx.modT[:]
                st.done(nc.vector.tensor_tensor(m, m, bias[:].rearrange("p l j -> p (l j)").unsqueeze(2).to_broadcast([P, 2 * MODS, 2]), ALU.add))
                st.settle()
                for l in range(2):
                    for h in range(2):
                        st.done(nc.vector.tensor_scalar(one[:, l, h], cx.mod(l, 3 * h + 1), 1.0, None, ALU.add))
                st.settle()
                for l in range(2):
                    for h in range(2):
                        st.done(nc.vector.tensor_tensor(cx.scale[:, l, h], one[:, l, h],
                                                        normg[:, 2 * l + h].unsqueeze(2).to_broadcast([P, KC, 2]), ALU.mult))


def norm(nc, sems, cx, name, hi, lo, layer=0, which=0, m=None, gate=None, final=None):
    with Stage(nc, sems, name) as s:
        sq, root, rstd, h = s.sb("sq", [P, KC, T]), s.sb("root", [P, T]), s.sb("rstd", [P, T]), s.sb("h", [P, KC, T])
        ss = s.ps("ss", [P, T])
        ready, squared, summed, rooted, own, stored = (s.sem(x) for x in ("x_ready", "squared", "summed", "rooted", "dve", "stored"))
        with nc.Block() as block:
            @block.tensor
            def _(pe):
                for k in range(KC):
                    pe.wait_ge(squared, k + 1)
                    mm = pe.matmul(ss[:], cx.ones[:], sq[:, k], start=k == 0, stop=k == KC - 1)
                mm.then_inc(summed, 1)

            @block.scalar
            def _(act):
                for k in range(KC):
                    act.wait_ge(ready, k + 1)
                    nc.scalar.activation(sq[:, k], cx.x[:, k], ACT.Square).then_inc(squared, 1)
                act.wait_ge(summed, 1)
                nc.scalar.activation(root[:], ss[:], ACT.Sqrt, bias=cx.eps[:, 0:1], scale=1.0 / D).then_inc(rooted, 1)

            @block.vector
            def _(dve):
                st = Steps(dve, own)
                if m is None:
                    dve.sem_inc(ready, KC)
                else:
                    for k in range(KC):
                        for c, a, b in SEGS:
                            x = cx.x[:, k, a:b]
                            ins = nc.vector.scalar_tensor_tensor(x, m[:, k, a:b], cx.mod(layer if gate is None else gate[0], gate[1])[:, k, c:c + 1], x, ALU.mult, ALU.add)
                            if c == 0:
                                st.done(ins)
                        ins.then_inc(ready, 1)
                dve.wait_ge(rooted, 1)
                st.done(nc.vector.reciprocal(rstd[:], root[:]))
                st.settle()
                dve.wait_ge(ready, KC)
                st.done(nc.vector.tensor_tensor(h[:], cx.x[:], rstd[:].unsqueeze(1).to_broadcast([P, KC, T]), ALU.mult))
                st.settle()
                for k in range(KC):
                    if final is not None:
                        nc.vector.tensor_scalar(h[:, k], h[:, k], cx.finalg[:, k:k + 1], None, ALU.mult).then_inc(stored, 1)
                        continue
                    for c, a, b in SEGS:
                        st.done(nc.vector.tensor_scalar(h[:, k, a:b], h[:, k, a:b], cx.scale[:, layer, which, k, c:c + 1],
                                                        cx.mod(layer, 3 * which)[:, k, c:c + 1], ALU.mult, ALU.add))
                if final is None:
                    st.settle()
                    st.done(hi_part(nc, hi[:], h[:]))
                    st.settle()
                    st.done(lo_part(nc, lo[:], h[:], hi[:]))

            if final is not None:
                @block.sync
                def _(sp):
                    sp.wait_ge(stored, KC)
                    sp.dma_start(final, h[:]).then_inc(ready, 16)
                    sp.wait_ge(ready, KC + 16)


def linear(nc, sems, name, w_dram, n, hi, lo, out):
    NW = 3 if n % 3 == 0 else 4
    with Stage(nc, sems, name) as s:
        w, wh, wl = (s.sb(x, [P, NW, KC, P]) for x in ("w", "wh", "wl"))
        acc = s.ps("acc", [P, NW, 512])
        loaded = [s.sem(f"w{i}_loaded") for i in range(NW)]
        masked, split, summed, copied = (s.sem(x) for x in ("masked", "split", "summed", "copied"))
        with nc.Block() as block:
            @block.sync
            def _(sp):
                with sp.Fori(0, n // NW) as i:
                    for u in range(NW):
                        sp.wait_ge(split, i * NW + u + 1)
                        sp.dma_start(w[:, u], w_dram[bass.ds(i * NW + u, 1)].rearrange("a p k m -> p (a k) m")).then_inc(loaded[u], 16)

            @block.vector
            def _(dve):
                dve.sem_inc(split, NW)
                with dve.Fori(0, n // NW) as i:
                    for u in range(NW):
                        dve.wait_ge(loaded[u], i * 16 + 16)
                        dve.wait_ge(summed, i * NW + u + 1)
                        hi_part(nc, wh[:, u], w[:, u]).then_inc(masked, 1)
                        dve.wait_ge(masked, i * NW + u + 1)
                        lo_part(nc, wl[:, u], w[:, u], wh[:, u]).then_inc(split, 1)

            @block.tensor
            def _(pe):
                pe.sem_inc(summed, NW)
                with pe.Fori(0, n // NW) as i:
                    for u in range(NW):
                        pe.wait_ge(split, i * NW + u + 1 + NW)
                        pe.wait_ge(copied, i * NW + u + 1)
                        for k in range(KC):
                            o = acc[:, u, 0:T]
                            pe.matmul(o, r32(wh[:, u, k]), r32(hi[:, k]), start=k == 0, stop=False)
                            pe.matmul(o, r32(wh[:, u, k]), r32(lo[:, k]), start=False, stop=False)
                            mm = pe.matmul(o, r32(wl[:, u, k]), r32(hi[:, k]), start=False, stop=k == KC - 1)
                        mm.then_inc(summed, 1)

            @block.scalar
            def _(act):
                act.sem_inc(copied, NW)
                with act.Fori(0, n // NW) as i:
                    for u in range(NW):
                        act.wait_ge(summed, i * NW + u + 1 + NW)
                        nc.scalar.activation(out[:, bass.ds(i * NW + u, 1)].rearrange("p a t -> p (a t)"), acc[:, u, 0:T], ACT.Copy).then_inc(copied, 1)


def values(nc, sems, cx, d, hi, lo, v):
    with Stage(nc, sems, "val") as s:
        w, wh, wl = (s.sb(x, [P, 2, KC, 512]) for x in ("w", "wh", "wl"))
        acc = s.ps("acc", [P, 6, 512])
        loaded, split, masked, summed = [s.sem("w0_loaded"), s.sem("w1_loaded")], s.sem("split"), s.sem("masked"), s.sem("summed")
        tables = s.sem("tables_loaded")
        with nc.Block() as block:
            @block.sync
            def _(sp):
                for j in range(2):
                    sp.dma_start(w[:, j], d["w_v"][j]).then_inc(loaded[j], 16)
                sp.dma_start(cx.const0[:], d["consts"][:, C_KEEP:C_ALL]).then_inc(tables, 16)
                sp.wait_ge(tables, 16)

            @block.vector
            def _(dve):
                for j in range(2):
                    dve.wait_ge(loaded[j], 16)
                    hi_part(nc, wh[:, j], w[:, j]).then_inc(masked, 1)
                    dve.wait_ge(masked, j + 1)
                    lo_part(nc, wl[:, j], w[:, j], wh[:, j]).then_inc(split, 1)

            @block.tensor
            def _(pe):
                for j in range(2):
                    pe.wait_ge(split, j + 1)
                    for t in range(NT):
                        o, cols = acc[:, 3 * j + t, :], slice(t * P, (t + 1) * P)
                        for k in range(KC):
                            pe.matmul(o, r32(hi[:, k, cols]), r32(wh[:, j, k]), start=k == 0, stop=False)
                            pe.matmul(o, r32(hi[:, k, cols]), r32(wl[:, j, k]), start=False, stop=False)
                            mm = pe.matmul(o, r32(lo[:, k, cols]), r32(wh[:, j, k]), start=False, stop=k == KC - 1)
                        mm.then_inc(summed, 1)

            @block.scalar
            def _(act):
                for j in range(2):
                    for t in range(NT):
                        act.wait_ge(summed, 3 * j + t + 1)
                        nc.scalar.activation(v[:, t, j, :], acc[:, 3 * j + t, :], ACT.Copy)


def rope(nc, sems, cx, y):
    LS = T - TP
    with Stage(nc, sems, "rope") as s:
        rot = s.ps("rot", [P, 4, 512])
        a, b = s.sb("a", [P, 4, LS]), s.sb("b", [P, 4, LS])
        turned, own = s.sem("turned"), s.sem("dve")
        with nc.Block() as block:
            @block.tensor
            def _(pe):
                for j in range(8):
                    if j >= 4:
                        pe.wait_ge(own, 3 * (j - 3))
                    pe.matmul(rot[:, j % 4, 0:LS], cx.const0[:, C_ROT - C_KEEP:C_ROT - C_KEEP + P], y[:, j, TP:T], start=True, stop=True).then_inc(turned, 1)

            @block.vector
            def _(dve):
                for j in range(8):
                    dve.wait_ge(turned, j + 1)
                    nc.vector.tensor_tensor(a[:, j % 4], y[:, j, TP:T], cx.const0[:, C_COS - C_KEEP:C_COS - C_KEEP + LS], ALU.mult).then_inc(own, 1)
                    nc.vector.tensor_tensor(b[:, j % 4], rot[:, j % 4, 0:LS], cx.const0[:, C_SIN - C_KEEP:C_SIN - C_KEEP + LS], ALU.mult).then_inc(own, 1)
                    dve.wait_ge(own, 3 * j + 2)
                    nc.vector.tensor_tensor(y[:, j, TP:T], a[:, j % 4], b[:, j % 4], ALU.add).then_inc(own, 1)


def attention(nc, sems, cx, d, y, v, o):
    SC = 64 ** -0.5
    LAM0 = 0.8 - 0.6 * math.exp(-0.3 * 0)
    items = [(h, q) for h in range(HEADS) for q in range(NT)]
    nk = [P if q == 0 else T for _, q in items]
    with Stage(nc, sems, "att") as s:
        ck, cv = s.sb("ck", [P, HEADS, P]), s.sb("cv", [P, 512])
        lp, lq = s.sb("lp", [P, 4, 64]), s.sb("lq", [P, 2, 64])
        ls, lam = s.sb("ls", [P, 2]), s.sb("lam", [P, 1])
        mx, nm, den, rd, rl = (s.sb(n, [P, 2, 2]) for n in ("mx", "nm", "den", "rd", "rl"))
        e, a, tt, at = s.sb("e", [P, 2, 2, T]), s.sb("a", [P, 2, T]), s.sb("tt", [P, 2, T]), s.sb("at", [P, 2, T])
        kn = s.sb("kn", [P, HEADS, P])
        sc, tr, ob = s.ps("sc", [P, 2, 2, 512]), s.ps("tr", [P, 2, 512]), s.ps("ob", [P, 2, 512])
        loaded, out = s.sem("caches_loaded"), s.sem("k_v_stored")
        lexp, own = s.sem("lam_exp"), s.sem("dve")
        scored, maxed, expd, mixed, turned, tcopied, attended, ocopied = (
            s.sem(x) for x in ("scored", "maxed", "exp", "mixed", "turned", "turned_copied", "attended", "o_copied"))
        kturned, kcopied, lsum = s.sem("k_turned"), s.sem("k_copied"), s.sem("lam_sums")
        with nc.Block() as block:
            @block.sync
            def _(sp):
                sp.dma_start(lp[:], d["da_lam"]).then_inc(loaded, 16)
                sp.dma_start(ck[:], d["cache_k"]).then_inc(loaded, 16)
                sp.dma_start(cv[:], d["cache_v"]).then_inc(loaded, 16)
                sp.dma_start(d["new_v"], v[:, 0, 0, :]).then_inc(out, 16)
                sp.wait_ge(kcopied, 1)
                sp.dma_start(d["new_k"], kn[:]).then_inc(out, 16)
                sp.wait_ge(out, 32)

            @block.tensor
            def _(pe):
                def scores(i):
                    h, q = items[i]
                    if i >= 2:
                        pe.wait_ge(expd, i - 1)
                    for m in range(2):
                        r = slice(64 * m, 64 * m + 64)
                        lhs = y[r, h, q * P:(q + 1) * P]
                        own_keys = slice(0, P) if q == 0 else slice(TP, T)
                        n = own_keys.stop - own_keys.start
                        mm = pe.matmul(sc[:, i % 2, m, 0:n], lhs, y[r, HEADS + h, own_keys], start=True, stop=True)
                        if q:
                            mm = pe.matmul(sc[:, i % 2, m, n:T], lhs, ck[r, h, :], start=True, stop=True)
                    mm.then_inc(scored, 1)

                pe.wait_ge(loaded, 48)
                for h in range(HEADS):
                    mm = pe.transpose(tr[:, 0, h * P:(h + 1) * P], y[:, HEADS + h, 0:TP], cx.ident)
                mm.then_inc(kturned, 1)
                pe.wait_ge(kcopied, 1)
                scores(0)
                for i, (h, q) in enumerate(items):
                    if i + 1 < len(items):
                        scores(i + 1)
                    pe.wait_ge(mixed, i + 1)
                    if i >= 2:
                        pe.wait_ge(tcopied, i - 1)
                    for j in range(nk[i] // P):
                        mm = pe.transpose(tr[:, i % 2, j * P:(j + 1) * P], a[:, i % 2, j * P:(j + 1) * P], cx.ident)
                    mm.then_inc(turned, 1)
                    pe.wait_ge(tcopied, i + 1)
                    if q == 0 and h >= 2:
                        pe.wait_ge(ocopied, h - 1)
                    for j in range(nk[i] // P):
                        vals = v[:, 0 if q == 0 else 1 + j, 0, h * P:(h + 1) * P] if j < 2 else cv[:, h * P:(h + 1) * P]
                        mm = pe.matmul(ob[:, h % 2, q * P:(q + 1) * P], vals, at[:, i % 2, j * P:(j + 1) * P],
                                       start=j == 0, stop=j == nk[i] // P - 1)
                    mm.then_inc(attended, 1)

            @block.vector
            def _(dve):
                st = Steps(dve, own)
                dve.wait_ge(loaded, 48)
                st.done(nc.vector.tensor_tensor(lq[:], lp[:, 0:4:2], lp[:, 1:4:2], ALU.mult))
                st.settle()
                nc.vector.tensor_reduce(ls[:], lq[:], X_AXIS, ALU.add).then_inc(lsum, 1)
                dve.wait_ge(lexp, 1)
                st.done(nc.vector.tensor_tensor(lam[:], ls[:, 0:1], ls[:, 1:2], ALU.subtract))
                st.settle()
                st.done(nc.vector.tensor_scalar(lam[:], lam[:], LAM0, None, ALU.add))
                st.settle()

                def maxima(i):
                    dve.wait_ge(scored, i + 1)
                    st.done(nc.vector.tensor_reduce(mx[:, i % 2], sc[:, i % 2, :, 0:nk[i]], X_AXIS, ALU.max))
                    st.settle()
                    if i >= 2:
                        dve.wait_ge(expd, i - 1)
                    nc.vector.tensor_scalar(nm[:, i % 2], mx[:, i % 2], -SC, None, ALU.mult).then_inc(maxed, 1)

                maxima(0)
                for i in range(len(items)):
                    if i + 1 < len(items):
                        maxima(i + 1)
                    n, b = nk[i], i % 2
                    dve.wait_ge(expd, i + 1)
                    st.done(nc.vector.reciprocal(rd[:, b], den[:, b]))
                    st.settle()
                    st.done(nc.vector.tensor_tensor(rl[:, b, 0:1], rd[:, b, 1:2], lam[:], ALU.mult))
                    st.settle()
                    st.done(nc.vector.tensor_scalar(tt[:, b, 0:n], e[:, b, 1, 0:n], rl[:, b, 0:1], None, ALU.mult))
                    st.settle()
                    if i >= 2:
                        dve.wait_ge(turned, i - 1)
                    nc.vector.scalar_tensor_tensor(a[:, b, 0:n], e[:, b, 0, 0:n], rd[:, b, 0:1], tt[:, b, 0:n], ALU.mult, ALU.subtract).then_inc(mixed, 1)

            @block.scalar
            def _(act):
                act.wait_ge(lsum, 1)
                nc.scalar.activation(ls[:], ls[:], ACT.Exp).then_inc(lexp, 1)
                act.wait_ge(kturned, 1)
                nc.scalar.activation(kn[:].rearrange("p h k -> p (h k)"), tr[:, 0, :], ACT.Copy).then_inc(kcopied, 1)

                def exps(i):
                    act.wait_ge(maxed, i + 1)
                    if i >= 2:
                        act.wait_ge(mixed, i - 1)
                    for m in range(2):
                        ins = nc.scalar.activation(e[:, i % 2, m, 0:nk[i]], sc[:, i % 2, m, 0:nk[i]], ACT.Exp,
                                                   bias=nm[:, i % 2, m:m + 1], scale=SC, accum_out=den[:, i % 2, m:m + 1])
                    ins.then_inc(expd, 1)

                exps(0)
                for i, (h, q) in enumerate(items):
                    if i + 1 < len(items):
                        exps(i + 1)
                    act.wait_ge(turned, i + 1)
                    if i >= 2:
                        act.wait_ge(attended, i - 1)
                    nc.scalar.activation(at[:, i % 2, 0:nk[i]], tr[:, i % 2, 0:nk[i]], ACT.Copy).then_inc(tcopied, 1)
                    if q == NT - 1:
                        act.wait_ge(attended, i + 1)
                        nc.scalar.activation(o[:, h, :], ob[:, h % 2, 0:T], ACT.Copy).then_inc(ocopied, 1)


def head_norm(nc, sems, cx, name, o, g_dram, factor, hi, lo, r=None):
    with Stage(nc, sems, name) as s:
        g, gf = s.sb("g", [P, 1]), s.sb("gf", [P, 1])
        sq, root, sg = s.sb("sq", [P, HEADS, T]), s.sb("root", [P, HEADS, T]), s.sb("sg", [P, HEADS, T])
        ss = s.ps("ss", [P, HEADS, 512])
        loaded, squared, summed, rooted, gated, own = (s.sem(x) for x in ("g_loaded", "squared", "summed", "rooted", "gated", "dve"))
        with nc.Block() as block:
            @block.sync
            def _(sp):
                sp.dma_start(g[:], g_dram).then_inc(loaded, 16)

            @block.scalar
            def _(act):
                nc.scalar.activation(sq[:], o[:], ACT.Square).then_inc(squared, 1)
                if r is not None:
                    nc.scalar.activation(sg[:], r, ACT.Sigmoid).then_inc(gated, 1)
                for h in range(HEADS):
                    act.wait_ge(summed, h + 1)
                    nc.scalar.activation(root[:, h], ss[:, h, 0:T], ACT.Sqrt, bias=cx.eps[:, 0:1], scale=1.0 / P).then_inc(rooted, 1)

            @block.tensor
            def _(pe):
                pe.wait_ge(squared, 1)
                for h in range(HEADS):
                    pe.matmul(ss[:, h, 0:T], cx.ones[:], sq[:, h], start=True, stop=True).then_inc(summed, 1)

            @block.vector
            def _(dve):
                st = Steps(dve, own)
                dve.wait_ge(loaded, 16)
                st.done(nc.vector.tensor_scalar(gf[:], g[:], factor, None, ALU.mult))
                dve.wait_ge(rooted, HEADS)
                st.done(nc.vector.reciprocal(root[:], root[:]))
                st.settle()
                st.done(nc.vector.scalar_tensor_tensor(o[:], o[:], gf[:, 0:1], root[:], ALU.mult, ALU.mult))
                st.settle()
                if r is not None:
                    dve.wait_ge(gated, 1)
                    st.done(nc.vector.tensor_tensor(sg[:], sg[:], r, ALU.mult))
                    st.settle()
                    st.done(nc.vector.tensor_tensor(o[:], o[:], sg[:], ALU.mult))
                    st.settle()
                st.done(hi_part(nc, hi, o[:]))
                st.settle()
                st.done(lo_part(nc, lo, o[:], hi))


def gla(nc, sems, cx, d, y, v, o):
    QG, KG, LOW = 8, 10, 16
    X = 4
    with Stage(nc, sems, "gla") as s:
        gu, gb, s0 = s.sb("gu", [16, 2, 256]), s.sb("gb", [P, X]), s.sb("s0", [P, X, P])
        z, m, az, b, eb = (s.sb(n, [P, X, T]) for n in ("z", "m", "az", "b", "eb"))
        qd, ki = s.sb("qd", [P, X, T]), s.sb("ki", [P, X, T])
        bl, el = s.sb("bl", [P, X, NCH]), s.sb("el", [P, X, NCH])
        ken = s.sb("ken", [P, X, NT, P])
        S = s.sb("S", [P, X, NCH, P])
        sf, unread = s.sb("sf", [P, X, P]), s.sb("unread", [P, X, P])
        am = s.sb("am", [P, 2, 2, P])
        wk = s.ps("wk", [P, 4, 512])
        ob = s.ps("ob", [P, 2, 512])
        loaded, gated, biased, own = s.sem("loaded"), s.sem("gates"), s.sem("biased"), s.sem("dve")
        logs, cums, ends, decays = s.sem("act"), s.sem("cumsum"), s.sem("ends"), s.sem("decays")
        keyed, turned, tcopied, updated, folded = (s.sem(x) for x in ("k_end", "k_turned", "k_copied", "kv", "state"))
        scored, masked, outed, ocopied, stored = (s.sem(x) for x in ("scored", "masked", "o_done", "o_copied", "stored"))

        seqs = {0: [[0, 1], [2, 3, 4, 5]], 1: [[1, 0], [5, 4, 3, 2]]}
        steps = [(2 * dr + hp, seqs[dr], q, j) for q in (0, 1) for j in range(4) for dr in range(2) for hp in range(2)
                 if j < len(seqs[dr][q])]
        items = [(h, t) for h in range(HEADS) for t in range(NT)]
        with nc.Block() as block:
            @block.sync
            def _(sp):
                sp.dma_start(gu[:], d["gate_up"]).then_inc(loaded, 16)
                sp.dma_start(gb[:], d["gate_bias"]).then_inc(loaded, 16)
                sp.dma_start(s0[:], d["state_gla"]).then_inc(loaded, 16)
                sp.wait_ge(folded, len(steps))
                sp.dma_start(d["new_gla"], sf[:]).then_inc(stored, 16)
                sp.wait_ge(stored, 16)

            @block.tensor
            def _(pe):
                pe.wait_ge(loaded, 48)
                for x in range(X):
                    dr, hp = divmod(x, 2)
                    pe.matmul(wk[:, x, 0:T], gu[:, dr, hp * P:(hp + 1) * P], y[0:16, LOW + dr, :], start=True, stop=True).then_inc(gated, 1)
                pe.wait_ge(biased, X)
                pe.wait_ge(keyed, 1)
                for x in range(X):
                    for t in range(NT):
                        mm = pe.transpose(wk[:, x, t * P:(t + 1) * P], eb[:, x, t * P:(t + 1) * P], cx.ident)
                    mm.then_inc(turned, 1)
                pe.wait_ge(tcopied, X)
                for i, (x, chunks, q, j) in enumerate(steps):
                    c = chunks[q][j]
                    hp, r = x % 2, slice(64 * (c % 2), 64 * (c % 2) + 64)
                    if i >= 4:
                        pe.wait_ge(folded, i - 3)
                    pe.matmul(wk[:, i % 4, 0:256], ken[r, x, c // 2, :], v[r, c // 2, 1, hp * 256:(hp + 1) * 256],
                              start=True, stop=True).then_inc(updated, 1)
                pe.wait_ge(folded, len(steps))

                def scores(i):
                    h, t = items[i]
                    r, cols = slice(64 * (h % 2), 64 * (h % 2) + 64), slice(t * P, (t + 1) * P)
                    for dr in range(2):
                        x = 2 * dr + h // 2
                        if i >= 2:
                            pe.wait_ge(masked, 2 * (i - 2) + dr + 1)
                        pe.matmul(wk[:, 2 * (i % 2) + dr, 0:P], ki[r, x, cols], qd[r, x, cols], start=True, stop=True).then_inc(scored, 1)

                scores(0)
                for i, (h, t) in enumerate(items):
                    if i + 1 < len(items):
                        scores(i + 1)
                    r = slice(64 * (h % 2), 64 * (h % 2) + 64)
                    pe.wait_ge(masked, 2 * i + 2)
                    if t == 0 and h >= 2:
                        pe.wait_ge(ocopied, h - 1)
                    for c in (2 * t, 2 * t + 1):
                        oo = ob[:, h % 2, c * CHUNK:(c + 1) * CHUNK]
                        cc = slice(CHUNK * (c % 2), CHUNK * (c % 2) + CHUNK)
                        for dr in range(2):
                            pe.matmul(oo, v[:, t, 1, h * P:(h + 1) * P], am[:, i % 2, dr, cc], start=dr == 0, stop=False)
                        for dr in range(2):
                            x = 2 * dr + h // 2
                            mm = pe.matmul(oo, S[r, x, c, :], qd[r, x, c * CHUNK:(c + 1) * CHUNK], start=False, stop=dr == 1)
                    mm.then_inc(outed, 1)

            @block.vector
            def _(dve):
                st = Steps(dve, own)
                st.done(nc.vector.memset(am[:], 0.0))
                st.done(nc.vector.memset(S[:, 0:2, 0, :], 0.0))
                st.done(nc.vector.memset(S[:, 2:4, 1, :], 0.0))
                dve.wait_ge(loaded, 48)
                for x in range(X):
                    dve.wait_ge(gated, x + 1)
                    nc.vector.tensor_scalar(z[:, x], wk[:, x, 0:T], gb[:, x:x + 1], None, ALU.add).then_inc(biased, 1)
                    st.done(nc.vector.tensor_copy(S[:, x, 2 if x < 2 else 5, :], s0[:, x, :]))
                dve.wait_ge(biased, X)
                st.done(nc.vector.tensor_scalar(m[:], z[:], 0.0, None, ALU.min))
                st.settle()
                dve.wait_ge(logs, 3)
                st.done(nc.vector.tensor_tensor(z[:], m[:], az[:], ALU.subtract))
                st.settle()
                st.done(nc.vector.tensor_scalar(z[:], z[:], 1.0 / 16.0, None, ALU.mult))
                st.settle()
                for x in range(X):
                    if x < 2:
                        out, g, keep = b[:, x], z[:, x], cx.const0[:, C_CH - C_KEEP:C_CH - C_KEEP + T]
                    else:
                        out, g, keep = b[:, x][:, ::-1], z[:, x][:, ::-1], cx.const0[:, C_CH - C_KEEP:C_CH - C_KEEP + T]
                    st.done(nc.vector.tensor_tensor_scan(out, keep, g, 0.0, ALU.mult, ALU.add))
                st.settle()
                bc = b[:].rearrange("p x (c i) -> p x c i", c=NCH)
                st.done(nc.vector.tensor_copy(bl[:, 0:2], bc[:, 0:2, :, CHUNK - 1]))
                ins = nc.vector.tensor_copy(bl[:, 2:4], bc[:, 2:4, :, 0])
                st.done(ins)
                st.settle()
                dve.sem_inc(cums, 1)
                for x in range(X):
                    ins = nc.vector.tensor_tensor(z[:, x].rearrange("p (c i) -> p c i", c=NCH),
                                                  bl[:, x].unsqueeze(2).to_broadcast([P, NCH, CHUNK]),
                                                  bc[:, x], ALU.subtract)
                ins.then_inc(ends, 1)
                qg, kg = y[:, QG:QG + 2, :], y[:, KG:KG + 2, :]
                dve.wait_ge(decays, 1)
                for dr in range(2):
                    st.done(nc.vector.scalar_tensor_tensor(qd[:, 2 * dr:2 * dr + 2], qg, 64 ** -0.5, m[:, 2 * dr:2 * dr + 2], ALU.mult, ALU.mult))
                dve.wait_ge(decays, 2)
                for dr in range(2):
                    st.done(nc.vector.tensor_tensor(ki[:, 2 * dr:2 * dr + 2], kg, az[:, 2 * dr:2 * dr + 2], ALU.mult))
                dve.wait_ge(decays, 4)
                for dr in range(2):
                    ins = nc.vector.tensor_tensor(eb[:, 2 * dr:2 * dr + 2], kg, eb[:, 2 * dr:2 * dr + 2], ALU.mult)
                ins.then_inc(keyed, 1)
                for i, (x, chunks, q, j) in enumerate(steps):
                    c = chunks[q][j]
                    last = j == len(chunks[q]) - 1
                    dve.wait_ge(updated, i + 1)
                    if j:
                        dve.wait_ge(folded, i - 3)
                    for hh in range(2):
                        r = slice(64 * hh, 64 * hh + 64)
                        dst = (sf, unread)[q][r, x, :] if last else S[r, x, chunks[q][j + 1], :]
                        ins = nc.vector.scalar_tensor_tensor(dst, S[r, x, c, :], el[r, x, c:c + 1], wk[r, i % 4, hh * P:(hh + 1) * P],
                                                             ALU.mult, ALU.add)
                    ins.then_inc(folded, 1)
                for i in range(len(items)):
                    if i >= 2:
                        dve.wait_ge(outed, i - 1)
                    for dr in range(2):
                        dve.wait_ge(scored, 2 * i + dr + 1)
                        mask = cx.const0[:, (C_MF, C_MB)[dr] - C_KEEP:(C_MF, C_MB)[dr] - C_KEEP + P].bitcast(I32)
                        nc.vector.copy_predicated(am[:, i % 2, dr, :], mask, wk[:, 2 * (i % 2) + dr, 0:P]).then_inc(masked, 1)

            @block.scalar
            def _(act):
                act.wait_ge(biased, X)
                nc.scalar.activation(az[:], z[:], ACT.Abs).then_inc(logs, 1)
                act.wait_ge(logs, 1)
                nc.scalar.activation(az[:], az[:], ACT.Exp, scale=-1.0).then_inc(logs, 1)
                act.wait_ge(logs, 2)
                nc.scalar.activation(az[:], az[:], ACT.Ln, bias=cx.ones[:, 0:1]).then_inc(logs, 1)
                act.wait_ge(cums, 1)
                nc.scalar.activation(m[:], b[:], ACT.Exp).then_inc(decays, 1)
                nc.scalar.activation(az[:], b[:], ACT.Exp, scale=-1.0).then_inc(decays, 1)
                act.wait_ge(ends, 1)
                nc.scalar.activation(eb[:], z[:], ACT.Exp).then_inc(decays, 1)
                nc.scalar.activation(el[:], bl[:], ACT.Exp).then_inc(decays, 1)
                for x in range(X):
                    act.wait_ge(turned, x + 1)
                    nc.scalar.activation(ken[:, x].rearrange("p t k -> p (t k)"), wk[:, x, 0:T], ACT.Copy).then_inc(tcopied, 1)
                for h in range(HEADS):
                    act.wait_ge(outed, NT * (h + 1))
                    nc.scalar.activation(o[:, h, :], ob[:, h % 2, 0:T], ACT.Copy).then_inc(ocopied, 1)


def retrieve(nc, sems, cx, name, keys_dram, q, i1T, i2T, gh, gl):
    J = 2 * PH
    with Stage(nc, sems, name) as s:
        keys = s.sb("keys", [P, J, NKEYS])
        sc, sc2 = s.sb("sc", [P, 2, J, NKEYS]), s.sb("sc2", [P, J, NKEYS])
        v16, ix, ixf, dx = s.sb("v16", [P, J, TOPK]), s.sb("ix", [P, J, TOPK], U32), s.sb("ixf", [P, J, TOPK]), s.sb("dx", [P, J, TOPK])
        cand, cand2 = s.sb("cand", [P, PH, NCAND]), s.sb("cand2", [P, PH, NCAND])
        top, pos = s.sb("top", [P, PH, TOPK]), s.sb("pos", [P, PH, TOPK], U32)
        posf, ex, den, row = s.sb("posf", [P, P]), s.sb("ex", [P, PH, TOPK]), s.sb("den", [P, PH, 1]), s.sb("row", [P, P])
        ge, pr = s.sb("ge", [P, P, TOPK]), s.sb("pr", [P, P, TOPK])
        pick = s.sb("pick", [P, 2, 3, P])
        g16 = s.sb("g16", [P, P], F16)
        ps, tr = s.ps("ps", [P, 4, 512]), s.ps("tr", [P, 2, 512])
        loaded, scored, copied, own = s.sem("keys_loaded"), s.sem("scored"), s.sem("copied"), s.sem("dve")
        sub, expd, picked, turned, stored = (s.sem(x) for x in ("cand_sub", "exp", "picked", "turned", "stored"))
        read = s.sem("scores_read")
        with nc.Block() as block:
            @block.sync
            def _(sp):
                sp.dma_start(keys[:], keys_dram).then_inc(loaded, 16)

            @block.tensor
            def _(pe):
                pe.wait_ge(loaded, 16)
                for t in range(NT):
                    for j in range(J):
                        if t and j % 4 == 0:
                            pe.wait_ge(copied, 4 * (t - 1) + j // 4 + 1)
                        mm = pe.matmul(ps[:, j // 4, (j % 4) * P:(j % 4 + 1) * P], q[:, j, t * P:(t + 1) * P], keys[:, j, :], start=True, stop=True)
                        if j % 4 == 3:
                            mm.then_inc(scored, 1)
                for t in range(NT):
                    pe.wait_ge(picked, t + 1)
                    if t >= 2:
                        pe.wait_ge(stored, t - 1)
                    for a in range(3):
                        mm = pe.transpose(tr[:, t % 2, a * P:(a + 1) * P], pick[:, t % 2, a, :], cx.ident)
                    mm.then_inc(turned, 1)

            @block.scalar
            def _(act):
                def exps(t):
                    act.wait_ge(sub, t + 1)
                    nc.scalar.activation(ex[:], ex[:], ACT.Exp).then_inc(expd, 1)

                for t in range(NT):
                    if t >= 2:
                        exps(t - 2)
                        act.wait_ge(read, t - 1)
                    for b in range(4):
                        act.wait_ge(scored, 4 * t + b + 1)
                        nc.scalar.activation(sc[:, t % 2, 4 * b:4 * b + 4].rearrange("p j n -> p (j n)"), ps[:, b, :], ACT.Copy).then_inc(copied, 1)
                exps(NT - 2)
                exps(NT - 1)

            @block.vector
            def _(dve):
                st = Steps(dve, own)
                vec = nc.vector

                def take(a):
                    dve.wait_ge(turned, a + 1)
                    cols = slice(a * P, (a + 1) * P)
                    for dst, k in ((i1T, 0), (i2T, 1)):
                        vec.tensor_copy(dst[:, cols], tr[:, a % 2, k * P:(k + 1) * P])
                    st.done(vec.tensor_copy(g16[:], tr[:, a % 2, 2 * P:3 * P]))
                    st.settle()
                    st.done(vec.tensor_copy(gh[:, cols], g16[:]))
                    st.settle()
                    vec.tensor_tensor(gl[:, cols], tr[:, a % 2, 2 * P:3 * P], gh[:, cols], ALU.subtract).then_inc(stored, 1)

                for t in range(NT):
                    dve.wait_ge(copied, 4 * t + 4)
                    x = sc[:, t % 2]
                    for j in range(J):
                        ins = vec.max(v16[:, j, 0:8], x[:, j])
                    st.done(ins)
                    st.settle()
                    for j in range(J):
                        vec.max_index(ix[:, j, 0:8], v16[:, j, 0:8], x[:, j])
                        ins = vec.match_replace(sc2[:, j], v16[:, j, 0:8], x[:, j], NEG)
                    st.done(ins)
                    st.settle()
                    dve.sem_inc(read, 1)
                    for j in range(J):
                        ins = vec.max(v16[:, j, 8:16], sc2[:, j])
                    st.done(ins)
                    st.settle()
                    for j in range(J):
                        ins = vec.max_index(ix[:, j, 8:16], v16[:, j, 8:16], sc2[:, j])
                    st.done(ins)
                    v = v16[:].rearrange("p (h w) k -> p h w k", w=2)
                    s1, s2 = v[:, :, 0], v[:, :, 1]
                    a = 0
                    while a < TOPK:
                        n = CAND_LEN[a]
                        rows = CAND_LEN.count(n) if n <= 2 else 1
                        out = cand[:, :, CAND_START[a]:CAND_START[a] + n * rows].rearrange("p h (r b) -> p h r b", r=rows)
                        ins = vec.tensor_tensor(out, s1[:, :, a:a + rows].unsqueeze(3).to_broadcast([P, PH, rows, n]),
                                                s2[:, :, 0:n].unsqueeze(2).to_broadcast([P, PH, rows, n]), ALU.add)
                        a += rows
                    st.done(ins)
                    st.settle()
                    st.done(vec.tensor_copy(ixf[:], ix[:]))
                    for h in range(PH):
                        ins = vec.max(top[:, h, 0:8], cand[:, h])
                    st.done(ins)
                    st.settle()
                    st.done(vec.tensor_copy(dx[:, :, 0:1], ixf[:, :, 0:1]))
                    st.done(vec.tensor_tensor(dx[:, :, 1:TOPK], ixf[:, :, 1:TOPK], ixf[:, :, 0:TOPK - 1], ALU.subtract))
                    for h in range(PH):
                        vec.max_index(pos[:, h, 0:8], top[:, h, 0:8], cand[:, h])
                        ins = vec.match_replace(cand2[:, h], top[:, h, 0:8], cand[:, h], NEG)
                    st.done(ins)
                    st.settle()
                    for h in range(PH):
                        ins = vec.max(top[:, h, 8:16], cand2[:, h])
                    st.done(ins)
                    st.settle()
                    for h in range(PH):
                        ins = vec.max_index(pos[:, h, 8:16], top[:, h, 8:16], cand2[:, h])
                    st.done(ins)
                    vec.tensor_tensor(ex[:], top[:], top[:, :, 0:1].to_broadcast([P, PH, TOPK]), ALU.subtract).then_inc(sub, 1)
                    st.settle()
                    st.done(vec.tensor_copy(posf[:], pos[:].rearrange("p h k -> p (h k)")))
                    st.settle()
                    starts = cx.const[:, C_ST:C_ST + 16].unsqueeze(1).to_broadcast([P, P, TOPK])
                    lens = cx.const[:, C_LEN:C_LEN + 16].unsqueeze(1).to_broadcast([P, P, TOPK])
                    sixteen = cx.const[:, C_I16:C_I16 + 16].unsqueeze(1).to_broadcast([P, P, TOPK])
                    st.done(vec.tensor_tensor(ge[:], posf[:].unsqueeze(2).to_broadcast([P, P, TOPK]), starts, ALU.is_ge))
                    st.settle()
                    if t >= 2:
                        dve.wait_ge(turned, t - 1)
                    dxr = dx[:].rearrange("p (h w) r -> p h w r", w=2)
                    gv = ge[:].rearrange("p (h k) r -> p h k r", h=PH)
                    pv = pr[:].rearrange("p (h k) r -> p h k r", h=PH)
                    st.done(vec.tensor_tensor(pv, gv, dxr[:, :, 0].unsqueeze(2).to_broadcast([P, PH, TOPK, TOPK]), ALU.mult))
                    st.settle()
                    st.done(vec.tensor_reduce(pick[:, t % 2, 0], pr[:], X_AXIS, ALU.add))
                    st.settle()
                    st.done(vec.tensor_tensor(pr[:], ge[:], lens, ALU.mult))
                    st.settle()
                    st.done(vec.tensor_reduce(row[:], pr[:], X_AXIS, ALU.add))
                    st.settle()
                    st.done(vec.tensor_tensor(posf[:], posf[:], row[:], ALU.subtract))
                    st.settle()
                    st.done(vec.tensor_tensor(ge[:], posf[:].unsqueeze(2).to_broadcast([P, P, TOPK]), sixteen, ALU.is_ge))
                    st.settle()
                    st.done(vec.tensor_tensor(pv, gv, dxr[:, :, 1].unsqueeze(2).to_broadcast([P, PH, TOPK, TOPK]), ALU.mult))
                    st.settle()
                    st.done(vec.tensor_reduce(pick[:, t % 2, 1], pr[:], X_AXIS, ALU.add))
                    dve.wait_ge(expd, t + 1)
                    st.done(vec.tensor_reduce(den[:], ex[:], X_AXIS, ALU.add))
                    st.settle()
                    st.done(vec.reciprocal(den[:], den[:]))
                    st.settle()
                    st.done(vec.tensor_scalar(den[:], den[:], GATE_SCALE, None, ALU.mult))
                    st.settle()
                    st.done(vec.tensor_tensor(pick[:, t % 2, 2].rearrange("p (h k) -> p h k", h=PH), ex[:],
                                              den[:].to_broadcast([P, PH, TOPK]), ALU.mult))
                    st.settle()
                    dve.sem_inc(picked, 1)
                    if t:
                        take(t - 1)
                take(NT - 1)


IB = 32
TB = T // IB


def experts(nc, sems, cx, name, d, layer, hi, lo, picks, A, acc, value=None, gate=None, score=None):
    i1T, i2T, gh, gl = picks
    with Stage(nc, sems, name) as s:
        if score is not None:
            ur, uh, ul = (s.sb(x, [P, 2, KC, P]) for x in ("ur", "uh", "ul"))
        if value is not None:
            vr, vh, vl = (s.sb(x, [P, 2, D]) for x in ("vr", "vh", "vl"))
            wh, wl = s.sb("wh", [P, 2, T]), s.sb("wl", [P, 2, T])
        if gate is not None:
            o1 = s.sb("o1", [P, 2, TB, P], F16)
            eq, oh, ol = (s.sb(x, [P, 2, TB, IB], F16) for x in ("eq", "oh", "ol"))
        bank = s.ps("s", [P, 2, 512])
        gbank, sbanks = 1, (2 if gate is None else 1)
        uload, vload = [s.sem("u0_loaded"), s.sem("u1_loaded")], [s.sem("v0_loaded"), s.sem("v1_loaded")]
        uhigh, vhigh, usplit, vsplit, whigh, wsplit = (s.sem(x) for x in ("u_high", "v_high", "u_split", "v_split", "w_high", "w_split"))
        scored, gelud, valued, compared, hot, gated, applied = (
            s.sem(x) for x in ("scored", "gelu", "valued", "compared", "one_hots", "gated", "gates_applied"))
        with nc.Block() as block:
            @block.sync
            def _(sp):
                with sp.Fori(0, IB // 2) as i:
                    for b in range(2):
                        if score is not None:
                            sp.wait_ge(usplit, i * 2 + b + 1)
                            src = d["peer_u"][layer, bass.ds(i * 2 + (b + score * IB), 1)]
                            sp.dma_start(ur[:, b], src.rearrange("a p (k m) -> p (a k) m", k=KC)).then_inc(uload[b], 16)
                        if value is not None:
                            sp.wait_ge(vsplit, i * 2 + b + 1)
                            src = d["peer_v"][layer, bass.ds(i * 2 + (b + value * IB), 1)]
                            sp.dma_start(vr[:, b], src.rearrange("a p m -> p (a m)")).then_inc(vload[b], 16)

            @block.scalar
            def _(act):
                def round_tables(n, b, turn):
                    if score is not None:
                        act.wait_ge(uload[b], turn * 16 + 16)
                        act.wait_ge(scored, n + 1)
                        nc.scalar.activation(r32(uh[:, b]), ur[:, b], ACT.Copy).then_inc(uhigh, 1)
                    if value is not None:
                        act.wait_ge(vload[b], turn * 16 + 16)
                        act.wait_ge(valued, n + 1)
                        nc.scalar.activation(r32(vh[:, b]), vr[:, b], ACT.Copy).then_inc(vhigh, 1)

                def gelu(n, b):
                    if score is None:
                        return
                    act.wait_ge(scored, n + 1 + 2)
                    if value is not None:
                        act.wait_ge(wsplit, n + 1)
                    out = A[:, score % 2, bass.ds(n, 1), :].rearrange("p a t -> p (a t)")
                    nc.scalar.activation(out, bank[:, b % sbanks, 0:T], ACT.Gelu_apprx_tanh).then_inc(gelud, 1)

                act.sem_inc(gelud, sbanks)
                round_tables(0, 0, 0)
                with act.Fori(0, IB // 2 - 1) as i:
                    round_tables(i * 2 + 1, 1, i)
                    gelu(i * 2, 0)
                    round_tables(i * 2 + 2, 0, i + 1)
                    gelu(i * 2 + 1, 1)
                round_tables(IB - 1, 1, IB // 2 - 1)
                gelu(IB - 2, 0)
                gelu(IB - 1, 1)

            @block.vector
            def _(dve):
                v = nc.vector

                def prepare(n, b):
                    if score is not None:
                        dve.wait_ge(uhigh, n + 1)
                        lo_part(nc, ul[:, b], ur[:, b], uh[:, b]).then_inc(usplit, 1)
                    if value is not None:
                        dve.wait_ge(vhigh, n + 1)
                        lo_part(nc, vl[:, b], vr[:, b], vh[:, b]).then_inc(vsplit, 1)
                        w = A[:, value % 2, bass.ds(n, 1), :].rearrange("p a t -> p (a t)")
                        hi_part(nc, wh[:, b], w).then_inc(whigh, 1)
                        dve.wait_ge(whigh, n + 1)
                        lo_part(nc, wl[:, b], w, wh[:, b]).then_inc(wsplit, 1)
                    if gate is not None:
                        toks = bass.ds(n * TB, TB)
                        dve.wait_ge(gated, n + 1)
                        small = [P, TB, IB]
                        v.tensor_tensor(eq[:, b], cx.iota[:, gate * IB:gate * IB + IB].unsqueeze(1).to_broadcast(small),
                                        i2T[:, toks].unsqueeze(2).to_broadcast(small), ALU.is_equal).then_inc(compared, 1)
                        v.tensor_tensor(o1[:, b], cx.iota[:].unsqueeze(1).to_broadcast([P, TB, P]),
                                        i1T[:, toks].unsqueeze(2).to_broadcast([P, TB, P]), ALU.is_equal)
                        dve.wait_ge(compared, n + 1)
                        v.tensor_tensor(oh[:, b], eq[:, b], gh[:, toks].unsqueeze(2).to_broadcast(small), ALU.mult)
                        v.tensor_tensor(ol[:, b], eq[:, b], gl[:, toks].unsqueeze(2).to_broadcast(small), ALU.mult).then_inc(hot, 1)

                def apply(n, b):
                    if gate is None:
                        return
                    dve.wait_ge(gated, n + 1 + 2)
                    at = A[:, gate % 2, :, bass.ds(n * TB, TB)]
                    v.scalar_tensor_tensor(at, bank[:, gbank, 0:T].rearrange("p (t i) -> p i t", t=TB), 1.0 / GATE_SCALE,
                                           at, ALU.mult, ALU.mult).then_inc(applied, 1)

                dve.sem_inc(usplit, 2)
                dve.sem_inc(vsplit, 2)
                dve.sem_inc(applied, 1)
                prepare(0, 0)
                with dve.Fori(0, IB // 2 - 1) as i:
                    prepare(i * 2 + 1, 1)
                    apply(i * 2, 0)
                    prepare(i * 2 + 2, 0)
                    apply(i * 2 + 1, 1)
                prepare(IB - 1, 1)
                apply(IB - 2, 0)
                apply(IB - 1, 1)

            @block.tensor
            def _(pe):
                def gates(n, b):
                    if gate is None:
                        return
                    pe.wait_ge(hot, n + 1)
                    pe.wait_ge(applied, n + 1)
                    for t in range(TB):
                        o = bank[:, gbank, t * IB:(t + 1) * IB]
                        pe.matmul(o, o1[:, b, t], oh[:, b, t], start=True, stop=False)
                        mm = pe.matmul(o, o1[:, b, t], ol[:, b, t], start=False, stop=True)
                    mm.then_inc(gated, 1)

                def scores(n, b):
                    if score is None:
                        return
                    pe.wait_ge(usplit, n + 1 + 2)
                    pe.wait_ge(gelud, n + 1)
                    o = bank[:, b % sbanks, 0:T]
                    for k in range(KC):
                        pe.matmul(o, r32(uh[:, b, k]), r32(hi[:, k]), start=k == 0, stop=False)
                        pe.matmul(o, r32(uh[:, b, k]), r32(lo[:, k]), start=False, stop=False)
                        mm = pe.matmul(o, r32(ul[:, b, k]), r32(hi[:, k]), start=False, stop=k == KC - 1)
                    mm.then_inc(scored, 1)

                def contract(n, b):
                    if value is None:
                        return
                    pe.wait_ge(wsplit, n + 1)
                    for t in range(NT):
                        w = slice(t * P, (t + 1) * P)
                        for lhs, rhs in ((wh, vh), (wh, vl), (wl, vh)):
                            for c in range(2):
                                mm = pe.matmul(acc[:, 2 * t + c, :], r32(lhs[:, b, w]), r32(rhs[:, b, c * 512:(c + 1) * 512]),
                                               start=False, stop=False, skip_group_check=True)
                    mm.then_inc(valued, 1)

                pe.sem_inc(scored, 2)
                pe.sem_inc(valued, 2)
                pe.sem_inc(gated, 2)
                with pe.Fori(0, IB // 2) as i:
                    for b in range(2):
                        n = i * 2 + b
                        gates(n, b)
                        contract(n, b)
                        scores(n, b)


def add_experts(nc, sems, cx, name, layer, acc):
    with Stage(nc, sems, name) as s:
        out = s.sb("out", [P, NT, D])
        tr = s.ps("tr", [P, 2, 512])
        copied, turned, added = s.sem("copied"), s.sem("turned"), s.sem("added")
        with nc.Block() as block:
            @block.scalar
            def _(act):
                for n in range(2 * NT):
                    nc.scalar.activation(out[:, n // 2, (n % 2) * 512:(n % 2 + 1) * 512], acc[:, n, :], ACT.Copy).then_inc(copied, 1)

            @block.tensor
            def _(pe):
                for n in range(2 * NT):
                    pe.wait_ge(copied, n + 1)
                    if n >= 2:
                        pe.wait_ge(added, n - 1)
                    for j in range(4):
                        mm = pe.transpose(tr[:, n % 2, j * P:(j + 1) * P], out[:, n // 2, (4 * (n % 2) + j) * P:(4 * (n % 2) + j + 1) * P], cx.ident)
                    mm.then_inc(turned, 1)

            @block.vector
            def _(dve):
                for n in range(2 * NT):
                    t = n // 2
                    dve.wait_ge(turned, n + 1)
                    for j in range(4):
                        k = 4 * (n % 2) + j
                        x = cx.x[:, k, t * P:(t + 1) * P]
                        ins = nc.vector.scalar_tensor_tensor(x, tr[:, n % 2, j * P:(j + 1) * P], cx.mod(layer, 5)[:, k, min(t, 1):min(t, 1) + 1], x, ALU.mult, ALU.add)
                    ins.then_inc(added, 1)


NPAIR = 32
NPD = 2 * NPAIR
QUAD = 4


def s5_parameters(nc, sems, cx, d, par):
    TWO_PI_HI, TWO_PI_LO = 6.28125, 2 * math.pi - 6.28125
    ROUND = 1.5 * 2.0 ** 23
    with Stage(nc, sems, "s5p") as s:
        raw = s.sb("raw", [P, 3, NPD])
        dt, th, kk, r, s2, sn = (s.sb(n, [P, NPD]) for n in ("dt", "th", "kk", "r", "s2", "sn"))
        lr, li, den, t1, t2 = (s.sb(n, [P, NPD]) for n in ("lr", "li", "den", "t1", "t2"))
        loaded, own, act_done, asked = s.sem("loaded"), s.sem("dve"), s.sem("act"), s.sem("asked")
        are, aim = raw[:, 0], raw[:, 1]
        with nc.Block() as block:
            @block.sync
            def _(sp):
                sp.dma_start(raw[:], d["s5_par"]).then_inc(loaded, 16)
                sp.dma_start(par.h0[:], d["state_s5"]).then_inc(loaded, 16)
                sp.dma_start(par.dskip[:], d["s5_d"]).then_inc(loaded, 16)

            @block.scalar
            def _(act):
                act.wait_ge(loaded, 48)
                nc.scalar.activation(dt[:], raw[:, 2], ACT.Exp).then_inc(act_done, 1)
                act.wait_ge(asked, 1)
                nc.scalar.activation(par.mag[:], t1[:], ACT.Exp).then_inc(act_done, 1)
                act.wait_ge(asked, 2)
                nc.scalar.activation(s2[:], r[:], ACT.Sin, scale=0.5).then_inc(act_done, 1)
                nc.scalar.activation(sn[:], r[:], ACT.Sin).then_inc(act_done, 1)

            @block.vector
            def _(dve):
                v = nc.vector
                st = Steps(dve, own)

                def tt(out, a, b, op):
                    st.done(v.tensor_tensor(out, a, b, op))
                    st.settle()

                def ts(out, a, x, y, op0, op1=None):
                    st.done(v.tensor_scalar(out, a, x, y, op0, op1) if op1 else v.tensor_scalar(out, a, x, None, op0))
                    st.settle()

                dve.wait_ge(loaded, 48)
                dve.wait_ge(act_done, 1)
                tt(t1[:], are, dt[:], ALU.mult)
                dve.sem_inc(asked, 1)
                tt(th[:], aim, dt[:], ALU.mult)
                ts(kk[:], th[:], 1.0 / (2 * math.pi), ROUND, ALU.mult, ALU.add)
                ts(kk[:], kk[:], -ROUND, None, ALU.add)
                st.done(v.scalar_tensor_tensor(r[:], kk[:], -TWO_PI_HI, th[:], ALU.mult, ALU.add))
                st.settle()
                st.done(v.scalar_tensor_tensor(r[:], kk[:], -TWO_PI_LO, r[:], ALU.mult, ALU.add))
                st.settle()
                ts(r[:], r[:], 3.1415925, -3.1415925, ALU.min, ALU.max)
                dve.sem_inc(asked, 1)
                dve.wait_ge(act_done, 4)
                tt(t2[:], s2[:], s2[:], ALU.mult)
                ts(par.rot[:, 0], t2[:], -2.0, 1.0, ALU.mult, ALU.add)
                st.done(v.tensor_copy(par.rot[:, 1], sn[:]))
                tt(lr[:], par.mag[:], par.rot[:, 0], ALU.mult)
                tt(li[:], par.mag[:], par.rot[:, 1], ALU.mult)
                ts(lr[:], lr[:], -1.0, None, ALU.add)
                tt(den[:], are, are, ALU.mult)
                tt(t1[:], aim, aim, ALU.mult)
                tt(den[:], den[:], t1[:], ALU.add)
                st.done(v.reciprocal(den[:], den[:]))
                st.settle()
                tt(t1[:], lr[:], are, ALU.mult)
                tt(t2[:], li[:], aim, ALU.mult)
                tt(t1[:], t1[:], t2[:], ALU.add)
                tt(par.coef[:, 0], t1[:], den[:], ALU.mult)
                tt(t1[:], li[:], are, ALU.mult)
                tt(t2[:], lr[:], aim, ALU.mult)
                tt(t1[:], t1[:], t2[:], ALU.subtract)
                tt(par.coef[:, 1], t1[:], den[:], ALU.mult)


def s5_scan(nc, sems, cx, d, u, par, y, fin):
    LMAX = T - TP
    with Stage(nc, sems, "s5") as s:
        bw, cw = s.sb("bw", [P, 2, 2, QUAD * 32]), s.sb("cw", [P, 2, 2, QUAD, 32])
        bb, t0 = s.sb("bb", [P, 2, 2, QUAD * 32]), s.sb("t0", [P, 2, 2, QUAD * 32])
        bt = s.sb("bt", [P, 2, 2, P])
        cp = s.sb("cp", [P, 2, QUAD, 2, P])
        uq = s.sb("uq", [P, T])
        cf = s.sb("cf", [P, 2, 2, QUAD])
        mg, hq, rq = s.sb("mg", [P, 2, QUAD]), s.sb("hq", [P, 2, 2, QUAD]), s.sb("rq", [P, 2, 2, QUAD])
        E, Ea, Eb = s.sb("E", [P, 2, QUAD, LMAX]), s.sb("Ea", [P, QUAD, P]), s.sb("Eb", [P, QUAD, P])
        tab = s.sb("tab", [P, 2, 2, QUAD, T])
        m1, m2, m3, m4 = (s.sb(n, [P, 2, T]) for n in ("m1", "m2", "m3", "m4"))
        z = s.sb("z", [P, 2, 2, T])
        n1, n2, n3, n4 = (s.sb(n, [P, 2, T]) for n in ("n1", "n2", "n3", "n4"))
        x = s.sb("x", [P, 2, 2, T])
        bu, yp, tr = s.ps("bu", [P, 2, 2, 512]), s.ps("yp", [P, 512]), s.ps("tr", [P, 2, 512])
        b_loaded, c_loaded, own, pool_own = s.sem("b_loaded"), s.sem("c_loaded"), s.sem("dve"), s.sem("pool")
        bbar, turned, btc, quad_ready = s.sem("bbar"), s.sem("b_turned"), s.sem("b_copied"), s.sem("quad_ready")
        table, laid, driven, pre, zdone, xr, xi, projected, ydone, zeroed, taken = (
            s.sem(n) for n in ("tables", "laid", "driven", "premultiplied", "z", "x_re", "x_im", "projected", "y_done", "zeroed", "finals"))
        NQ = KC
        ITEMS = [(dr, p) for dr in range(2) for p in range(QUAD)]
        NI = len(ITEMS)
        LEVELS = 8
        DVE_OWN = 2 + 2 * (1 + 2 * LEVELS) + 2 * NI
        with nc.Block() as block:
            @block.sync
            def _(sp):
                sp.sem_inc(projected, NI)
                with sp.Fori(0, NQ) as q:
                    sp.wait_ge(ydone, q + 1)
                    sp.dma_start(bw[:], d["s5_b"][bass.ds(q, 1)].rearrange("a p r d m -> p (a r) d m")).then_inc(b_loaded, 16)
                    sp.wait_ge(projected, q * NI + NI)
                    sp.dma_start(cw[:], d["s5_c"][bass.ds(q, 1)].rearrange("a p r d j m -> p (a r) d j m")).then_inc(c_loaded, 16)

            @block.tensor
            def _(pe):
                with pe.Fori(0, NQ) as q:
                    pe.wait_ge(bbar, q + 1)
                    for ri in range(2):
                        for dr in range(2):
                            mm = pe.transpose(tr[:, ri, dr * P:(dr + 1) * P], bb[:, ri, dr, :], cx.ident)
                    mm.then_inc(turned, 1)
                    pe.wait_ge(btc, q * 2 + 2)

                    def drive(i):
                        dr, p = ITEMS[i]
                        r = slice(32 * p, 32 * p + 32)
                        pe.wait_ge(pre, q * NI + i + 1)
                        for ri in range(2):
                            mm = pe.matmul(bu[:, i % 2, ri, 0:T], bt[r, ri, dr, :], uq[r, :], start=True, stop=True)
                        mm.then_inc(driven, 1)

                    drive(0)
                    for i, (dr, p) in enumerate(ITEMS):
                        if i + 1 < NI:
                            drive(i + 1)
                        if i == 0:
                            pe.wait_ge(laid, q * 3 + 3)
                            pe.wait_ge(ydone, q + 1)
                        pe.wait_ge(xr, q * NI + i + 1)
                        pe.matmul(yp[:, 0:T], cp[:, dr, p, 0, :], x[:, i % 2, 0], start=i == 0, stop=False)
                        pe.wait_ge(xi, q * NI + i + 1)
                        pe.matmul(yp[:, 0:T], cp[:, dr, p, 1, :], x[:, i % 2, 1], start=False, stop=i == NI - 1).then_inc(projected, 1)

            @block.scalar
            def _(act):
                act.wait_ge(zeroed, 1)
                with act.Fori(0, NQ) as q:
                    act.wait_ge(ydone, q + 1)
                    nc.scalar.activation(uq[:], u[:, bass.ds(q, 1), :].rearrange("p a t -> p (a t)"), ACT.Copy)
                    for dr in range(2):
                        at = bass.ds(q * QUAD + dr * NPAIR, QUAD)
                        nc.scalar.activation(cf[:, :, dr], par.coef[:, :, at], ACT.Copy)
                        nc.scalar.activation(rq[:, :, dr], par.rot[:, :, at], ACT.Copy)
                        nc.scalar.activation(hq[:, :, dr], par.h0[:, :, at], ACT.Copy)
                        ins = nc.scalar.activation(mg[:, dr], par.mag[:, at], ACT.Copy)
                    ins.then_inc(quad_ready, 1)
                    act.wait_ge(turned, q + 1)
                    for ri in range(2):
                        nc.scalar.activation(bt[:, ri].rearrange("p d m -> p (d m)"), tr[:, ri, 0:2 * P], ACT.Copy).then_inc(btc, 1)
                    act.wait_ge(c_loaded, q * 16 + 16)
                    for p in range(QUAD):
                        nc.scalar.activation(cp[:, :, p, 0, 32 * p:32 * p + 32], cw[:, 0, :, p, :], ACT.Copy)
                        ins = nc.scalar.activation(cp[:, :, p, 1, 32 * p:32 * p + 32], cw[:, 1, :, p, :], ACT.Copy, scale=-1.0)
                    ins.then_inc(laid, 1)
                    for dr in range(2):
                        act.wait_ge(table, q * 2 + dr + 1)
                        for ri in range(2):
                            rev = -1 if dr else 1
                            nc.scalar.activation(tab[:, dr, ri, :, 0:TP], E[:, ri, :, 0:TP][:, :, ::rev], ACT.Copy)
                            ins = nc.scalar.activation(tab[:, dr, ri, :, TP:T], E[:, ri, :, 0:LMAX][:, :, ::rev], ACT.Copy)
                        ins.then_inc(laid, 1)
                    for i, (dr, p) in enumerate(ITEMS):
                        act.wait_ge(xr, q * NI + i + 1)
                        act.wait_ge(xi, q * NI + i + 1)
                        last = TP - 1 if dr == 0 else 0
                        nc.scalar.activation(fin[:, :, bass.ds(q * QUAD + (dr * NPAIR + p), 1)], x[:, i % 2, :, last:last + 1], ACT.Copy).then_inc(taken, 1)

            @block.gpsimd
            def _(pool):
                g = nc.gpsimd
                with pool.Fori(0, NQ) as q:
                    for i, (dr, p) in enumerate(ITEMS):
                        b = i % 2
                        pool.wait_ge(zdone, q * NI + i + 1)
                        tc, ts = tab[:, dr, 0, p], tab[:, dr, 1, p]
                        g.tensor_tensor(n3[:, b], z[:, b, 0], ts, ALU.mult).then_inc(pool_own, 1)
                        g.tensor_tensor(n4[:, b], z[:, b, 1], tc, ALU.mult).then_inc(pool_own, 1)
                        pool.wait_ge(pool_own, (q * NI + i) * 2 + 2)
                        pool.wait_ge(projected, q * NI + i + 1 + NI - 2)
                        pool.wait_ge(taken, q * NI + i + 1)
                        g.tensor_tensor(x[:, b, 1], n3[:, b], n4[:, b], ALU.add).then_inc(xi, 1)

            @block.vector
            def _(dve):
                v = nc.vector
                v.memset(cp[:], 0.0).then_inc(zeroed, 1)
                dve.sem_inc(pre, 2)
                dve.sem_inc(ydone, 1)
                dve.sem_inc(taken, 2)
                with dve.Fori(0, NQ) as q:
                    st = Steps(dve, own, q * DVE_OWN)
                    dve.wait_ge(quad_ready, q + 1)
                    dve.wait_ge(b_loaded, q * 16 + 16)
                    shape = [P, 2, QUAD, 32]
                    w4 = lambda a, ri: a[:, ri].rearrange("p d (j m) -> p d j m", j=QUAD)
                    co = lambda ri: cf[:, ri].unsqueeze(3).to_broadcast(shape)
                    v.tensor_tensor(w4(bb, 0), w4(bw, 0), co(0), ALU.mult)
                    v.tensor_tensor(w4(bb, 1), w4(bw, 1), co(0), ALU.mult)
                    v.tensor_tensor(w4(t0, 0), w4(bw, 1), co(1), ALU.mult)
                    st.done(v.tensor_tensor(w4(t0, 1), w4(bw, 0), co(1), ALU.mult))
                    st.settle()
                    st.done(v.tensor_tensor(bb[:, 0], bb[:, 0], t0[:, 0], ALU.subtract))
                    v.tensor_tensor(bb[:, 1], bb[:, 1], t0[:, 1], ALU.add).then_inc(bbar, 1)
                    for dr in range(2):
                        if dr:
                            dve.wait_ge(laid, q * 3 + 2)
                        else:
                            dve.wait_ge(projected, q * NI + NI)
                        st.done(v.tensor_copy(E[:, :, :, 0:1], rq[:, :, dr].unsqueeze(3)))
                        st.settle()
                        for lv in range(LEVELS):
                            m = 1 << lv
                            sh = [P, QUAD, m]
                            er, ei = E[:, 0, :, 0:m], E[:, 1, :, 0:m]
                            mr, mi = E[:, 0, :, m - 1:m].to_broadcast(sh), E[:, 1, :, m - 1:m].to_broadcast(sh)
                            nr, ni = E[:, 0, :, m:2 * m], E[:, 1, :, m:2 * m]
                            v.tensor_tensor(nr, er, mr, ALU.mult)
                            v.tensor_tensor(ni, er, mi, ALU.mult)
                            v.tensor_tensor(Ea[:, :, 0:m], ei, mi, ALU.mult)
                            st.done(v.tensor_tensor(Eb[:, :, 0:m], ei, mr, ALU.mult))
                            st.settle()
                            v.tensor_tensor(nr, nr, Ea[:, :, 0:m], ALU.subtract)
                            ins = v.tensor_tensor(ni, ni, Eb[:, :, 0:m], ALU.add)
                            st.done(ins)
                            st.settle()
                        dve.sem_inc(table, 1)
                    for i, (dr, p) in enumerate(ITEMS):
                        b = i % 2
                        dve.wait_ge(driven, q * NI + i + 1)
                        if i % QUAD == 0:
                            dve.wait_ge(laid, q * 3 + 2 + dr)
                        tc, ts = tab[:, dr, 0, p], tab[:, dr, 1, p]
                        br, bi = bu[:, b, 0, 0:T], bu[:, b, 1, 0:T]
                        v.tensor_tensor(m1[:, b], br, tc, ALU.mult)
                        v.tensor_tensor(m2[:, b], bi, ts, ALU.mult)
                        v.tensor_tensor(m3[:, b], bi, tc, ALU.mult)
                        ins = v.tensor_tensor(m4[:, b], br, ts, ALU.mult)
                        ins.then_inc(pre, 1)
                        dve.wait_ge(pre, q * NI + i + 3)
                        v.tensor_tensor(m1[:, b], m1[:, b], m2[:, b], ALU.add)
                        st.done(v.tensor_tensor(m3[:, b], m3[:, b], m4[:, b], ALU.subtract))
                        st.settle()
                        dve.wait_ge(xi, q * NI + i - 1) if i >= 2 else dve.wait_ge(projected, q * NI + NI)
                        for ri, src in ((0, m1), (1, m3)):
                            for c, lo_, hi_ in SEGS:
                                zz, ss = z[:, b, ri, lo_:hi_], src[:, b, lo_:hi_]
                                if dr:
                                    zz, ss = zz[:, ::-1], ss[:, ::-1]
                                init = hq[:, ri, dr, p:p + 1] if c else 0.0
                                ins = v.tensor_tensor_scan(zz, mg[:, dr, p:p + 1].to_broadcast([P, hi_ - lo_]), ss, init, ALU.mult, ALU.add)
                        ins.then_inc(zdone, 1)
                        dve.wait_ge(zdone, q * NI + i + 1)
                        v.tensor_tensor(n1[:, b], z[:, b, 0], tc, ALU.mult)
                        st.done(v.tensor_tensor(n2[:, b], z[:, b, 1], ts, ALU.mult))
                        st.settle()
                        dve.wait_ge(projected, q * NI + i + 1 + NI - 2)
                        dve.wait_ge(taken, q * NI + i + 1)
                        v.tensor_tensor(x[:, b, 0], n1[:, b], n2[:, b], ALU.subtract).then_inc(xr, 1)
                    dve.wait_ge(projected, q * NI + 2 * NI)
                    yq = y[:, bass.ds(q, 1), :].rearrange("p a t -> p (a t)")
                    ins = v.scalar_tensor_tensor(yq, uq[:], par.dskip[:, bass.ds(q, 1)], yp[:, 0:T], ALU.mult, ALU.add)
                    ins.then_inc(ydone, 1)
                    used = st.n
                assert used == DVE_OWN


def glu_inputs(nc, sems, cx, y, hi, lo):
    with Stage(nc, sems, "gin") as s:
        g = s.sb("g", [P, KC, T])
        gelud, own = s.sem("gelu"), s.sem("dve")
        with nc.Block() as block:
            @block.scalar
            def _(act):
                for k in range(KC):
                    nc.scalar.activation(g[:, k], y[:, k], ACT.Gelu_apprx_tanh).then_inc(gelud, 1)

            @block.vector
            def _(dve):
                for k in range(KC):
                    dve.wait_ge(gelud, k + 1)
                    ins = hi_part(nc, hi[:, k], g[:, k])
                ins.then_inc(own, 1)
                dve.wait_ge(own, 1)
                lo_part(nc, lo[:], g[:], hi[:])


def glu(nc, sems, cx, zz, m):
    with Stage(nc, sems, "glu") as s:
        sg = s.sb("sg", [P, KC, T])
        sig = s.sem("sigmoid")
        with nc.Block() as block:
            @block.scalar
            def _(act):
                for k in range(KC):
                    nc.scalar.activation(sg[:, k], zz[:, KC + k], ACT.Sigmoid).then_inc(sig, 1)

            @block.vector
            def _(dve):
                for k in range(KC):
                    dve.wait_ge(sig, k + 1)
                    nc.vector.tensor_tensor(m[:, k], sg[:, k], zz[:, k], ALU.mult)


class Context:

    def mod(self, layer, j):
        return self.modT[:, layer * MODS + j * KC:layer * MODS + (j + 1) * KC, :]


class S5Parameters:
    pass


def peer(nc, sems, cx, d, layer):
    groups = NKEYS // IB
    with Stage(nc, sems, f"peer{layer}") as s:
        hi, lo = s.sb("hi", [P, KC, T]), s.sb("lo", [P, KC, T])
        picks = s.sb("i1T", [P, T], F16), s.sb("i2T", [P, T], F16), s.sb("gh", [P, T]), s.sb("gl", [P, T])
        norm(nc, sems, cx, f"n{layer}1", hi, lo, layer, 1)
        with Stage(nc, sems, f"pq{layer}") as s2:
            q = s2.sb("q", [P, 2 * PH, T])
            linear(nc, sems, f"ql{layer}", d["w_query"][layer], 2 * PH, hi, lo, q)
            retrieve(nc, sems, cx, f"ret{layer}", d["sub_keys"][layer], q, *picks)
        acc = s.ps("acc", [P, 2 * NT, 512])
        with Stage(nc, sems, f"pe{layer}") as s3:
            A = s3.sb("A", [P, 2, IB, T])
            with nc.Block() as block:
                @block.vector
                def _(dve):
                    nc.vector.memset(acc[:], 0.0)
            for step in range(groups + 2):
                of = lambda g: g if 0 <= g < groups else None
                experts(nc, sems, cx, f"ex{layer}{step}", d, layer, hi, lo, picks, A, acc,
                        score=of(step), gate=of(step - 1), value=of(step - 2))
        add_experts(nc, sems, cx, f"ad{layer}", layer, acc)


def build(nc, d):
    sems = Semaphores(nc)
    with Stage(nc, sems, "g") as g:
        cx = Context()
        cx.const, cx.x = g.sb("const", [P, C_KEEP]), g.sb("x", [P, KC, T])
        cx.modT, cx.scale = g.sb("modT", [P, 2 * MODS, 2]), g.sb("scale", [P, 2, 2, KC, 2])
        cx.ones, cx.eps, cx.finalg = g.sb("ones", [P, P]), g.sb("eps", [P, 1]), g.sb("finalg", [P, KC])
        cx.iota = g.sb("iota", [P, P], F16)
        cx.ident = cx.const[:, C_ID:C_ID + P]
        modulation(nc, sems, cx, d)

        with Stage(nc, sems, "l0") as s:
            hi, lo, y, v = s.sb("hi", [P, KC, T]), s.sb("lo", [P, KC, T]), s.sb("y", [P, 18, T]), s.sb("v", [P, NT, 2, 512])
            cx.const0 = s.sb("const0", [P, C_ALL - C_KEEP])
            norm(nc, sems, cx, "n00", hi, lo, 0, 0)
            linear(nc, sems, "in0", d["w_in0"], 18, hi, lo, y)
            values(nc, sems, cx, d, hi, lo, v)
            with Stage(nc, sems, "o0") as s2:
                o = s2.sb("o", [P, HEADS, T])
                rope(nc, sems, cx, y)
                attention(nc, sems, cx, d, y, v, o)
                head_norm(nc, sems, cx, "dan", o, d["subln_g"], 1.0 - (0.8 - 0.6 * math.exp(-0.3 * 0)), hi[:, 0:HEADS], lo[:, 0:HEADS])
                gla(nc, sems, cx, d, y, v, o)
                head_norm(nc, sems, cx, "gln", o, d["gla_g"], 1.0, hi[:, HEADS:KC], lo[:, HEADS:KC], r=y[:, 12:16])
            m = y[:, 0:KC]
            linear(nc, sems, "out0", d["w_out0"], KC, hi, lo, m)
            residual(nc, sems, cx, "r0", m, 0)
        sems.clear()
        peer(nc, sems, cx, d, 0)
        sems.clear()

        with Stage(nc, sems, "l1") as s:
            hi, lo, zz = s.sb("hi", [P, KC, T]), s.sb("lo", [P, KC, T]), s.sb("zz", [P, 2 * KC, T])
            u, y = zz[:, 0:KC], zz[:, KC:2 * KC]
            norm(nc, sems, cx, "n10", hi, lo, 1, 0)
            linear(nc, sems, "in1", d["s5_w_in"], KC, hi, lo, u)
            with Stage(nc, sems, "s5o") as s2:
                par = S5Parameters()
                par.mag, par.dskip = s2.sb("mag", [P, NPD]), s2.sb("dskip", [P, KC])
                par.rot, par.coef, par.h0 = s2.sb("rot", [P, 2, NPD]), s2.sb("coef", [P, 2, NPD]), s2.sb("h0", [P, 2, NPD])
                fin = s2.sb("fin", [P, 2, NPD])
                stored = s2.sem("stored")
                s5_parameters(nc, sems, cx, d, par)
                s5_scan(nc, sems, cx, d, u, par, y, fin)
                with nc.Block() as block:
                    @block.sync
                    def _(sp):
                        sp.dma_start(d["new_s5"], fin[:]).then_inc(stored, 16)
                        sp.wait_ge(stored, 16)
            glu_inputs(nc, sems, cx, y, hi, lo)
            linear(nc, sems, "out1", d["s5_w_out"], 2 * KC, hi, lo, zz)
            m = s.sb("m", [P, KC, T])
            glu(nc, sems, cx, zz, m)
            residual(nc, sems, cx, "r1", m, 1)
        sems.clear()
        peer(nc, sems, cx, d, 1)
        norm(nc, sems, cx, "fin", None, None, final=d["y"])


def residual(nc, sems, cx, name, m, layer):
    with nc.Block() as block:
        @block.vector
        def _(dve):
            for k in range(KC):
                for c, a, b in SEGS:
                    x = cx.x[:, k, a:b]
                    nc.vector.scalar_tensor_tensor(x, m[:, k, a:b], cx.mod(layer, 2)[:, k, c:c + 1], x, ALU.mult, ALU.add)


def col_tiles(w):
    k, n = w.shape
    return np.ascontiguousarray(w.reshape(k // P, P, n // P, P).transpose(2, 1, 0, 3))


def on_partitions(v):
    return np.ascontiguousarray(np.moveaxis(v.reshape(v.shape[:-1] + (-1, P)), -1, 0))


def by_pair(a):
    a = a.reshape((2, NPAIR, 2, 64) + a.shape[3:])
    return np.ascontiguousarray(np.moveaxis(a, (2, 3), (0, 1)).reshape((P, 2, NPAIR) + a.shape[4:]))


def layouts(i):
    d = {}
    x = np.concatenate([i["x_prompt"][0], i["x_sample"][0]], 0)
    d["x"] = np.ascontiguousarray(x.reshape(T, KC, P).transpose(2, 1, 0))
    d["cond"] = np.ascontiguousarray(np.stack([i["c_ctx"], i["c"][0]], 0).reshape(2, KC, P).transpose(2, 1, 0))
    d["consts"] = constants()
    d["ada_w"] = np.ascontiguousarray(i["ada_w"].reshape(2, KC, P, 12, 512).transpose(0, 3, 2, 1, 4)).reshape(24, P, KC, 512)
    d["ada_b"] = on_partitions(i["ada_b"])
    d["norm_g"] = on_partitions(i["norm_g"].reshape(4, D))
    d["final_g"] = on_partitions(i["final_norm_g"])
    w = i["mix0_w_in"][0]
    low = np.zeros((D, 2 * P), np.float32)
    low[:, 0:16], low[:, P:P + 16] = w[:, 3072:3088], w[:, 3088:3104]
    d["w_in0"] = col_tiles(np.concatenate([w[:, 0:1024], w[:, 1536:2048], w[:, 2560:3072], low], 1))
    vw = np.stack([w[:, 1024:1536], w[:, 2048:2560]])
    d["w_v"] = np.ascontiguousarray(vw.reshape(2, KC, P, 512).transpose(0, 2, 1, 3))
    d["w_out0"] = col_tiles(i["mix0_w_out"][0])
    d["da_lam"] = np.ascontiguousarray(np.broadcast_to(i["da_lam"], (P, 4, 64)))
    d["subln_g"] = i["da_subln_g"].reshape(P, 1)
    d["gla_g"] = i["gla_norm_g"].reshape(P, 1)
    d["cache_k"] = np.ascontiguousarray(i["cache_da_k"][0, 0].reshape(P, HEADS, P).transpose(2, 1, 0))
    d["cache_v"] = i["cache_da_v"][0, 0].reshape(P, 512)
    d["gate_up"] = np.ascontiguousarray(i["gla_gate_up"][0].transpose(1, 0, 2))
    d["gate_bias"] = np.ascontiguousarray(i["gla_gate_bias"][0].reshape(4, P).T)
    d["state_gla"] = np.ascontiguousarray(i["state_gla"][0, 0].reshape(4, P, P).transpose(1, 0, 2))
    d["s5_w_in"], d["s5_w_out"] = col_tiles(i["s5_w_in"][0]), col_tiles(i["s5_w_out"][0])
    dt = np.broadcast_to(i["s5_log_dt"][0][:, :, None], (2, 64, 64))
    d["s5_par"] = np.stack([by_pair(a).reshape(P, NPD) for a in (i["s5_a_re"][0], i["s5_a_im"][0], dt)], 1)
    d["state_s5"] = np.stack([by_pair(i["state_s5"][0, 0, ..., r]).reshape(P, NPD) for r in range(2)], 1)
    d["s5_d"] = on_partitions(i["s5_d"][0])
    for name, re, im in (("s5_b", i["s5_b_re"][0], i["s5_b_im"][0]),
                         ("s5_c", i["s5_c_re"][0].transpose(0, 1, 3, 2), i["s5_c_im"][0].transpose(0, 1, 3, 2))):
        both = np.zeros((2, 2, 64, 2, NPAIR, 2, 16), np.float32)
        for ri, a in enumerate((re, im)):
            pair = a.reshape(2, NPAIR, 2, 64, 16)
            for gg in range(2):
                both[ri, gg, :, :, :, gg, :] = pair[:, :, gg].transpose(2, 0, 1, 3)
        w = both.reshape(2, P, 2, KC, QUAD, 32).transpose(3, 1, 0, 2, 4, 5)
        d[name] = np.ascontiguousarray(w.reshape(KC, P, 2, 2, QUAD * 32) if name == "s5_b" else w)
    d["w_query"] = np.stack([col_tiles(w) for w in i["peer_w_query"]])
    d["sub_keys"] = np.ascontiguousarray(i["peer_sub_keys"].reshape(2, 2 * PH, NKEYS, P).transpose(0, 3, 1, 2))
    u = i["peer_u"].reshape(2, NKEYS, NKEYS, KC, P)
    d["peer_u"] = np.ascontiguousarray(u.transpose(0, 2, 4, 3, 1)).reshape(2, NKEYS, P, D)
    d["peer_v"] = np.ascontiguousarray(i["peer_v"].reshape(2, NKEYS, NKEYS, D).transpose(0, 2, 1, 3))
    return d


OUTS = {"y": (P, KC, T), "new_k": (P, HEADS, P), "new_v": (P, 512), "new_gla": (P, 4, P), "new_s5": (P, 2, NPD)}


def kernel(**inputs):
    import concourse.bacc as bacc
    from concourse.bass_utils import run_bass_kernel_spmd

    nc = bacc.Bacc("TRN2", target_bir_lowering=False, num_devices=1)
    arrays = layouts({k: np.asarray(v) for k, v in inputs.items()})
    d = {k: nc.dram_tensor(f"in_{k}", a.shape, F32, kind="ExternalInput").ap() for k, a in arrays.items()}
    d.update({k: nc.dram_tensor(f"out_{k}", s, F32, kind="ExternalOutput").ap() for k, s in OUTS.items()})
    build(nc, d)
    r = run_bass_kernel_spmd(nc, [{f"in_{k}": a for k, a in arrays.items()}], core_ids=[0]).results[0]
    y = r["out_y"].transpose(2, 1, 0).reshape(T, D)
    s5 = r["out_new_s5"].reshape(2, 64, 2, 2, NPAIR)
    return (
        y[None, :TP], y[None, TP:],
        r["out_new_k"].reshape(1, 1, P, 2 * HEADS, 64),
        r["out_new_v"].reshape(1, 1, P, HEADS, P),
        r["out_new_gla"].transpose(1, 0, 2).reshape(1, 1, 2, HEADS, 64, P),
        np.ascontiguousarray(s5.transpose(3, 4, 0, 1, 2)).reshape(1, 1, 2, 64, 64, 2),
    )
```

```python
import math
from contextlib import ExitStack

import numpy as np
import concourse.bass as bass
from concourse import mybir
from concourse.alu_op_type import AluOpType as ALU

ACT = mybir.ActivationFunctionType
F32 = mybir.dt.float32
F32R = mybir.dt.float32r
F16 = mybir.dt.float16
I32 = mybir.dt.int32
U32 = mybir.dt.uint32
X_AXIS = mybir.AxisListType.X

P = 128
D = 1024
KC = D // P
T = 384
TP = 128
NT = T // P
SEGS = ((0, 0, TP), (1, TP, T))
EPS = 1e-6
HEADS = 4
CHUNK = 64
NCH = T // CHUNK
PH = 8
TOPK = 16
NKEYS = 128
NEG = -3.0e38
GATE_SCALE = 1024.0
MODS = 6 * KC

CAND_LEN = [TOPK // (a + 1) for a in range(TOPK)]
CAND_START = [sum(CAND_LEN[:a]) for a in range(TOPK)]
NCAND = sum(CAND_LEN)

C_ID, C_ST, C_LEN, C_I16, C_IOTA = 0, 128, 144, 160, 176
C_KEEP = 304
C_ROT, C_MF, C_MB, C_CH, C_COS, C_SIN = 304, 432, 560, 688, 1072, 1328
C_ALL = 1584


def constants():
    c = np.zeros((P, C_ALL), np.float32)
    c[:, C_ID:C_ID + P] = np.eye(P)
    r = np.zeros((P, P), np.float32)
    for d in range(P):
        if d % 32 < 16:
            r[d, d + 16] = -1.0
        else:
            r[d, d - 16] = 1.0
    c[:, C_ROT:C_ROT + P] = r.T
    c[:, C_IOTA:C_IOTA + P] = np.arange(P)
    s, t = np.meshgrid(np.arange(P), np.arange(P), indexing="ij")
    same = s // CHUNK == t // CHUNK
    c[:, C_MF:C_MF + P] = same & (s <= t)
    c[:, C_MB:C_MB + P] = same & (s >= t)
    c[:, C_CH:C_CH + T] = np.arange(T) % CHUNK != 0
    c[:, C_ST:C_ST + 16] = CAND_START
    c[:, C_LEN + 1:C_LEN + 16] = CAND_LEN[:15]
    c[:, C_I16:C_I16 + 16] = np.arange(16)
    pos = np.arange(256)
    inv = 10000.0 ** (-np.arange(16, dtype=np.float32) / 16)
    row = (pos // 64).astype(np.float32)[:, None] * inv
    col = (pos % 64).astype(np.float32)[:, None] * inv
    ang = np.concatenate([row, row, col, col], 1).T
    c[:, C_COS:C_COS + 256] = np.tile(np.cos(ang), (2, 1))
    c[:, C_SIN:C_SIN + 256] = np.tile(np.sin(ang), (2, 1))
    return c


class Stage:

    def __init__(self, nc, sems, name):
        self.nc, self.sems, self.name, self.mem = nc, sems, name, ExitStack()

    def __enter__(self):
        return self

    def __exit__(self, *e):
        return self.mem.__exit__(*e)

    def sb(self, name, shape, dt=F32):
        return self.mem.enter_context(self.nc.sbuf_tensor(f"{self.name}_{name}", shape, dt))

    def ps(self, name, shape):
        return self.mem.enter_context(self.nc.psum_tensor(f"{self.name}_{name}", shape, F32))

    def sem(self, name):
        return self.sems.new(f"{self.name}_{name}")


class Semaphores:

    def __init__(self, nc):
        self.nc, self.taken = nc, []

    def new(self, name):
        self.taken.append(self.nc.alloc_semaphore(name))
        return self.taken[-1]

    def clear(self):
        self.nc.clear_and_free_semaphores(self.taken)
        self.nc.all_engine_barrier()
        self.taken = []


class Steps:

    def __init__(self, eng, sem, base=0):
        self.eng, self.sem, self.base, self.n = eng, sem, base, 0

    def done(self, ins):
        self.n += 1
        ins.then_inc(self.sem, 1)
        return ins

    def settle(self):
        self.eng.wait_ge(self.sem, self.base + self.n)


def r32(ap):
    return ap.bitcast(F32R)


def hi_part(nc, out, x):
    return nc.vector.tensor_copy(r32(out), x)


def lo_part(nc, out, x, hi):
    return nc.vector.tensor_tensor(r32(out), x, hi, ALU.subtract)


def modulation(nc, sems, cx, d):
    NW = 3
    N = 2 * 12
    with Stage(nc, sems, "mod") as s:
        w = s.sb("w", [P, NW, KC, 512])
        bias, cond, sg, row = s.sb("bias", [P, 2, MODS]), s.sb("cond", [P, KC, 2]), s.sb("sg", [P, KC, 2]), s.sb("row", [P, NW, 512])
        normg = s.sb("normg", [P, 4, KC])
        one = s.sb("one", [P, 2, 2, KC, 2])
        acc, tr = s.ps("acc", [P, NW, 512]), s.ps("tr", [P, NW, 512])
        small, loaded = s.sem("small"), [s.sem(f"w{i}_loaded") for i in range(NW)]
        sig, silu = s.sem("sigmoid"), s.sem("silu")
        summed, copied, turned, stored = s.sem("summed"), s.sem("copied"), s.sem("turned"), s.sem("stored")
        own, cleared = s.sem("dve"), s.sem("rows_cleared")
        with nc.Block() as block:
            @block.sync
            def _(sp):
                sp.dma_start(cond[:], d["cond"]).then_inc(small, 16)
                sp.dma_start(cx.const[:], d["consts"][:, 0:C_KEEP]).then_inc(small, 16)
                sp.dma_start(bias[:], d["ada_b"]).then_inc(small, 16)
                sp.dma_start(normg[:], d["norm_g"]).then_inc(small, 16)
                sp.dma_start(cx.x[:], d["x"]).then_inc(small, 16)
                sp.dma_start(cx.finalg[:], d["final_g"]).then_inc(small, 16)
                with sp.Fori(0, N // NW) as i:
                    for u in range(NW):
                        sp.wait_ge(summed, i * NW + u + 1)
                        sp.dma_start(w[:, u], d["ada_w"][bass.ds(i * NW + u, 1)].rearrange("a p k n -> p (a k) n")).then_inc(loaded[u], 16)

            @block.tensor
            def _(pe):
                pe.sem_inc(summed, NW)
                pe.sem_inc(turned, NW)
                pe.wait_ge(silu, 1)
                with pe.Fori(0, N // NW) as i:
                    for u in range(NW):
                        pe.wait_ge(loaded[u], i * 16 + 16)
                        pe.wait_ge(copied, i * NW + u + 1)
                        for k in range(KC):
                            mm = pe.matmul(acc[0:2, u, :], sg[:, k, :], w[:, u, k, :], start=k == 0, stop=k == KC - 1)
                        mm.then_inc(summed, 1)
                    for u in range(NW):
                        pe.wait_ge(copied, i * NW + u + 1 + NW)
                        pe.wait_ge(stored, i * NW + u + 1)
                        for b in range(4):
                            mm = pe.transpose(tr[:, u, b * P:(b + 1) * P], row[:, u, b * P:(b + 1) * P], cx.ident)
                        mm.then_inc(turned, 1)

            @block.scalar
            def _(act):
                act.sem_inc(copied, NW)
                act.wait_ge(cleared, 1)
                act.wait_ge(small, 96)
                nc.scalar.activation(sg[:], cond[:], ACT.Sigmoid).then_inc(sig, 1)
                with act.Fori(0, N // NW) as i:
                    for u in range(NW):
                        act.wait_ge(summed, i * NW + u + 1 + NW)
                        act.wait_ge(turned, i * NW + u + 1)
                        nc.scalar.activation(row[0:2, u], acc[0:2, u, :], ACT.Copy).then_inc(copied, 1)

            @block.vector
            def _(dve):
                dve.sem_inc(stored, NW)
                st = Steps(dve, own)
                nc.vector.memset(row[:], 0.0).then_inc(cleared, 1)
                st.done(nc.vector.memset(cx.ones[:], 1.0))
                st.done(nc.vector.memset(cx.eps[:], EPS))
                dve.wait_ge(small, 96)
                st.done(nc.vector.tensor_copy(cx.iota[:], cx.const[:, C_IOTA:C_IOTA + P]))
                dve.wait_ge(sig, 1)
                nc.vector.tensor_tensor(sg[:], sg[:], cond[:], ALU.mult).then_inc(silu, 1)
                with dve.Fori(0, N // NW) as i:
                    for u in range(NW):
                        dve.wait_ge(turned, i * NW + u + 1 + NW)
                        nc.vector.tensor_copy(cx.modT[:, bass.ds((i * NW + u) * 4, 4), :],
                                              tr[:, u].rearrange("p (b c) -> p b c", b=4)[:, :, 0:2]).then_inc(stored, 1)
                dve.wait_ge(stored, N + NW)
                m = cx.modT[:]
                st.done(nc.vector.tensor_tensor(m, m, bias[:].rearrange("p l j -> p (l j)").unsqueeze(2).to_broadcast([P, 2 * MODS, 2]), ALU.add))
                st.settle()
                for l in range(2):
                    for h in range(2):
                        st.done(nc.vector.tensor_scalar(one[:, l, h], cx.mod(l, 3 * h + 1), 1.0, None, ALU.add))
                st.settle()
                for l in range(2):
                    for h in range(2):
                        st.done(nc.vector.tensor_tensor(cx.scale[:, l, h], one[:, l, h],
                                                        normg[:, 2 * l + h].unsqueeze(2).to_broadcast([P, KC, 2]), ALU.mult))


def norm(nc, sems, cx, name, hi, lo, layer=0, which=0, m=None, gate=None, final=None):
    with Stage(nc, sems, name) as s:
        sq, root, rstd, h = s.sb("sq", [P, KC, T]), s.sb("root", [P, T]), s.sb("rstd", [P, T]), s.sb("h", [P, KC, T])
        ss = s.ps("ss", [P, T])
        ready, squared, summed, rooted, own, stored = (s.sem(x) for x in ("x_ready", "squared", "summed", "rooted", "dve", "stored"))
        with nc.Block() as block:
            @block.tensor
            def _(pe):
                for k in range(KC):
                    pe.wait_ge(squared, k + 1)
                    mm = pe.matmul(ss[:], cx.ones[:], sq[:, k], start=k == 0, stop=k == KC - 1)
                mm.then_inc(summed, 1)

            @block.scalar
            def _(act):
                for k in range(KC):
                    act.wait_ge(ready, k + 1)
                    nc.scalar.activation(sq[:, k], cx.x[:, k], ACT.Square).then_inc(squared, 1)
                act.wait_ge(summed, 1)
                nc.scalar.activation(root[:], ss[:], ACT.Sqrt, bias=cx.eps[:, 0:1], scale=1.0 / D).then_inc(rooted, 1)

            @block.vector
            def _(dve):
                st = Steps(dve, own)
                if m is None:
                    dve.sem_inc(ready, KC)
                else:
                    for k in range(KC):
                        for c, a, b in SEGS:
                            x = cx.x[:, k, a:b]
                            ins = nc.vector.scalar_tensor_tensor(x, m[:, k, a:b], cx.mod(layer if gate is None else gate[0], gate[1])[:, k, c:c + 1], x, ALU.mult, ALU.add)
                            if c == 0:
                                st.done(ins)
                        ins.then_inc(ready, 1)
                dve.wait_ge(rooted, 1)
                st.done(nc.vector.reciprocal(rstd[:], root[:]))
                st.settle()
                dve.wait_ge(ready, KC)
                st.done(nc.vector.tensor_tensor(h[:], cx.x[:], rstd[:].unsqueeze(1).to_broadcast([P, KC, T]), ALU.mult))
                st.settle()
                for k in range(KC):
                    if final is not None:
                        nc.vector.tensor_scalar(h[:, k], h[:, k], cx.finalg[:, k:k + 1], None, ALU.mult).then_inc(stored, 1)
                        continue
                    for c, a, b in SEGS:
                        st.done(nc.vector.tensor_scalar(h[:, k, a:b], h[:, k, a:b], cx.scale[:, layer, which, k, c:c + 1],
                                                        cx.mod(layer, 3 * which)[:, k, c:c + 1], ALU.mult, ALU.add))
                if final is None:
                    st.settle()
                    st.done(hi_part(nc, hi[:], h[:]))
                    st.settle()
                    st.done(lo_part(nc, lo[:], h[:], hi[:]))

            if final is not None:
                @block.sync
                def _(sp):
                    sp.wait_ge(stored, KC)
                    sp.dma_start(final, h[:]).then_inc(ready, 16)
                    sp.wait_ge(ready, KC + 16)


def linear(nc, sems, name, w_dram, n, hi, lo, out):
    NW = 3 if n % 3 == 0 else 4
    with Stage(nc, sems, name) as s:
        w, wh, wl = (s.sb(x, [P, NW, KC, P]) for x in ("w", "wh", "wl"))
        acc = s.ps("acc", [P, NW, 512])
        loaded = [s.sem(f"w{i}_loaded") for i in range(NW)]
        masked, split, summed, copied = (s.sem(x) for x in ("masked", "split", "summed", "copied"))
        with nc.Block() as block:
            @block.sync
            def _(sp):
                with sp.Fori(0, n // NW) as i:
                    for u in range(NW):
                        sp.wait_ge(split, i * NW + u + 1)
                        sp.dma_start(w[:, u], w_dram[bass.ds(i * NW + u, 1)].rearrange("a p k m -> p (a k) m")).then_inc(loaded[u], 16)

            @block.vector
            def _(dve):
                dve.sem_inc(split, NW)
                with dve.Fori(0, n // NW) as i:
                    for u in range(NW):
                        dve.wait_ge(loaded[u], i * 16 + 16)
                        dve.wait_ge(summed, i * NW + u + 1)
                        hi_part(nc, wh[:, u], w[:, u]).then_inc(masked, 1)
                        dve.wait_ge(masked, i * NW + u + 1)
                        lo_part(nc, wl[:, u], w[:, u], wh[:, u]).then_inc(split, 1)

            @block.tensor
            def _(pe):
                pe.sem_inc(summed, NW)
                with pe.Fori(0, n // NW) as i:
                    for u in range(NW):
                        pe.wait_ge(split, i * NW + u + 1 + NW)
                        pe.wait_ge(copied, i * NW + u + 1)
                        for k in range(KC):
                            o = acc[:, u, 0:T]
                            pe.matmul(o, r32(wh[:, u, k]), r32(hi[:, k]), start=k == 0, stop=False)
                            pe.matmul(o, r32(wh[:, u, k]), r32(lo[:, k]), start=False, stop=False)
                            mm = pe.matmul(o, r32(wl[:, u, k]), r32(hi[:, k]), start=False, stop=k == KC - 1)
                        mm.then_inc(summed, 1)

            @block.scalar
            def _(act):
                act.sem_inc(copied, NW)
                with act.Fori(0, n // NW) as i:
                    for u in range(NW):
                        act.wait_ge(summed, i * NW + u + 1 + NW)
                        nc.scalar.activation(out[:, bass.ds(i * NW + u, 1)].rearrange("p a t -> p (a t)"), acc[:, u, 0:T], ACT.Copy).then_inc(copied, 1)


def values(nc, sems, cx, d, hi, lo, v):
    with Stage(nc, sems, "val") as s:
        w, wh, wl = (s.sb(x, [P, 2, KC, 512]) for x in ("w", "wh", "wl"))
        acc = s.ps("acc", [P, 6, 512])
        loaded, split, masked, summed = [s.sem("w0_loaded"), s.sem("w1_loaded")], s.sem("split"), s.sem("masked"), s.sem("summed")
        tables = s.sem("tables_loaded")
        with nc.Block() as block:
            @block.sync
            def _(sp):
                for j in range(2):
                    sp.dma_start(w[:, j], d["w_v"][j]).then_inc(loaded[j], 16)
                sp.dma_start(cx.const0[:], d["consts"][:, C_KEEP:C_ALL]).then_inc(tables, 16)
                sp.wait_ge(tables, 16)

            @block.vector
            def _(dve):
                for j in range(2):
                    dve.wait_ge(loaded[j], 16)
                    hi_part(nc, wh[:, j], w[:, j]).then_inc(masked, 1)
                    dve.wait_ge(masked, j + 1)
                    lo_part(nc, wl[:, j], w[:, j], wh[:, j]).then_inc(split, 1)

            @block.tensor
            def _(pe):
                for j in range(2):
                    pe.wait_ge(split, j + 1)
                    for t in range(NT):
                        o, cols = acc[:, 3 * j + t, :], slice(t * P, (t + 1) * P)
                        for k in range(KC):
                            pe.matmul(o, r32(hi[:, k, cols]), r32(wh[:, j, k]), start=k == 0, stop=False)
                            pe.matmul(o, r32(hi[:, k, cols]), r32(wl[:, j, k]), start=False, stop=False)
                            mm = pe.matmul(o, r32(lo[:, k, cols]), r32(wh[:, j, k]), start=False, stop=k == KC - 1)
                        mm.then_inc(summed, 1)

            @block.scalar
            def _(act):
                for j in range(2):
                    for t in range(NT):
                        act.wait_ge(summed, 3 * j + t + 1)
                        nc.scalar.activation(v[:, t, j, :], acc[:, 3 * j + t, :], ACT.Copy)


def rope(nc, sems, cx, y):
    LS = T - TP
    with Stage(nc, sems, "rope") as s:
        rot = s.ps("rot", [P, 4, 512])
        a, b = s.sb("a", [P, 4, LS]), s.sb("b", [P, 4, LS])
        turned, own = s.sem("turned"), s.sem("dve")
        with nc.Block() as block:
            @block.tensor
            def _(pe):
                for j in range(8):
                    if j >= 4:
                        pe.wait_ge(own, 3 * (j - 3))
                    pe.matmul(rot[:, j % 4, 0:LS], cx.const0[:, C_ROT - C_KEEP:C_ROT - C_KEEP + P], y[:, j, TP:T], start=True, stop=True).then_inc(turned, 1)

            @block.vector
            def _(dve):
                for j in range(8):
                    dve.wait_ge(turned, j + 1)
                    nc.vector.tensor_tensor(a[:, j % 4], y[:, j, TP:T], cx.const0[:, C_COS - C_KEEP:C_COS - C_KEEP + LS], ALU.mult).then_inc(own, 1)
                    nc.vector.tensor_tensor(b[:, j % 4], rot[:, j % 4, 0:LS], cx.const0[:, C_SIN - C_KEEP:C_SIN - C_KEEP + LS], ALU.mult).then_inc(own, 1)
                    dve.wait_ge(own, 3 * j + 2)
                    nc.vector.tensor_tensor(y[:, j, TP:T], a[:, j % 4], b[:, j % 4], ALU.add).then_inc(own, 1)


def attention(nc, sems, cx, d, y, v, o):
    SC = 64 ** -0.5
    LAM0 = 0.8 - 0.6 * math.exp(-0.3 * 0)
    items = [(h, q) for h in range(HEADS) for q in range(NT)]
    nk = [P if q == 0 else T for _, q in items]
    with Stage(nc, sems, "att") as s:
        ck, cv = s.sb("ck", [P, HEADS, P]), s.sb("cv", [P, 512])
        lp, lq = s.sb("lp", [P, 4, 64]), s.sb("lq", [P, 2, 64])
        ls, lam = s.sb("ls", [P, 2]), s.sb("lam", [P, 1])
        mx, nm, den, rd, rl = (s.sb(n, [P, 2, 2]) for n in ("mx", "nm", "den", "rd", "rl"))
        e, a, tt, at = s.sb("e", [P, 2, 2, T]), s.sb("a", [P, 2, T]), s.sb("tt", [P, 2, T]), s.sb("at", [P, 2, T])
        kn = s.sb("kn", [P, HEADS, P])
        sc, tr, ob = s.ps("sc", [P, 2, 2, 512]), s.ps("tr", [P, 2, 512]), s.ps("ob", [P, 2, 512])
        loaded, out = s.sem("caches_loaded"), s.sem("k_v_stored")
        lexp, own = s.sem("lam_exp"), s.sem("dve")
        scored, maxed, expd, mixed, turned, tcopied, attended, ocopied = (
            s.sem(x) for x in ("scored", "maxed", "exp", "mixed", "turned", "turned_copied", "attended", "o_copied"))
        kturned, kcopied, lsum = s.sem("k_turned"), s.sem("k_copied"), s.sem("lam_sums")
        with nc.Block() as block:
            @block.sync
            def _(sp):
                sp.dma_start(lp[:], d["da_lam"]).then_inc(loaded, 16)
                sp.dma_start(ck[:], d["cache_k"]).then_inc(loaded, 16)
                sp.dma_start(cv[:], d["cache_v"]).then_inc(loaded, 16)
                sp.dma_start(d["new_v"], v[:, 0, 0, :]).then_inc(out, 16)
                sp.wait_ge(kcopied, 1)
                sp.dma_start(d["new_k"], kn[:]).then_inc(out, 16)
                sp.wait_ge(out, 32)

            @block.tensor
            def _(pe):
                def scores(i):
                    h, q = items[i]
                    if i >= 2:
                        pe.wait_ge(expd, i - 1)
                    for m in range(2):
                        r = slice(64 * m, 64 * m + 64)
                        lhs = y[r, h, q * P:(q + 1) * P]
                        own_keys = slice(0, P) if q == 0 else slice(TP, T)
                        n = own_keys.stop - own_keys.start
                        mm = pe.matmul(sc[:, i % 2, m, 0:n], lhs, y[r, HEADS + h, own_keys], start=True, stop=True)
                        if q:
                            mm = pe.matmul(sc[:, i % 2, m, n:T], lhs, ck[r, h, :], start=True, stop=True)
                    mm.then_inc(scored, 1)

                pe.wait_ge(loaded, 48)
                for h in range(HEADS):
                    mm = pe.transpose(tr[:, 0, h * P:(h + 1) * P], y[:, HEADS + h, 0:TP], cx.ident)
                mm.then_inc(kturned, 1)
                pe.wait_ge(kcopied, 1)
                scores(0)
                for i, (h, q) in enumerate(items):
                    if i + 1 < len(items):
                        scores(i + 1)
                    pe.wait_ge(mixed, i + 1)
                    if i >= 2:
                        pe.wait_ge(tcopied, i - 1)
                    for j in range(nk[i] // P):
                        mm = pe.transpose(tr[:, i % 2, j * P:(j + 1) * P], a[:, i % 2, j * P:(j + 1) * P], cx.ident)
                    mm.then_inc(turned, 1)
                    pe.wait_ge(tcopied, i + 1)
                    if q == 0 and h >= 2:
                        pe.wait_ge(ocopied, h - 1)
                    for j in range(nk[i] // P):
                        vals = v[:, 0 if q == 0 else 1 + j, 0, h * P:(h + 1) * P] if j < 2 else cv[:, h * P:(h + 1) * P]
                        mm = pe.matmul(ob[:, h % 2, q * P:(q + 1) * P], vals, at[:, i % 2, j * P:(j + 1) * P],
                                       start=j == 0, stop=j == nk[i] // P - 1)
                    mm.then_inc(attended, 1)

            @block.vector
            def _(dve):
                st = Steps(dve, own)
                dve.wait_ge(loaded, 48)
                st.done(nc.vector.tensor_tensor(lq[:], lp[:, 0:4:2], lp[:, 1:4:2], ALU.mult))
                st.settle()
                nc.vector.tensor_reduce(ls[:], lq[:], X_AXIS, ALU.add).then_inc(lsum, 1)
                dve.wait_ge(lexp, 1)
                st.done(nc.vector.tensor_tensor(lam[:], ls[:, 0:1], ls[:, 1:2], ALU.subtract))
                st.settle()
                st.done(nc.vector.tensor_scalar(lam[:], lam[:], LAM0, None, ALU.add))
                st.settle()

                def maxima(i):
                    dve.wait_ge(scored, i + 1)
                    st.done(nc.vector.tensor_reduce(mx[:, i % 2], sc[:, i % 2, :, 0:nk[i]], X_AXIS, ALU.max))
                    st.settle()
                    if i >= 2:
                        dve.wait_ge(expd, i - 1)
                    nc.vector.tensor_scalar(nm[:, i % 2], mx[:, i % 2], -SC, None, ALU.mult).then_inc(maxed, 1)

                maxima(0)
                for i in range(len(items)):
                    if i + 1 < len(items):
                        maxima(i + 1)
                    n, b = nk[i], i % 2
                    dve.wait_ge(expd, i + 1)
                    st.done(nc.vector.reciprocal(rd[:, b], den[:, b]))
                    st.settle()
                    st.done(nc.vector.tensor_tensor(rl[:, b, 0:1], rd[:, b, 1:2], lam[:], ALU.mult))
                    st.settle()
                    st.done(nc.vector.tensor_scalar(tt[:, b, 0:n], e[:, b, 1, 0:n], rl[:, b, 0:1], None, ALU.mult))
                    st.settle()
                    if i >= 2:
                        dve.wait_ge(turned, i - 1)
                    nc.vector.scalar_tensor_tensor(a[:, b, 0:n], e[:, b, 0, 0:n], rd[:, b, 0:1], tt[:, b, 0:n], ALU.mult, ALU.subtract).then_inc(mixed, 1)

            @block.scalar
            def _(act):
                act.wait_ge(lsum, 1)
                nc.scalar.activation(ls[:], ls[:], ACT.Exp).then_inc(lexp, 1)
                act.wait_ge(kturned, 1)
                nc.scalar.activation(kn[:].rearrange("p h k -> p (h k)"), tr[:, 0, :], ACT.Copy).then_inc(kcopied, 1)

                def exps(i):
                    act.wait_ge(maxed, i + 1)
                    if i >= 2:
                        act.wait_ge(mixed, i - 1)
                    for m in range(2):
                        ins = nc.scalar.activation(e[:, i % 2, m, 0:nk[i]], sc[:, i % 2, m, 0:nk[i]], ACT.Exp,
                                                   bias=nm[:, i % 2, m:m + 1], scale=SC, accum_out=den[:, i % 2, m:m + 1])
                    ins.then_inc(expd, 1)

                exps(0)
                for i, (h, q) in enumerate(items):
                    if i + 1 < len(items):
                        exps(i + 1)
                    act.wait_ge(turned, i + 1)
                    if i >= 2:
                        act.wait_ge(attended, i - 1)
                    nc.scalar.activation(at[:, i % 2, 0:nk[i]], tr[:, i % 2, 0:nk[i]], ACT.Copy).then_inc(tcopied, 1)
                    if q == NT - 1:
                        act.wait_ge(attended, i + 1)
                        nc.scalar.activation(o[:, h, :], ob[:, h % 2, 0:T], ACT.Copy).then_inc(ocopied, 1)


def head_norm(nc, sems, cx, name, o, g_dram, factor, hi, lo, r=None):
    with Stage(nc, sems, name) as s:
        g, gf = s.sb("g", [P, 1]), s.sb("gf", [P, 1])
        sq, root, sg = s.sb("sq", [P, HEADS, T]), s.sb("root", [P, HEADS, T]), s.sb("sg", [P, HEADS, T])
        ss = s.ps("ss", [P, HEADS, 512])
        loaded, squared, summed, rooted, gated, own = (s.sem(x) for x in ("g_loaded", "squared", "summed", "rooted", "gated", "dve"))
        with nc.Block() as block:
            @block.sync
            def _(sp):
                sp.dma_start(g[:], g_dram).then_inc(loaded, 16)

            @block.scalar
            def _(act):
                nc.scalar.activation(sq[:], o[:], ACT.Square).then_inc(squared, 1)
                if r is not None:
                    nc.scalar.activation(sg[:], r, ACT.Sigmoid).then_inc(gated, 1)
                for h in range(HEADS):
                    act.wait_ge(summed, h + 1)
                    nc.scalar.activation(root[:, h], ss[:, h, 0:T], ACT.Sqrt, bias=cx.eps[:, 0:1], scale=1.0 / P).then_inc(rooted, 1)

            @block.tensor
            def _(pe):
                pe.wait_ge(squared, 1)
                for h in range(HEADS):
                    pe.matmul(ss[:, h, 0:T], cx.ones[:], sq[:, h], start=True, stop=True).then_inc(summed, 1)

            @block.vector
            def _(dve):
                st = Steps(dve, own)
                dve.wait_ge(loaded, 16)
                st.done(nc.vector.tensor_scalar(gf[:], g[:], factor, None, ALU.mult))
                dve.wait_ge(rooted, HEADS)
                st.done(nc.vector.reciprocal(root[:], root[:]))
                st.settle()
                st.done(nc.vector.scalar_tensor_tensor(o[:], o[:], gf[:, 0:1], root[:], ALU.mult, ALU.mult))
                st.settle()
                if r is not None:
                    dve.wait_ge(gated, 1)
                    st.done(nc.vector.tensor_tensor(sg[:], sg[:], r, ALU.mult))
                    st.settle()
                    st.done(nc.vector.tensor_tensor(o[:], o[:], sg[:], ALU.mult))
                    st.settle()
                st.done(hi_part(nc, hi, o[:]))
                st.settle()
                st.done(lo_part(nc, lo, o[:], hi))


def gla(nc, sems, cx, d, y, v, o):
    QG, KG, LOW = 8, 10, 16
    X = 4
    with Stage(nc, sems, "gla") as s:
        gu, gb, s0 = s.sb("gu", [16, 2, 256]), s.sb("gb", [P, X]), s.sb("s0", [P, X, P])
        z, m, az, b, eb = (s.sb(n, [P, X, T]) for n in ("z", "m", "az", "b", "eb"))
        qd, ki = s.sb("qd", [P, X, T]), s.sb("ki", [P, X, T])
        bl, el = s.sb("bl", [P, X, NCH]), s.sb("el", [P, X, NCH])
        ken = s.sb("ken", [P, X, NT, P])
        S = s.sb("S", [P, X, NCH, P])
        sf, unread = s.sb("sf", [P, X, P]), s.sb("unread", [P, X, P])
        am = s.sb("am", [P, 2, 2, P])
        wk = s.ps("wk", [P, 4, 512])
        ob = s.ps("ob", [P, 2, 512])
        loaded, gated, biased, own = s.sem("loaded"), s.sem("gates"), s.sem("biased"), s.sem("dve")
        logs, cums, ends, decays = s.sem("act"), s.sem("cumsum"), s.sem("ends"), s.sem("decays")
        keyed, turned, tcopied, updated, folded = (s.sem(x) for x in ("k_end", "k_turned", "k_copied", "kv", "state"))
        scored, masked, outed, ocopied, stored = (s.sem(x) for x in ("scored", "masked", "o_done", "o_copied", "stored"))

        seqs = {0: [[0, 1], [2, 3, 4, 5]], 1: [[1, 0], [5, 4, 3, 2]]}
        steps = [(2 * dr + hp, seqs[dr], q, j) for q in (0, 1) for j in range(4) for dr in range(2) for hp in range(2)
                 if j < len(seqs[dr][q])]
        items = [(h, t) for h in range(HEADS) for t in range(NT)]
        with nc.Block() as block:
            @block.sync
            def _(sp):
                sp.dma_start(gu[:], d["gate_up"]).then_inc(loaded, 16)
                sp.dma_start(gb[:], d["gate_bias"]).then_inc(loaded, 16)
                sp.dma_start(s0[:], d["state_gla"]).then_inc(loaded, 16)
                sp.wait_ge(folded, len(steps))
                sp.dma_start(d["new_gla"], sf[:]).then_inc(stored, 16)
                sp.wait_ge(stored, 16)

            @block.tensor
            def _(pe):
                pe.wait_ge(loaded, 48)
                for x in range(X):
                    dr, hp = divmod(x, 2)
                    pe.matmul(wk[:, x, 0:T], gu[:, dr, hp * P:(hp + 1) * P], y[0:16, LOW + dr, :], start=True, stop=True).then_inc(gated, 1)
                pe.wait_ge(biased, X)
                pe.wait_ge(keyed, 1)
                for x in range(X):
                    for t in range(NT):
                        mm = pe.transpose(wk[:, x, t * P:(t + 1) * P], eb[:, x, t * P:(t + 1) * P], cx.ident)
                    mm.then_inc(turned, 1)
                pe.wait_ge(tcopied, X)
                for i, (x, chunks, q, j) in enumerate(steps):
                    c = chunks[q][j]
                    hp, r = x % 2, slice(64 * (c % 2), 64 * (c % 2) + 64)
                    if i >= 4:
                        pe.wait_ge(folded, i - 3)
                    pe.matmul(wk[:, i % 4, 0:256], ken[r, x, c // 2, :], v[r, c // 2, 1, hp * 256:(hp + 1) * 256],
                              start=True, stop=True).then_inc(updated, 1)
                pe.wait_ge(folded, len(steps))

                def scores(i):
                    h, t = items[i]
                    r, cols = slice(64 * (h % 2), 64 * (h % 2) + 64), slice(t * P, (t + 1) * P)
                    for dr in range(2):
                        x = 2 * dr + h // 2
                        if i >= 2:
                            pe.wait_ge(masked, 2 * (i - 2) + dr + 1)
                        pe.matmul(wk[:, 2 * (i % 2) + dr, 0:P], ki[r, x, cols], qd[r, x, cols], start=True, stop=True).then_inc(scored, 1)

                scores(0)
                for i, (h, t) in enumerate(items):
                    if i + 1 < len(items):
                        scores(i + 1)
                    r = slice(64 * (h % 2), 64 * (h % 2) + 64)
                    pe.wait_ge(masked, 2 * i + 2)
                    if t == 0 and h >= 2:
                        pe.wait_ge(ocopied, h - 1)
                    for c in (2 * t, 2 * t + 1):
                        oo = ob[:, h % 2, c * CHUNK:(c + 1) * CHUNK]
                        cc = slice(CHUNK * (c % 2), CHUNK * (c % 2) + CHUNK)
                        for dr in range(2):
                            pe.matmul(oo, v[:, t, 1, h * P:(h + 1) * P], am[:, i % 2, dr, cc], start=dr == 0, stop=False)
                        for dr in range(2):
                            x = 2 * dr + h // 2
                            mm = pe.matmul(oo, S[r, x, c, :], qd[r, x, c * CHUNK:(c + 1) * CHUNK], start=False, stop=dr == 1)
                    mm.then_inc(outed, 1)

            @block.vector
            def _(dve):
                st = Steps(dve, own)
                st.done(nc.vector.memset(am[:], 0.0))
                st.done(nc.vector.memset(S[:, 0:2, 0, :], 0.0))
                st.done(nc.vector.memset(S[:, 2:4, 1, :], 0.0))
                dve.wait_ge(loaded, 48)
                for x in range(X):
                    dve.wait_ge(gated, x + 1)
                    nc.vector.tensor_scalar(z[:, x], wk[:, x, 0:T], gb[:, x:x + 1], None, ALU.add).then_inc(biased, 1)
                    st.done(nc.vector.tensor_copy(S[:, x, 2 if x < 2 else 5, :], s0[:, x, :]))
                dve.wait_ge(biased, X)
                st.done(nc.vector.tensor_scalar(m[:], z[:], 0.0, None, ALU.min))
                st.settle()
                dve.wait_ge(logs, 3)
                st.done(nc.vector.tensor_tensor(z[:], m[:], az[:], ALU.subtract))
                st.settle()
                st.done(nc.vector.tensor_scalar(z[:], z[:], 1.0 / 16.0, None, ALU.mult))
                st.settle()
                for x in range(X):
                    if x < 2:
                        out, g, keep = b[:, x], z[:, x], cx.const0[:, C_CH - C_KEEP:C_CH - C_KEEP + T]
                    else:
                        out, g, keep = b[:, x][:, ::-1], z[:, x][:, ::-1], cx.const0[:, C_CH - C_KEEP:C_CH - C_KEEP + T]
                    st.done(nc.vector.tensor_tensor_scan(out, keep, g, 0.0, ALU.mult, ALU.add))
                st.settle()
                bc = b[:].rearrange("p x (c i) -> p x c i", c=NCH)
                st.done(nc.vector.tensor_copy(bl[:, 0:2], bc[:, 0:2, :, CHUNK - 1]))
                ins = nc.vector.tensor_copy(bl[:, 2:4], bc[:, 2:4, :, 0])
                st.done(ins)
                st.settle()
                dve.sem_inc(cums, 1)
                for x in range(X):
                    ins = nc.vector.tensor_tensor(z[:, x].rearrange("p (c i) -> p c i", c=NCH),
                                                  bl[:, x].unsqueeze(2).to_broadcast([P, NCH, CHUNK]),
                                                  bc[:, x], ALU.subtract)
                ins.then_inc(ends, 1)
                qg, kg = y[:, QG:QG + 2, :], y[:, KG:KG + 2, :]
                dve.wait_ge(decays, 1)
                for dr in range(2):
                    st.done(nc.vector.scalar_tensor_tensor(qd[:, 2 * dr:2 * dr + 2], qg, 64 ** -0.5, m[:, 2 * dr:2 * dr + 2], ALU.mult, ALU.mult))
                dve.wait_ge(decays, 2)
                for dr in range(2):
                    st.done(nc.vector.tensor_tensor(ki[:, 2 * dr:2 * dr + 2], kg, az[:, 2 * dr:2 * dr + 2], ALU.mult))
                dve.wait_ge(decays, 4)
                for dr in range(2):
                    ins = nc.vector.tensor_tensor(eb[:, 2 * dr:2 * dr + 2], kg, eb[:, 2 * dr:2 * dr + 2], ALU.mult)
                ins.then_inc(keyed, 1)
                for i, (x, chunks, q, j) in enumerate(steps):
                    c = chunks[q][j]
                    last = j == len(chunks[q]) - 1
                    dve.wait_ge(updated, i + 1)
                    if j:
                        dve.wait_ge(folded, i - 3)
                    for hh in range(2):
                        r = slice(64 * hh, 64 * hh + 64)
                        dst = (sf, unread)[q][r, x, :] if last else S[r, x, chunks[q][j + 1], :]
                        ins = nc.vector.scalar_tensor_tensor(dst, S[r, x, c, :], el[r, x, c:c + 1], wk[r, i % 4, hh * P:(hh + 1) * P],
                                                             ALU.mult, ALU.add)
                    ins.then_inc(folded, 1)
                for i in range(len(items)):
                    if i >= 2:
                        dve.wait_ge(outed, i - 1)
                    for dr in range(2):
                        dve.wait_ge(scored, 2 * i + dr + 1)
                        mask = cx.const0[:, (C_MF, C_MB)[dr] - C_KEEP:(C_MF, C_MB)[dr] - C_KEEP + P].bitcast(I32)
                        nc.vector.copy_predicated(am[:, i % 2, dr, :], mask, wk[:, 2 * (i % 2) + dr, 0:P]).then_inc(masked, 1)

            @block.scalar
            def _(act):
                act.wait_ge(biased, X)
                nc.scalar.activation(az[:], z[:], ACT.Abs).then_inc(logs, 1)
                act.wait_ge(logs, 1)
                nc.scalar.activation(az[:], az[:], ACT.Exp, scale=-1.0).then_inc(logs, 1)
                act.wait_ge(logs, 2)
                nc.scalar.activation(az[:], az[:], ACT.Ln, bias=cx.ones[:, 0:1]).then_inc(logs, 1)
                act.wait_ge(cums, 1)
                nc.scalar.activation(m[:], b[:], ACT.Exp).then_inc(decays, 1)
                nc.scalar.activation(az[:], b[:], ACT.Exp, scale=-1.0).then_inc(decays, 1)
                act.wait_ge(ends, 1)
                nc.scalar.activation(eb[:], z[:], ACT.Exp).then_inc(decays, 1)
                nc.scalar.activation(el[:], bl[:], ACT.Exp).then_inc(decays, 1)
                for x in range(X):
                    act.wait_ge(turned, x + 1)
                    nc.scalar.activation(ken[:, x].rearrange("p t k -> p (t k)"), wk[:, x, 0:T], ACT.Copy).then_inc(tcopied, 1)
                for h in range(HEADS):
                    act.wait_ge(outed, NT * (h + 1))
                    nc.scalar.activation(o[:, h, :], ob[:, h % 2, 0:T], ACT.Copy).then_inc(ocopied, 1)


IB = 32
HALVES = (slice(0, KC // 2), slice(KC // 2, KC))
TB = T // IB


def retrieve(nc, sems, cx, name, d, layer, q, i1T, i2T, gh, gl, hi, lo, A0):
    J = 2 * PH
    with Stage(nc, sems, name) as s:
        keys = s.sb("keys", [P, J, NKEYS])
        sc, sc2 = s.sb("sc", [P, 2, J, NKEYS]), s.sb("sc2", [P, J, NKEYS])
        v16, ix, ixf, dx = s.sb("v16", [P, J, TOPK]), s.sb("ix", [P, J, TOPK], U32), s.sb("ixf", [P, J, TOPK]), s.sb("dx", [P, J, TOPK])
        cand, cand2 = s.sb("cand", [P, PH, NCAND]), s.sb("cand2", [P, PH, NCAND])
        top, pos = s.sb("top", [P, PH, TOPK]), s.sb("pos", [P, PH, TOPK], U32)
        posf, ex, den, row = s.sb("posf", [P, P]), s.sb("ex", [P, NT, PH, TOPK]), s.sb("den", [P, NT, PH]), s.sb("row", [P, P])
        ge, pr = s.sb("ge", [P, P, TOPK], F16), s.sb("pr", [P, P, TOPK], F16)
        pick = s.sb("pick", [P, NT, 3, P])
        g16 = s.sb("g16", [P, P], F16)
        ur, uh, ul = (s.sb(x, [P, 2, KC, P]) for x in ("ur", "uh", "ul"))
        warm = s.sb("warm", [P, 1])
        ps, bank = s.ps("ps", [P, 4, 512]), s.ps("s", [P, 2, 512])
        loaded, scored, copied, own = s.sem("keys_loaded"), s.sem("scored"), s.sem("copied"), s.sem("dve")
        sub, expd, picked, turned, stored = (s.sem(x) for x in ("cand_sub", "exp", "picked", "turned", "stored"))
        read = s.sem("scores_read")
        uload = [s.sem("u0_loaded"), s.sem("u1_loaded")]
        uhigh, usplit, uscored, gelud = (s.sem(x) for x in ("u_high", "u_split", "u_scored", "gelu"))
        PAIRS, FIRST = IB // 2, 5
        with nc.Block() as block:
            @block.sync
            def _(sp):
                sp.dma_start(keys[:], d["sub_keys"][layer]).then_inc(loaded, 16)
                with sp.Fori(0, PAIRS) as i:
                    for b in range(2):
                        sp.wait_ge(usplit, i * 4 + 2 * b + 2)
                        src = d["peer_u"][layer, bass.ds(i * 2 + b, 1)]
                        sp.dma_start(ur[:, b], src.rearrange("a p (k m) -> p (a k) m", k=KC)).then_inc(uload[b], 16)

            @block.tensor
            def _(pe):
                def key_scores(t):
                    for j in range(J):
                        if t and j % 4 == 0:
                            pe.wait_ge(copied, 4 * (t - 1) + j // 4 + 1)
                        mm = pe.matmul(ps[:, j // 4, (j % 4) * P:(j % 4 + 1) * P], q[:, j, t * P:(t + 1) * P], keys[:, j, :], start=True, stop=True)
                        if j % 4 == 3:
                            mm.then_inc(scored, 1)

                def expert_scores(n, b):
                    pe.wait_ge(gelud, n + 1)
                    o = bank[:, b, 0:T]
                    for k in range(KC):
                        if k % (KC // 2) == 0:
                            pe.wait_ge(usplit, n * 2 + k // (KC // 2) + 1 + 4)
                        pe.matmul(o, r32(uh[:, b, k]), r32(hi[:, k]), start=k == 0, stop=False)
                        pe.matmul(o, r32(uh[:, b, k]), r32(lo[:, k]), start=False, stop=False)
                        mm = pe.matmul(o, r32(ul[:, b, k]), r32(hi[:, k]), start=False, stop=k == KC - 1)
                    mm.then_inc(uscored, 1)

                pe.sem_inc(uscored, 2)
                pe.wait_ge(loaded, 16)
                key_scores(0)
                key_scores(1)
                with pe.Fori(0, FIRST) as i:
                    for b in range(2):
                        expert_scores(i * 2 + b, b)
                key_scores(2)
                with pe.Fori(FIRST, PAIRS) as i:
                    for b in range(2):
                        expert_scores(i * 2 + b, b)
                pe.wait_ge(picked, 1)
                for t in range(NT):
                    for a in range(3):
                        mm = pe.transpose(ps[:, t, a * P:(a + 1) * P], pick[:, t, a, :], cx.ident)
                    mm.then_inc(turned, 1)

            @block.scalar
            def _(act):
                def copy_scores(t):
                    if t >= 2:
                        act.wait_ge(read, t - 1)
                    for b in range(4):
                        act.wait_ge(scored, 4 * t + b + 1)
                        nc.scalar.activation(sc[:, t % 2, 4 * b:4 * b + 4].rearrange("p j n -> p (j n)"), ps[:, b, :], ACT.Copy).then_inc(copied, 1)

                def round_u(n, b, turn):
                    act.wait_ge(uload[b], turn * 16 + 16)
                    act.wait_ge(uscored, n + 1)
                    for h in HALVES:
                        nc.scalar.activation(r32(uh[:, b, h]), ur[:, b, h], ACT.Copy).then_inc(uhigh, 1)

                def gelu(n, b):
                    act.wait_ge(uscored, n + 1 + 2)
                    nc.scalar.activation(A0[:, bass.ds(n, 1), :].rearrange("p a t -> p (a t)"), bank[:, b, 0:T], ACT.Gelu_apprx_tanh).then_inc(gelud, 1)

                def pair(i):
                    round_u(i * 2 + 1, 1, i)
                    gelu(i * 2, 0)
                    round_u(i * 2 + 2, 0, i + 1)
                    gelu(i * 2 + 1, 1)

                act.sem_inc(gelud, 2)
                nc.scalar.activation(warm[:], cx.eps[:], ACT.Gelu_apprx_tanh)
                round_u(0, 0, 0)
                copy_scores(0)
                copy_scores(1)
                with act.Fori(0, FIRST) as i:
                    pair(i)
                copy_scores(2)
                with act.Fori(FIRST, PAIRS - 1) as i:
                    pair(i)
                round_u(IB - 1, 1, PAIRS - 1)
                gelu(IB - 2, 0)
                gelu(IB - 1, 1)
                act.wait_ge(sub, NT)
                nc.scalar.activation(ex[:], ex[:], ACT.Exp).then_inc(expd, 1)

            @block.gpsimd
            def _(pool):
                pool.sem_inc(usplit, 4)
                with pool.Fori(0, PAIRS) as i:
                    for b in range(2):
                        for a, h in enumerate(HALVES):
                            pool.wait_ge(uhigh, i * 4 + 2 * b + a + 1)
                            nc.gpsimd.tensor_tensor(r32(ul[:, b, h]), ur[:, b, h], uh[:, b, h], ALU.subtract).then_inc(usplit, 1)

            @block.vector
            def _(dve):
                st = Steps(dve, own)
                vec = nc.vector

                def take(a):
                    dve.wait_ge(turned, a + 1)
                    cols = slice(a * P, (a + 1) * P)
                    for dst, k in ((i1T, 0), (i2T, 1)):
                        vec.tensor_copy(dst[:, cols], ps[:, a, k * P:(k + 1) * P])
                    st.done(vec.tensor_copy(g16[:], ps[:, a, 2 * P:3 * P]))
                    st.settle()
                    st.done(vec.tensor_copy(gh[:, cols], g16[:]))
                    st.settle()
                    vec.tensor_tensor(gl[:, cols], ps[:, a, 2 * P:3 * P], gh[:, cols], ALU.subtract).then_inc(stored, 1)

                for t in range(NT):
                    dve.wait_ge(copied, 4 * t + 4)
                    x = sc[:, t % 2]
                    for j in range(J):
                        ins = vec.max(v16[:, j, 0:8], x[:, j])
                    st.done(ins)
                    st.settle()
                    for j in range(J):
                        vec.max_index(ix[:, j, 0:8], v16[:, j, 0:8], x[:, j])
                        ins = vec.match_replace(sc2[:, j], v16[:, j, 0:8], x[:, j], NEG)
                    st.done(ins)
                    st.settle()
                    dve.sem_inc(read, 1)
                    for j in range(J):
                        ins = vec.max(v16[:, j, 8:16], sc2[:, j])
                    st.done(ins)
                    st.settle()
                    for j in range(J):
                        ins = vec.max_index(ix[:, j, 8:16], v16[:, j, 8:16], sc2[:, j])
                    st.done(ins)
                    v = v16[:].rearrange("p (h w) k -> p h w k", w=2)
                    s1, s2 = v[:, :, 0], v[:, :, 1]
                    a = 0
                    while a < TOPK:
                        n = CAND_LEN[a]
                        rows = CAND_LEN.count(n) if n <= 2 else 1
                        out = cand[:, :, CAND_START[a]:CAND_START[a] + n * rows].rearrange("p h (r b) -> p h r b", r=rows)
                        ins = vec.tensor_tensor(out, s1[:, :, a:a + rows].unsqueeze(3).to_broadcast([P, PH, rows, n]),
                                                s2[:, :, 0:n].unsqueeze(2).to_broadcast([P, PH, rows, n]), ALU.add)
                        a += rows
                    st.done(ins)
                    st.settle()
                    st.done(vec.tensor_copy(ixf[:], ix[:]))
                    for h in range(PH):
                        ins = vec.max(top[:, h, 0:8], cand[:, h])
                    st.done(ins)
                    st.settle()
                    st.done(vec.tensor_copy(dx[:, :, 0:1], ixf[:, :, 0:1]))
                    st.done(vec.tensor_tensor(dx[:, :, 1:TOPK], ixf[:, :, 1:TOPK], ixf[:, :, 0:TOPK - 1], ALU.subtract))
                    for h in range(PH):
                        vec.max_index(pos[:, h, 0:8], top[:, h, 0:8], cand[:, h])
                        ins = vec.match_replace(cand2[:, h], top[:, h, 0:8], cand[:, h], NEG)
                    st.done(ins)
                    st.settle()
                    for h in range(PH):
                        ins = vec.max(top[:, h, 8:16], cand2[:, h])
                    st.done(ins)
                    st.settle()
                    for h in range(PH):
                        ins = vec.max_index(pos[:, h, 8:16], top[:, h, 8:16], cand2[:, h])
                    st.done(ins)
                    vec.tensor_tensor(ex[:, t], top[:], top[:, :, 0:1].to_broadcast([P, PH, TOPK]), ALU.subtract).then_inc(sub, 1)
                    st.settle()
                    st.done(vec.tensor_copy(posf[:], pos[:].rearrange("p h k -> p (h k)")))
                    st.settle()
                    starts = cx.const[:, C_ST:C_ST + 16].unsqueeze(1).to_broadcast([P, P, TOPK])
                    lens = cx.const[:, C_LEN:C_LEN + 16].unsqueeze(1).to_broadcast([P, P, TOPK])
                    sixteen = cx.const[:, C_I16:C_I16 + 16].unsqueeze(1).to_broadcast([P, P, TOPK])
                    st.done(vec.tensor_tensor(ge[:], posf[:].unsqueeze(2).to_broadcast([P, P, TOPK]), starts, ALU.is_ge))
                    st.settle()
                    dxr = dx[:].rearrange("p (h w) r -> p h w r", w=2)
                    gv = ge[:].rearrange("p (h k) r -> p h k r", h=PH)
                    pv = pr[:].rearrange("p (h k) r -> p h k r", h=PH)
                    st.done(vec.tensor_tensor(pv, gv, dxr[:, :, 0].unsqueeze(2).to_broadcast([P, PH, TOPK, TOPK]), ALU.mult))
                    st.settle()
                    st.done(vec.tensor_reduce(pick[:, t, 0], pr[:], X_AXIS, ALU.add))
                    st.settle()
                    st.done(vec.tensor_tensor(pr[:], ge[:], lens, ALU.mult))
                    st.settle()
                    st.done(vec.tensor_reduce(row[:], pr[:], X_AXIS, ALU.add))
                    st.settle()
                    st.done(vec.tensor_tensor(posf[:], posf[:], row[:], ALU.subtract))
                    st.settle()
                    st.done(vec.tensor_tensor(ge[:], posf[:].unsqueeze(2).to_broadcast([P, P, TOPK]), sixteen, ALU.is_ge))
                    st.settle()
                    st.done(vec.tensor_tensor(pv, gv, dxr[:, :, 1].unsqueeze(2).to_broadcast([P, PH, TOPK, TOPK]), ALU.mult))
                    st.settle()
                    st.done(vec.tensor_reduce(pick[:, t, 1], pr[:], X_AXIS, ALU.add))
                    st.settle()
                dve.wait_ge(expd, 1)
                dn = den[:].rearrange("p t h -> p (t h)")
                st.done(vec.tensor_reduce(dn, ex[:].rearrange("p t h k -> p (t h) k"), X_AXIS, ALU.add))
                st.settle()
                st.done(vec.reciprocal(dn, dn))
                st.settle()
                st.done(vec.tensor_scalar(dn, dn, GATE_SCALE, None, ALU.mult))
                st.settle()
                for t in range(NT):
                    st.done(vec.tensor_tensor(pick[:, t, 2].rearrange("p (h k) -> p h k", h=PH), ex[:, t],
                                              den[:, t].unsqueeze(2).to_broadcast([P, PH, TOPK]), ALU.mult))
                st.settle()
                dve.sem_inc(picked, 1)
                for t in range(NT):
                    take(t)


def experts(nc, sems, cx, name, d, layer, hi, lo, picks, A, acc, value=None, gate=None, score=None):
    i1T, i2T, gh, gl = picks
    with Stage(nc, sems, name) as s:
        if score is not None:
            ur, uh, ul = (s.sb(x, [P, 2, KC, P]) for x in ("ur", "uh", "ul"))
            warm = s.sb("warm", [P, 1])
        if value is not None:
            vr, vh, vl = (s.sb(x, [P, 2, D]) for x in ("vr", "vh", "vl"))
            wh, wl = s.sb("wh", [P, 2, T]), s.sb("wl", [P, 2, T])
        if gate is not None:
            o1 = s.sb("o1", [P, 2, TB, P], F16)
            eq, oh, ol = (s.sb(x, [P, 2, TB, IB], F16) for x in ("eq", "oh", "ol"))
        bank = s.ps("s", [P, 2, 512])
        gbank, sbanks = 1, (2 if gate is None else 1)
        uload, vload = [s.sem("u0_loaded"), s.sem("u1_loaded")], [s.sem("v0_loaded"), s.sem("v1_loaded")]
        uhigh, vhigh, usplit, vsplit, whigh, wsplit = (s.sem(x) for x in ("u_high", "v_high", "u_split", "v_split", "w_high", "w_split"))
        scored, gelud, valued, compared, hot, gated, applied = (
            s.sem(x) for x in ("scored", "gelu", "valued", "compared", "one_hots", "gated", "gates_applied"))
        with nc.Block() as block:
            @block.sync
            def _(sp):
                with sp.Fori(0, IB // 2) as i:
                    for b in range(2):
                        if score is not None:
                            sp.wait_ge(usplit, i * 4 + 2 * b + 2)
                            src = d["peer_u"][layer, bass.ds(i * 2 + (b + score * IB), 1)]
                            sp.dma_start(ur[:, b], src.rearrange("a p (k m) -> p (a k) m", k=KC)).then_inc(uload[b], 16)
                        if value is not None:
                            sp.wait_ge(vsplit, i * 2 + b + 1)
                            src = d["peer_v"][layer, bass.ds(i * 2 + (b + value * IB), 1)]
                            sp.dma_start(vr[:, b], src.rearrange("a p m -> p (a m)")).then_inc(vload[b], 16)

            @block.scalar
            def _(act):
                def round_tables(n, b, turn):
                    if score is not None:
                        act.wait_ge(uload[b], turn * 16 + 16)
                        act.wait_ge(scored, n + 1)
                        for h in HALVES:
                            nc.scalar.activation(r32(uh[:, b, h]), ur[:, b, h], ACT.Copy).then_inc(uhigh, 1)
                    if value is not None:
                        act.wait_ge(vload[b], turn * 16 + 16)
                        act.wait_ge(valued, n + 1)
                        nc.scalar.activation(r32(vh[:, b]), vr[:, b], ACT.Copy).then_inc(vhigh, 1)
                        if score is None:
                            w = A[value % 2][:, bass.ds(n, 1), :].rearrange("p a t -> p (a t)")
                            nc.scalar.activation(r32(wh[:, b]), w, ACT.Copy).then_inc(whigh, 1)

                def gelu(n, b):
                    if score is None:
                        return
                    act.wait_ge(scored, n + 1 + 2)
                    if value is not None:
                        act.wait_ge(wsplit, n + 1)
                    out = A[score % 2][:, bass.ds(n, 1), :].rearrange("p a t -> p (a t)")
                    nc.scalar.activation(out, bank[:, b % sbanks, 0:T], ACT.Gelu_apprx_tanh).then_inc(gelud, 1)

                act.sem_inc(gelud, sbanks)
                if score is not None:
                    nc.scalar.activation(warm[:], cx.eps[:], ACT.Gelu_apprx_tanh)
                round_tables(0, 0, 0)
                with act.Fori(0, IB // 2 - 1) as i:
                    round_tables(i * 2 + 1, 1, i)
                    gelu(i * 2, 0)
                    round_tables(i * 2 + 2, 0, i + 1)
                    gelu(i * 2 + 1, 1)
                round_tables(IB - 1, 1, IB // 2 - 1)
                gelu(IB - 2, 0)
                gelu(IB - 1, 1)

            @block.vector
            def _(dve):
                v = nc.vector

                def one_hots(n, b):
                    if gate is None:
                        return
                    toks = bass.ds(n * TB, TB)
                    dve.wait_ge(gated, n + 1)
                    small = [P, TB, IB]
                    v.tensor_tensor(eq[:, b], cx.iota[:, gate * IB:gate * IB + IB].unsqueeze(1).to_broadcast(small),
                                    i2T[:, toks].unsqueeze(2).to_broadcast(small), ALU.is_equal).then_inc(compared, 1)
                    v.tensor_tensor(o1[:, b], cx.iota[:].unsqueeze(1).to_broadcast([P, TB, P]),
                                    i1T[:, toks].unsqueeze(2).to_broadcast([P, TB, P]), ALU.is_equal)
                    dve.wait_ge(compared, n + 1)
                    v.tensor_tensor(oh[:, b], eq[:, b], gh[:, toks].unsqueeze(2).to_broadcast(small), ALU.mult)
                    v.tensor_tensor(ol[:, b], eq[:, b], gl[:, toks].unsqueeze(2).to_broadcast(small), ALU.mult).then_inc(hot, 1)

                def split(n, b):
                    if value is None:
                        return
                    if score is not None:
                        dve.wait_ge(vhigh, n + 1)
                        lo_part(nc, vl[:, b], vr[:, b], vh[:, b]).then_inc(vsplit, 1)
                    w = A[value % 2][:, bass.ds(n, 1), :].rearrange("p a t -> p (a t)")
                    if score is not None:
                        dve.wait_ge(valued, n + 1)
                        hi_part(nc, wh[:, b], w).then_inc(whigh, 1)
                    dve.wait_ge(whigh, n + 1)
                    lo_part(nc, wl[:, b], w, wh[:, b]).then_inc(wsplit, 1)

                def apply(n, b):
                    if gate is None:
                        return
                    dve.wait_ge(gated, n + 1 + 2)
                    at = A[gate % 2][:, :, bass.ds(n * TB, TB)]
                    v.scalar_tensor_tensor(at, bank[:, gbank, 0:T].rearrange("p (t i) -> p i t", t=TB), 1.0 / GATE_SCALE,
                                           at, ALU.mult, ALU.mult).then_inc(applied, 1)

                dve.sem_inc(applied, 1)
                one_hots(0, 0)
                split(0, 0)
                if gate is not None or value is not None:
                    with dve.Fori(0, IB // 2 - 1) as i:
                        for b in range(2):
                            one_hots(i * 2 + b + 1, 1 - b)
                            apply(i * 2 + b, b)
                            split(i * 2 + b + 1, 1 - b)
                    one_hots(IB - 1, 1)
                    apply(IB - 2, 0)
                    split(IB - 1, 1)
                    apply(IB - 1, 1)

            @block.gpsimd
            def _(pool):
                pool.sem_inc(usplit, 4)
                pool.sem_inc(vsplit, 2)
                if score is not None:
                    with pool.Fori(0, IB // 2) as i:
                        for b in range(2):
                            for a, h in enumerate(HALVES):
                                pool.wait_ge(uhigh, i * 4 + 2 * b + a + 1)
                                nc.gpsimd.tensor_tensor(r32(ul[:, b, h]), ur[:, b, h], uh[:, b, h], ALU.subtract).then_inc(usplit, 1)
                elif value is not None:
                    with pool.Fori(0, IB // 2) as i:
                        for b in range(2):
                            pool.wait_ge(vhigh, i * 2 + b + 1)
                            nc.gpsimd.tensor_tensor(r32(vl[:, b]), vr[:, b], vh[:, b], ALU.subtract).then_inc(vsplit, 1)

            @block.tensor
            def _(pe):
                def gates(n, b):
                    if gate is None:
                        return
                    pe.wait_ge(hot, n + 1)
                    pe.wait_ge(applied, n + 1)
                    for t in range(TB):
                        o = bank[:, gbank, t * IB:(t + 1) * IB]
                        pe.matmul(o, o1[:, b, t], oh[:, b, t], start=True, stop=False)
                        mm = pe.matmul(o, o1[:, b, t], ol[:, b, t], start=False, stop=True)
                    mm.then_inc(gated, 1)

                def scores(n, b):
                    if score is None:
                        return
                    pe.wait_ge(gelud, n + 1)
                    o = bank[:, b % sbanks, 0:T]
                    for k in range(KC):
                        if k % (KC // 2) == 0:
                            pe.wait_ge(usplit, n * 2 + k // (KC // 2) + 1 + 4)
                        pe.matmul(o, r32(uh[:, b, k]), r32(hi[:, k]), start=k == 0, stop=False)
                        pe.matmul(o, r32(uh[:, b, k]), r32(lo[:, k]), start=False, stop=False)
                        mm = pe.matmul(o, r32(ul[:, b, k]), r32(hi[:, k]), start=False, stop=k == KC - 1)
                    mm.then_inc(scored, 1)

                def contract(n, b):
                    if value is None:
                        return
                    pe.wait_ge(vsplit, n + 1 + 2)
                    pe.wait_ge(wsplit, n + 1)
                    for t in range(NT):
                        w = slice(t * P, (t + 1) * P)
                        for lhs, rhs in ((wh, vh), (wh, vl), (wl, vh)):
                            for c in range(2):
                                mm = pe.matmul(acc[:, 2 * t + c, :], r32(lhs[:, b, w]), r32(rhs[:, b, c * 512:(c + 1) * 512]),
                                               start=False, stop=False, skip_group_check=True)
                    mm.then_inc(valued, 1)

                pe.sem_inc(scored, 2)
                pe.sem_inc(valued, 2)
                pe.sem_inc(gated, 2)
                with pe.Fori(0, IB // 2) as i:
                    for b in range(2):
                        n = i * 2 + b
                        gates(n, b)
                        contract(n, b)
                        scores(n, b)


def add_experts(nc, sems, cx, name, layer, acc):
    with Stage(nc, sems, name) as s:
        out = s.sb("out", [P, NT, D])
        tr = s.ps("tr", [P, 2, 512])
        copied, turned, added = s.sem("copied"), s.sem("turned"), s.sem("added")
        with nc.Block() as block:
            @block.scalar
            def _(act):
                for n in range(2 * NT):
                    nc.scalar.activation(out[:, n // 2, (n % 2) * 512:(n % 2 + 1) * 512], acc[:, n, :], ACT.Copy).then_inc(copied, 1)

            @block.tensor
            def _(pe):
                for n in range(2 * NT):
                    pe.wait_ge(copied, n + 1)
                    if n >= 2:
                        pe.wait_ge(added, n - 1)
                    for j in range(4):
                        mm = pe.transpose(tr[:, n % 2, j * P:(j + 1) * P], out[:, n // 2, (4 * (n % 2) + j) * P:(4 * (n % 2) + j + 1) * P], cx.ident)
                    mm.then_inc(turned, 1)

            @block.vector
            def _(dve):
                for n in range(2 * NT):
                    t = n // 2
                    dve.wait_ge(turned, n + 1)
                    for j in range(4):
                        k = 4 * (n % 2) + j
                        x = cx.x[:, k, t * P:(t + 1) * P]
                        ins = nc.vector.scalar_tensor_tensor(x, tr[:, n % 2, j * P:(j + 1) * P], cx.mod(layer, 5)[:, k, min(t, 1):min(t, 1) + 1], x, ALU.mult, ALU.add)
                    ins.then_inc(added, 1)


CH = 8
GC = P // CH
MID = 4
NPAIR = 32
NPD = 2 * NPAIR
QUAD = 4
QP = 2 * QUAD
CP, CS = TP // CH, (T - TP) // CH
SLOTS = CP + CS + 2
SEQS = ((0, CP), (CP + 1, CS))
ROWS = SLOTS - 1
MIN_LOG = -10.0


def s5_prepare(nc, sems, cx, d, u, par):
    TWO_PI_HI, TWO_PI_LO = 6.28125, 2 * math.pi - 6.28125
    ROUND = 1.5 * 2.0 ** 23
    NP_ = 2 * MID + 2
    with Stage(nc, sems, "s5p") as s:
        raw, h0 = s.sb("raw", [P, 3, NPD]), s.sb("h0", [P, 2, NPD])
        dt, th, kk, r, s2, sn = (s.sb(n, [P, NPD]) for n in ("dt", "th", "kk", "r", "s2", "sn"))
        lr, li, den, t1, t2, mag, magc, inv = (s.sb(n, [P, NPD]) for n in ("lr", "li", "den", "t1", "t2", "mag", "magc", "inv"))
        rot, coef, r8 = s.sb("rot", [P, 2, NPD]), s.sb("coef", [P, 2, NPD]), s.sb("r8", [P, 2, 2, NPD])
        LP = s.sb("LP", [P, 2, NPD, NP_])
        E = s.sb("E", [P, 2, NPD, CS])
        ta, tb = s.sb("ta", [P, NPD * CS // 2]), s.sb("tb", [P, NPD * CS // 2])
        uq, U = s.sb("uq", [P, CH, CP + CS]), s.sb("U", [CP + CS, QP, CH, GC])
        pa, pb = s.ps("pa", [P, 2, 512]), s.ps("pb", [P, 512])
        loaded, own, act_done, asked = s.sem("loaded"), s.sem("dve"), s.sem("act"), s.sem("asked")
        zeroed, rotations, tabled = s.sem("zeroed"), s.sem("rotations"), s.sem("pre_filled")
        uqc, ut, uu, ub, ucd = (s.sem(n) for n in ("u_copied", "u_turned", "u_grouped", "u_chunked", "uc_copied"))
        are, aim = raw[:, 0], raw[:, 1]
        quads = lambda a: a.rearrange("p (q d j) n -> p q d j n", d=2, j=QUAD)
        def post_parts(dr, at, n):
            m = min(n + 1, CS)
            return (slice(at, at + m), slice(0, m), 1) if dr == 0 else (slice(at + n + 1 - m, at + n + 1), slice(0, m), -1)

        def pre_parts(dr, at, n):
            return (slice(at + 1, at + n + 1), slice(0, n), 1) if dr == 0 else (slice(at, at + n), slice(0, n), -1)

        with nc.Block() as block:
            @block.sync
            def _(sp):
                sp.dma_start(raw[:], d["s5_par"]).then_inc(loaded, 16)
                sp.dma_start(h0[:], d["state_s5"]).then_inc(loaded, 16)
                sp.dma_start(par.dskip[:], d["s5_d"]).then_inc(loaded, 16)
                sp.dma_start(par.masks[:], d["s5_masks"]).then_inc(loaded, 16)

            @block.scalar
            def _(act):
                act.wait_ge(loaded, 64)
                nc.scalar.activation(dt[:], raw[:, 2], ACT.Exp).then_inc(act_done, 1)
                act.wait_ge(asked, 1)
                nc.scalar.activation(mag[:], t1[:], ACT.Exp)
                nc.scalar.activation(magc[:], t2[:], ACT.Exp)
                nc.scalar.activation(inv[:], t2[:], ACT.Exp, scale=-1.0)
                nc.scalar.activation(par.mag8[:].rearrange("p q d -> p (q d)"), t2[:], ACT.Exp, scale=float(CH)).then_inc(act_done, 1)
                act.wait_ge(asked, 2)
                nc.scalar.activation(s2[:], r[:], ACT.Sin, scale=0.5)
                nc.scalar.activation(sn[:], r[:], ACT.Sin).then_inc(act_done, 1)
                act.wait_ge(zeroed, 3)
                with act.Fori(0, KC) as q:
                    nc.scalar.activation(uq[:], u[:, bass.ds(q, 1), :].rearrange("p a (k s) -> p (a s) k", s=CH), ACT.Copy).then_inc(uqc, 1)
                    act.wait_ge(ut, q + 1)
                    for h in range(2):
                        src = pa[0:CP + CS, h, :].rearrange("k (s g c) -> k s g c", s=CH // 2, g=QP)
                        ins = nc.scalar.activation(U[:, :, h * CH // 2:(h + 1) * CH // 2, :].rearrange("k g s c -> k s g c"), src, ACT.Copy)
                    ins.then_inc(uu, 1)
                    act.wait_ge(ub, q + 1)
                    src = pb[:, 0:QP * (CP + CS)].rearrange("p (g k) -> p g k", g=QP)
                    dst = par.uc[:, bass.ds(q * QP, QP), :]
                    nc.scalar.activation(dst[:, :, 1:CP + 1], src[:, :, 0:CP], ACT.Copy)
                    nc.scalar.activation(dst[:, :, CP + 2:SLOTS], src[:, :, CP:], ACT.Copy).then_inc(ucd, 1)
                act.wait_ge(rotations, 1)
                for dr in range(2):
                    for at, n in SEQS:
                        to, fr, way = post_parts(dr, at, n)
                        for ri in range(2):
                            nc.scalar.activation(quads4(par.post[:, :, ri], dr)[:, :, :, to], quads(E[:, ri])[:, :, dr, :, fr][:, :, :, ::way], ACT.Copy)

            @block.tensor
            def _(pe):
                with pe.Fori(0, KC) as q:
                    pe.wait_ge(uqc, q + 1)
                    for st_ in range(CH):
                        mm = pe.matmul(pa[0:CP + CS, st_ // 4, (st_ % 4) * P:(st_ % 4 + 1) * P], uq[:, st_], cx.ident, start=True, stop=True)
                    mm.then_inc(ut, 1)
                    pe.wait_ge(uu, q + 1)
                    for g in range(QP):
                        lhs = U[:, g].rearrange("k s c -> k (s c)")
                        mm = pe.matmul(pb[:, g * (CP + CS):(g + 1) * (CP + CS)], lhs, cx.ident[0:CP + CS, 0:CP + CS], start=True, stop=True)
                    mm.then_inc(ub, 1)

            @block.gpsimd
            def _(pool):
                g = nc.gpsimd
                g.memset(par.uc[:], 0.0).then_inc(zeroed, 1)
                g.memset(par.post[:], 0.0).then_inc(zeroed, 1)
                g.memset(par.pre[:], 0.0).then_inc(zeroed, 1)
                pool.wait_ge(zeroed, 3)
                pool.wait_ge(rotations, 1)
                for dr in range(2):
                    for at, n in SEQS:
                        to, fr, way = pre_parts(dr, at, n)
                        for ri in range(2):
                            m8 = par.mag8[:, :, dr * QUAD:(dr + 1) * QUAD].unsqueeze(3).to_broadcast([P, KC, QUAD, n])
                            g.tensor_tensor(quads4(par.pre[:, :, ri], dr)[:, :, :, to], quads(E[:, ri])[:, :, dr, :, fr][:, :, :, ::way], m8, ALU.mult)

            @block.vector
            def _(dve):
                v = nc.vector
                st = Steps(dve, own)

                def tt(out, a, b, op):
                    st.done(v.tensor_tensor(out, a, b, op))
                    st.settle()

                def ts(out, a, x, y, op0, op1=None):
                    st.done(v.tensor_scalar(out, a, x, y, op0, op1) if op1 else v.tensor_scalar(out, a, x, None, op0))
                    st.settle()

                def cmul(o, a, b, x, y):
                    v.tensor_tensor(x, a[1], b[1], ALU.mult)
                    v.tensor_tensor(y, a[1], b[0], ALU.mult)
                    v.tensor_tensor(o[0], a[0], b[0], ALU.mult)
                    st.done(v.tensor_tensor(o[1], a[0], b[1], ALU.mult))
                    st.settle()
                    v.tensor_tensor(o[0], o[0], x, ALU.subtract)
                    st.done(v.tensor_tensor(o[1], o[1], y, ALU.add))
                    st.settle()

                both = lambda a: (a[:, 0], a[:, 1])
                dve.wait_ge(loaded, 64)
                dve.wait_ge(act_done, 1)
                tt(t1[:], are, dt[:], ALU.mult)
                ts(t2[:], t1[:], MIN_LOG, None, ALU.max)
                dve.sem_inc(asked, 1)
                tt(th[:], aim, dt[:], ALU.mult)
                ts(kk[:], th[:], 1.0 / (2 * math.pi), ROUND, ALU.mult, ALU.add)
                ts(kk[:], kk[:], -ROUND, None, ALU.add)
                st.done(v.scalar_tensor_tensor(r[:], kk[:], -TWO_PI_HI, th[:], ALU.mult, ALU.add))
                st.settle()
                st.done(v.scalar_tensor_tensor(r[:], kk[:], -TWO_PI_LO, r[:], ALU.mult, ALU.add))
                st.settle()
                ts(r[:], r[:], 3.1415925, -3.1415925, ALU.min, ALU.max)
                dve.sem_inc(asked, 1)
                dve.wait_ge(act_done, 3)
                tt(t2[:], s2[:], s2[:], ALU.mult)
                ts(rot[:, 0], t2[:], -2.0, 1.0, ALU.mult, ALU.add)
                st.done(v.tensor_copy(rot[:, 1], sn[:]))
                tt(lr[:], mag[:], rot[:, 0], ALU.mult)
                tt(li[:], mag[:], rot[:, 1], ALU.mult)
                ts(lr[:], lr[:], -1.0, None, ALU.add)
                tt(den[:], are, are, ALU.mult)
                tt(t1[:], aim, aim, ALU.mult)
                tt(den[:], den[:], t1[:], ALU.add)
                st.done(v.reciprocal(den[:], den[:]))
                st.settle()
                tt(t1[:], lr[:], are, ALU.mult)
                tt(t2[:], li[:], aim, ALU.mult)
                tt(t1[:], t1[:], t2[:], ALU.add)
                tt(coef[:, 0], t1[:], den[:], ALU.mult)
                tt(t1[:], li[:], are, ALU.mult)
                tt(t2[:], lr[:], aim, ALU.mult)
                tt(t1[:], t1[:], t2[:], ALU.subtract)
                tt(coef[:, 1], t1[:], den[:], ALU.mult)
                small = (t1[:], t2[:])
                cmul(both(r8[:, 0]), both(rot[:]), both(rot[:]), *small)
                cmul(both(r8[:, 1]), both(r8[:, 0]), both(r8[:, 0]), *small)
                cmul(both(r8[:, 0]), both(r8[:, 1]), both(r8[:, 1]), *small)
                v.memset(E[:, 0, :, 0:1], 1.0)
                v.memset(E[:, 1, :, 0:1], 0.0)
                st.done(v.tensor_copy(E[:, :, :, 1:2], r8[:, 0].unsqueeze(3)))
                st.settle()
                m, cur = 2, 0
                while m < CS:
                    cmul(both(r8[:, 1 - cur]), both(r8[:, cur]), both(r8[:, cur]), *small)
                    cur = 1 - cur
                    step = tuple(r8[:, cur, ri].unsqueeze(2).to_broadcast([P, NPD, m]) for ri in range(2))
                    part = tuple(a[:, 0:NPD * m].rearrange("p (n m) -> p n m", m=m) for a in (ta, tb))
                    cmul(both(E[:, :, :, m:2 * m]), both(E[:, :, :, 0:m]), step, *part)
                    m *= 2
                dve.sem_inc(rotations, 1)
                pw = lambda a, b, way=1: tuple(LP[:, ri, :, a:b][:, :, ::way] for ri in range(2))
                one = MID + 1
                v.memset(LP[:, 0, :, one:one + 1], 1.0)
                v.memset(LP[:, 1, :, one:one + 1], 0.0)
                v.tensor_tensor(LP[:, 0, :, one + 1], magc[:], rot[:, 0], ALU.mult)
                v.tensor_tensor(LP[:, 1, :, one + 1], magc[:], rot[:, 1], ALU.mult)
                v.tensor_tensor(LP[:, 0, :, one - 1], inv[:], rot[:, 0], ALU.mult)
                st.done(v.scalar_tensor_tensor(LP[:, 1, :, one - 1], inv[:], -1.0, rot[:, 1], ALU.mult, ALU.mult))
                st.settle()
                tmp = lambda n: tuple(a[:, 0:NPD * n].rearrange("p (n m) -> p n m", m=n) for a in (ta, tb))
                cmul(pw(one + 2, one + 3), pw(one + 1, one + 2), pw(one + 1, one + 2), *tmp(1))
                cmul(pw(one - 2, one - 1), pw(one - 1, one), pw(one - 1, one), *tmp(1))
                wide = lambda x: tuple(a.to_broadcast([P, NPD, 2]) for a in x)
                cmul(pw(one + 3, one + 5), pw(one + 1, one + 3), wide(pw(one + 2, one + 3)), *tmp(2))
                cmul(pw(one - 4, one - 2), pw(one - 2, one), wide(pw(one - 2, one - 1)), *tmp(2))
                cmul(pw(0, 1), pw(1, 2), pw(one - 1, one), *tmp(1))
                st.done(v.tensor_copy(par.last[:], LP[:, :, :, 0]))
                L5 = (lr[:], li[:])
                cmul(L5, tuple(a[:, :, 0] for a in pw(one + MID, one + MID + 1)), tuple(a[:, :, 0] for a in pw(one + 1, one + 2)), *small)
                cmul(both(par.z0), L5, both(h0[:]), *small)
                for dr in range(2):
                    ex = pw(2, NP_, -1) if dr == 0 else pw(2, NP_)
                    ex = tuple(quads(a)[:, :, dr] for a in ex)
                    co = tuple(coef[:, ri].rearrange("p (q d j) -> p q d j", d=2, j=QUAD)[:, :, dr].unsqueeze(3).to_broadcast([P, KC, QUAD, CH]) for ri in range(2))
                    dst = tuple(par.wt[:, :, ri, dr * QUAD:(dr + 1) * QUAD, :] for ri in range(3))
                    part = tuple(a[:, 0:NPD * CH // 2].rearrange("p (q j m) -> p q j m", q=KC, m=CH) for a in (ta, tb))
                    cmul(dst[0:2], ex, co, *part)
                    st.done(v.tensor_scalar(dst[2], dst[1], -1.0, None, ALU.mult))
                    ex = pw(1, NP_ - 1) if dr == 0 else pw(1, NP_ - 1, -1)
                    ex = tuple(quads(a)[:, :, dr] for a in ex)
                    dst = tuple(par.vt[:, :, ri, dr * QUAD:(dr + 1) * QUAD, :] for ri in range(2))
                    v.tensor_copy(dst[0], ex[0])
                    st.done(v.tensor_scalar(dst[1], ex[1], -1.0, None, ALU.mult))


def quads4(a, dr):
    return a[:, :, dr * QUAD:(dr + 1) * QUAD, :]


def s5_scan(nc, sems, cx, d, u, par, y, fin):
    NQ = KC
    with Stage(nc, sems, "s5") as s:
        bc = s.sb("bc", [P, 2, 4, QP, GC])
        W, V = s.sb("W", [P, 2, 2, QP, P]), s.sb("V", [P, 2, 2, QP, P])
        wa, va, pa = s.sb("wa", [P, QP, P]), s.sb("va", [P, QP, P]), s.sb("pa", [P, QP, P])
        WT = s.sb("WT", [P, 2, QP, P])
        MS = s.sb("MS", [P, QP, P])
        uq, ma = s.sb("uq", [P, QP, SLOTS + 1]), s.sb("ma", [P, 2, 2, QUAD, SLOTS])
        W2 = QUAD * SLOTS
        m1, m2, m3, m4, n1, n2, k1, k2 = (s.sb(n, [P, 2, W2]) for n in ("m1", "m2", "m3", "m4", "n1", "n2", "k1", "k2"))
        bs, H, S = (s.sb(n, [P, 2, 2, W2]) for n in ("bs", "H", "S"))
        Y, SF = s.sb("Y", [ROWS, CH, QP, GC]), s.sb("SF", [P, 2, NPD])
        big, X, yp = s.ps("big", [P, 4, 512]), s.ps("X", [P, 2, 512]), s.ps("yp", [P, 2, 512])
        loaded = [s.sem("bc0_loaded"), s.sem("bc1_loaded")]
        own, pool_own = s.sem("dve"), s.sem("pool")
        wr, wi, vr, vi, turned, wtc, params, xdone, hdone, sr, si = (s.sem(n) for n in (
            "w_re", "w_im", "v_re", "v_im", "w_turned", "wt_copied", "params", "x", "h", "s_re", "s_im"))
        mprod, msdone, ysum, ycopied, yturned, ydone, zeroed = (s.sem(n) for n in (
            "m_product", "m_masked", "y_sum", "y_copied", "y_turned", "y_done", "zeroed"))
        pairs = lambda a: a.rearrange("p d (j n) -> p d j n", j=QUAD)
        flat = lambda a: a.rearrange("p a r n -> p (a r) n")
        shape = [P, QP, CH, GC]
        steps = lambda a: a.rearrange("p g (s c) -> p g s c", c=GC)

        def tables(tab, n, k):
            return tab[:, bass.ds(n, 1), k].rearrange("p a g s -> p (a g) s").unsqueeze(3).to_broadcast(shape)

        def chans(b, k):
            return bc[:, b, k].unsqueeze(2).to_broadcast(shape)

        def rot(tab, n, k):
            return tab[:, bass.ds(n, 1), k].rearrange("p a (d j) n -> p (a d) (j n)", d=2)

        with nc.Block() as block:
            @block.sync
            def _(sp):
                def load(n, b):
                    sp.dma_start(bc[:, b], d["s5_bc"][bass.ds(n, 1)].rearrange("a p r g c -> p (a r) g c")).then_inc(loaded[b], 16)

                for b in range(2):
                    load(b, b)
                with sp.Fori(1, NQ // 2) as i:
                    for b in range(2):
                        sp.wait_ge(vr, i * 2 + (b - 1))
                        sp.wait_ge(vi, i * 2 + (b - 1))
                        load(i * 2 + b, b)

            @block.gpsimd
            def _(pool):
                g = nc.gpsimd

                def build(n, b, turn):
                    pool.wait_ge(loaded[b], turn * 16 + 16)
                    for out, tmp, x, tab, ks, op, done, k in ((W, pa, 0, par.wt, (1, 0), ALU.add, wi, 0), (V, pa, 2, par.vt, (1, 0), ALU.subtract, vi, 1)):
                        o = steps(out[:, b, 1])
                        g.tensor_tensor(o, chans(b, x), tables(tab, n, ks[0]), ALU.mult).then_inc(pool_own, 1)
                        g.tensor_tensor(steps(tmp[:]), chans(b, x + 1), tables(tab, n, ks[1]), ALU.mult).then_inc(pool_own, 1)
                        pool.wait_ge(pool_own, n * 6 + 2 * k + 2)
                        g.tensor_tensor(o, o, steps(tmp[:]), op).then_inc(done, 1)
                        pool.wait_ge(done, n + 1)

                def turn_back(n):
                    pool.wait_ge(hdone, n + 1)
                    g.tensor_tensor(k1[:], H[:, :, 1], rot(par.post, n, 0), ALU.mult).then_inc(pool_own, 1)
                    g.tensor_tensor(k2[:], H[:, :, 0], rot(par.post, n, 1), ALU.mult).then_inc(pool_own, 1)
                    pool.wait_ge(pool_own, n * 6 + 6)
                    g.tensor_tensor(S[:, :, 1], k1[:], k2[:], ALU.add).then_inc(si, 1)

                build(0, 0, 0)
                with pool.Fori(0, NQ // 2 - 1) as i:
                    turn_back(i * 2)
                    build(i * 2 + 1, 1, i)
                    turn_back(i * 2 + 1)
                    build(i * 2 + 2, 0, i + 1)
                turn_back(NQ - 2)
                build(NQ - 1, 1, NQ // 2 - 1)
                turn_back(NQ - 1)

            @block.vector
            def _(dve):
                v = nc.vector
                BUILD, QUADN = 4, 14

                def build(n, b, turn):
                    st = Steps(dve, own, n * (BUILD + QUADN))
                    dve.wait_ge(loaded[b], turn * 16 + 16)
                    parts = ((W, wa, 0, par.wt, 2), (V, va, 2, par.vt, 1))
                    for out, tmp, x, tab, minus in parts:
                        st.done(v.tensor_tensor(steps(out[:, b, 0]), chans(b, x), tables(tab, n, 0), ALU.mult))
                        st.done(v.tensor_tensor(steps(tmp[:]), chans(b, x + 1), tables(tab, n, minus), ALU.mult))
                    st.settle()
                    for (out, tmp, *_), done in zip(parts, (wr, vr)):
                        v.tensor_tensor(out[:, b, 0], out[:, b, 0], tmp[:], ALU.add).then_inc(done, 1)
                    assert st.n == BUILD

                def states(n, st):
                    dve.wait_ge(xdone, n + 1)
                    xs = [X[:, ri, 0:2 * W2].rearrange("p (d w) -> p d w", d=2) for ri in range(2)]
                    for out, x, k in ((m1, 0, 0), (m2, 1, 1), (m3, 1, 0), (m4, 0, 1)):
                        ins = v.tensor_tensor(out[:], xs[x], rot(par.pre, n, k), ALU.mult)
                    st.done(ins)
                    st.settle()
                    st.done(v.tensor_tensor(bs[:, :, 0], m1[:], m2[:], ALU.add))
                    st.done(v.tensor_tensor(bs[:, :, 1], m3[:], m4[:], ALU.subtract))
                    st.settle()
                    for dr in range(2):
                        slot = CP + 1 if dr == 0 else SLOTS - 1
                        at = bass.ds(n * QP + dr * QUAD, QUAD)
                        st.done(v.tensor_copy(bs[:, dr].rearrange("p r (j n) -> p r j n", j=QUAD)[:, :, :, slot], par.z0[:, :, at]))
                    st.settle()
                    for dr in range(2):
                        way = -1 if dr else 1
                        all_ = lambda a: a.rearrange("p r w -> p (r w)")[:, ::way]
                        a = ma[:, dr].rearrange("p r j n -> p (r j n)")[:, ::way]
                        ins = v.tensor_tensor_scan(all_(H[:, dr]), a, all_(bs[:, dr]), 0.0, ALU.mult, ALU.add)
                        if dr == 0:
                            st.done(ins)
                    ins.then_inc(hdone, 1)
                    st.settle()
                    dve.wait_ge(hdone, n + 1)
                    st.done(v.tensor_tensor(n1[:], H[:, :, 0], rot(par.post, n, 0), ALU.mult))
                    st.done(v.tensor_tensor(n2[:], H[:, :, 1], rot(par.post, n, 1), ALU.mult))
                    st.settle()
                    v.tensor_tensor(S[:, :, 0], n1[:], n2[:], ALU.subtract).then_inc(sr, 1)

                def mask(n, st):
                    dve.wait_ge(mprod, n + 1)
                    for dr, out in ((0, MS), (1, wa)):
                        src = big[:, 2 * dr:2 * dr + 2, :].rearrange("p b (g m) -> p (b g) m", m=P)
                        st.done(v.tensor_tensor(out[:], src, par.masks[:, dr].unsqueeze(1).to_broadcast([P, QP, P]), ALU.mult))
                    st.settle()
                    v.tensor_tensor(MS[:], MS[:], wa[:], ALU.add).then_inc(msdone, 1)
                    dve.wait_ge(msdone, n + 2)

                def outputs(n):
                    dve.wait_ge(yturned, n + 1)
                    src = X[:, 0, 0:CH * ROWS].rearrange("p (t k) -> p k t", t=CH)
                    for at, rows in ((0, slice(0, CP)), (TP, slice(CP + 1, ROWS))):
                        toks = slice(at, at + (rows.stop - rows.start) * CH)
                        a, o = (z[:, bass.ds(n, 1), toks].rearrange("p a (k t) -> p (a k) t", t=CH) for z in (u, y))
                        ins = v.scalar_tensor_tensor(o, a, par.dskip[:, bass.ds(n, 1)], src[:, rows], ALU.mult, ALU.add)
                    ins.then_inc(ydone, 1)

                def quad(n):
                    st = Steps(dve, own, n * (BUILD + QUADN) + BUILD)
                    states(n, st)
                    mask(n, st)
                    for _ in range(QUADN - st.n):
                        dve.sem_inc(own, 1)

                v.memset(ma[:], 0.0).then_inc(zeroed, 1)
                dve.sem_inc(msdone, 1)
                dve.sem_inc(ydone, 1)
                build(0, 0, 0)
                with dve.Fori(0, NQ // 2 - 1) as i:
                    quad(i * 2)
                    build(i * 2 + 1, 1, i)
                    outputs(i * 2)
                    quad(i * 2 + 1)
                    build(i * 2 + 2, 0, i + 1)
                    outputs(i * 2 + 1)
                quad(NQ - 2)
                build(NQ - 1, 1, NQ // 2 - 1)
                outputs(NQ - 2)
                quad(NQ - 1)
                outputs(NQ - 1)
                st = Steps(dve, own, NQ * (BUILD + QUADN))
                a, b = par.last, SF
                x, y_ = m1[:].rearrange("p d w -> p (d w)")[:, 0:NPD], m2[:].rearrange("p d w -> p (d w)")[:, 0:NPD]
                v.tensor_tensor(x, a[:, 1], b[:, 1], ALU.mult)
                v.tensor_tensor(y_, a[:, 1], b[:, 0], ALU.mult)
                v.tensor_tensor(fin[:, 0], a[:, 0], b[:, 0], ALU.mult)
                st.done(v.tensor_tensor(fin[:, 1], a[:, 0], b[:, 1], ALU.mult))
                st.settle()
                v.tensor_tensor(fin[:, 0], fin[:, 0], x, ALU.subtract)
                v.tensor_tensor(fin[:, 1], fin[:, 1], y_, ALU.add)

            @block.scalar
            def _(act):
                act.wait_ge(zeroed, 1)
                with act.Fori(0, NQ) as n:
                    nc.scalar.activation(uq[:], par.uc[:, bass.ds(n * QP, QP), :], ACT.Copy)
                    for dr in range(2):
                        m8 = par.mag8[:, bass.ds(n, 1), dr * QUAD:(dr + 1) * QUAD]
                        for at, k in SEQS:
                            at = at + 1 - dr
                            src = m8.unsqueeze(3).to_broadcast([P, 1, QUAD, k]).rearrange("p a j k -> p (a j) k")
                            for ri in range(2):
                                ins = nc.scalar.activation(ma[:, dr, ri, :, at:at + k], src, ACT.Copy)
                    ins.then_inc(params, 1)
                    for rnd in range(4):
                        act.wait_ge(turned, n * 4 + rnd + 1)
                        ri, dr = rnd // 2, rnd % 2
                        nc.scalar.activation(WT[:, ri, dr * QUAD:(dr + 1) * QUAD, :].rearrange("p j m -> p (j m)"), big[:, rnd, :], ACT.Copy).then_inc(wtc, 1)
                    act.wait_ge(sr, n + 1)
                    act.wait_ge(si, n + 1)
                    for dr in range(2):
                        slot = CP if dr == 0 else 0
                        src = S[:, dr].rearrange("p r (j n) -> p r j n", j=QUAD)[:, :, :, slot]
                        nc.scalar.activation(SF[:, :, bass.ds(n * QP + dr * QUAD, QUAD)], src, ACT.Copy)
                    act.wait_ge(ysum, n + 1)
                    for gg in range(2):
                        src = yp[0:ROWS, gg, :].rearrange("k (j t c) -> k j t c", j=QUAD, t=CH)
                        dst = Y[:].rearrange("k t (j w) c -> k w j t c", w=2)[:, gg]
                        nc.scalar.activation(dst, src, ACT.Copy).then_inc(ycopied, 1)

            @block.tensor
            def _(pe):
                def quad(n, b):
                    pe.wait_ge(wr, n + 1)
                    pe.wait_ge(wi, n + 1)
                    pe.wait_ge(msdone, n + 1)
                    for rnd in range(4):
                        ri, dr = rnd // 2, rnd % 2
                        for j in range(QUAD):
                            mm = pe.transpose(big[:, rnd, j * P:(j + 1) * P], W[:, b, ri, dr * QUAD + j, :], cx.ident)
                        mm.then_inc(turned, 1)
                    pe.wait_ge(wtc, n * 4 + 4)
                    pe.wait_ge(params, n + 1)
                    pe.wait_ge(ydone, n + 1)
                    for g in range(QP):
                        dr, j = g // QUAD, g % QUAD
                        for gg in range(2):
                            rows = slice(64 * gg, 64 * gg + 64)
                            for ri in range(2):
                                mm = pe.matmul(X[rows, ri, g * SLOTS:(g + 1) * SLOTS], WT[:, ri, g, rows], uq[:, 2 * j + gg, dr:dr + SLOTS], start=True, stop=True)
                    mm.then_inc(xdone, 1)
                    pe.wait_ge(vr, n + 1)
                    pe.wait_ge(vi, n + 1)
                    for dr in range(2):
                        for j in range(QUAD):
                            for gg in range(2):
                                rows = slice(64 * gg, 64 * gg + 64)
                                for ri in range(2):
                                    mm = pe.matmul(big[:, 2 * dr + gg, j * P:(j + 1) * P], W[rows, b, ri, dr * QUAD + j, :], V[rows, b, ri, dr * QUAD + j, :], start=ri == 0, stop=ri == 1)
                    mm.then_inc(mprod, 1)
                    pe.wait_ge(msdone, n + 2)
                    pe.wait_ge(sr, n + 1)
                    pe.wait_ge(si, n + 1)
                    for j in range(QUAD):
                        o = [yp[0:ROWS, gg, j * P:(j + 1) * P] for gg in range(2)]
                        for gg in range(2):
                            pe.matmul(o[gg], uq[:, 2 * j + gg, 1:1 + ROWS], MS[:, gg * QUAD + j, :], start=True, stop=False)
                        for dr in range(2):
                            for ri in range(2):
                                for gg in range(2):
                                    rows = slice(64 * gg, 64 * gg + 64)
                                    st = S[rows, dr, ri, j * SLOTS + dr:j * SLOTS + dr + ROWS]
                                    mm = pe.matmul(o[gg], st, V[rows, b, ri, dr * QUAD + j, :], start=False, stop=dr == 1 and ri == 1)
                    mm.then_inc(ysum, 1)
                    pe.wait_ge(ycopied, n * 2 + 2)
                    for t in range(CH):
                        mm = pe.matmul(X[:, 0, t * ROWS:(t + 1) * ROWS], Y[:, t].rearrange("k g c -> k (g c)"), cx.ident[0:ROWS, 0:ROWS], start=True, stop=True)
                    mm.then_inc(yturned, 1)

                with pe.Fori(0, NQ // 2) as i:
                    for b in range(2):
                        quad(i * 2 + b, b)


def glu_inputs(nc, sems, cx, y, hi, lo):
    with Stage(nc, sems, "gin") as s:
        g = s.sb("g", [P, KC, T])
        gelud, own = s.sem("gelu"), s.sem("dve")
        with nc.Block() as block:
            @block.scalar
            def _(act):
                for k in range(KC):
                    nc.scalar.activation(g[:, k], y[:, k], ACT.Gelu_apprx_tanh).then_inc(gelud, 1)

            @block.vector
            def _(dve):
                for k in range(KC):
                    dve.wait_ge(gelud, k + 1)
                    ins = hi_part(nc, hi[:, k], g[:, k])
                ins.then_inc(own, 1)
                dve.wait_ge(own, 1)
                lo_part(nc, lo[:], g[:], hi[:])


def glu(nc, sems, cx, zz, m):
    with Stage(nc, sems, "glu") as s:
        sg = s.sb("sg", [P, KC, T])
        sig = s.sem("sigmoid")
        with nc.Block() as block:
            @block.scalar
            def _(act):
                for k in range(KC):
                    nc.scalar.activation(sg[:, k], zz[:, KC + k], ACT.Sigmoid).then_inc(sig, 1)

            @block.vector
            def _(dve):
                for k in range(KC):
                    dve.wait_ge(sig, k + 1)
                    nc.vector.tensor_tensor(m[:, k], sg[:, k], zz[:, k], ALU.mult)


class Context:

    def mod(self, layer, j):
        return self.modT[:, layer * MODS + j * KC:layer * MODS + (j + 1) * KC, :]


class S5Parameters:

    def __init__(self, s):
        self.dskip, self.masks = s.sb("dskip", [P, KC]), s.sb("masks", [P, 2, P])
        self.mag8, self.z0, self.last = s.sb("mag8", [P, KC, QP]), s.sb("z0", [P, 2, NPD]), s.sb("last", [P, 2, NPD])
        self.wt, self.vt = s.sb("wt", [P, KC, 3, QP, CH]), s.sb("vt", [P, KC, 2, QP, CH])
        self.pre, self.post = s.sb("pre", [P, KC, 2, QP, SLOTS]), s.sb("post", [P, KC, 2, QP, SLOTS])
        self.uc = s.sb("uc", [P, 2 * NPAIR, SLOTS + 1])


def peer(nc, sems, cx, d, layer):
    groups = NKEYS // IB
    with Stage(nc, sems, f"peer{layer}") as s:
        hi, lo = s.sb("hi", [P, KC, T]), s.sb("lo", [P, KC, T])
        picks = s.sb("i1T", [P, T], F16), s.sb("i2T", [P, T], F16), s.sb("gh", [P, T]), s.sb("gl", [P, T])
        A = [s.sb("A0", [P, IB, T])]
        norm(nc, sems, cx, f"n{layer}1", hi, lo, layer, 1)
        with Stage(nc, sems, f"pq{layer}") as s2:
            q = s2.sb("q", [P, 2 * PH, T])
            linear(nc, sems, f"ql{layer}", d["w_query"][layer], 2 * PH, hi, lo, q)
            retrieve(nc, sems, cx, f"ret{layer}", d, layer, q, *picks, hi, lo, A[0])
        acc = s.ps("acc", [P, 2 * NT, 512])
        with Stage(nc, sems, f"pe{layer}") as s3:
            A.append(s3.sb("A1", [P, IB, T]))
            with nc.Block() as block:
                @block.vector
                def _(dve):
                    nc.vector.memset(acc[:], 0.0)
            for step in range(1, groups + 2):
                of = lambda g: g if 0 <= g < groups else None
                experts(nc, sems, cx, f"ex{layer}{step}", d, layer, hi, lo, picks, A, acc,
                        score=of(step), gate=of(step - 1), value=of(step - 2))
        add_experts(nc, sems, cx, f"ad{layer}", layer, acc)


def build(nc, d):
    sems = Semaphores(nc)
    with Stage(nc, sems, "g") as g:
        cx = Context()
        cx.const, cx.x = g.sb("const", [P, C_KEEP]), g.sb("x", [P, KC, T])
        cx.modT, cx.scale = g.sb("modT", [P, 2 * MODS, 2]), g.sb("scale", [P, 2, 2, KC, 2])
        cx.ones, cx.eps, cx.finalg = g.sb("ones", [P, P]), g.sb("eps", [P, 1]), g.sb("finalg", [P, KC])
        cx.iota = g.sb("iota", [P, P], F16)
        cx.ident = cx.const[:, C_ID:C_ID + P]
        modulation(nc, sems, cx, d)

        with Stage(nc, sems, "l0") as s:
            hi, lo, y, v = s.sb("hi", [P, KC, T]), s.sb("lo", [P, KC, T]), s.sb("y", [P, 18, T]), s.sb("v", [P, NT, 2, 512])
            cx.const0 = s.sb("const0", [P, C_ALL - C_KEEP])
            norm(nc, sems, cx, "n00", hi, lo, 0, 0)
            linear(nc, sems, "in0", d["w_in0"], 18, hi, lo, y)
            values(nc, sems, cx, d, hi, lo, v)
            with Stage(nc, sems, "o0") as s2:
                o = s2.sb("o", [P, HEADS, T])
                rope(nc, sems, cx, y)
                attention(nc, sems, cx, d, y, v, o)
                head_norm(nc, sems, cx, "dan", o, d["subln_g"], 1.0 - (0.8 - 0.6 * math.exp(-0.3 * 0)), hi[:, 0:HEADS], lo[:, 0:HEADS])
                gla(nc, sems, cx, d, y, v, o)
                head_norm(nc, sems, cx, "gln", o, d["gla_g"], 1.0, hi[:, HEADS:KC], lo[:, HEADS:KC], r=y[:, 12:16])
            m = y[:, 0:KC]
            linear(nc, sems, "out0", d["w_out0"], KC, hi, lo, m)
            residual(nc, sems, cx, "r0", m, 0)
        sems.clear()
        peer(nc, sems, cx, d, 0)
        sems.clear()

        with Stage(nc, sems, "l1") as s:
            zz = s.sb("zz", [P, 2 * KC, T])
            u, y = zz[:, 0:KC], zz[:, KC:2 * KC]
            with Stage(nc, sems, "i1") as s2:
                hi, lo = s2.sb("hi", [P, KC, T]), s2.sb("lo", [P, KC, T])
                norm(nc, sems, cx, "n10", hi, lo, 1, 0)
                linear(nc, sems, "in1", d["s5_w_in"], KC, hi, lo, u)
            with Stage(nc, sems, "s5o") as s2:
                par = S5Parameters(s2)
                fin = s2.sb("fin", [P, 2, NPD])
                stored = s2.sem("stored")
                s5_prepare(nc, sems, cx, d, u, par)
                s5_scan(nc, sems, cx, d, u, par, y, fin)
                with nc.Block() as block:
                    @block.sync
                    def _(sp):
                        sp.dma_start(d["new_s5"], fin[:]).then_inc(stored, 16)
                        sp.wait_ge(stored, 16)
            hi, lo = s.sb("hi", [P, KC, T]), s.sb("lo", [P, KC, T])
            glu_inputs(nc, sems, cx, y, hi, lo)
            linear(nc, sems, "out1", d["s5_w_out"], 2 * KC, hi, lo, zz)
            m = s.sb("m", [P, KC, T])
            glu(nc, sems, cx, zz, m)
            residual(nc, sems, cx, "r1", m, 1)
        sems.clear()
        peer(nc, sems, cx, d, 1)
        norm(nc, sems, cx, "fin", None, None, final=d["y"])


def residual(nc, sems, cx, name, m, layer):
    with nc.Block() as block:
        @block.vector
        def _(dve):
            for k in range(KC):
                for c, a, b in SEGS:
                    x = cx.x[:, k, a:b]
                    nc.vector.scalar_tensor_tensor(x, m[:, k, a:b], cx.mod(layer, 2)[:, k, c:c + 1], x, ALU.mult, ALU.add)


def col_tiles(w):
    k, n = w.shape
    return np.ascontiguousarray(w.reshape(k // P, P, n // P, P).transpose(2, 1, 0, 3))


def on_partitions(v):
    return np.ascontiguousarray(np.moveaxis(v.reshape(v.shape[:-1] + (-1, P)), -1, 0))


def by_pair(a):
    a = a.reshape((2, KC, QUAD, 2, 64) + a.shape[3:])
    return np.ascontiguousarray(np.moveaxis(a, (3, 4, 1), (0, 1, 2)).reshape((P, KC, 2, QUAD) + a.shape[5:]))


def layouts(i):
    d = {}
    x = np.concatenate([i["x_prompt"][0], i["x_sample"][0]], 0)
    d["x"] = np.ascontiguousarray(x.reshape(T, KC, P).transpose(2, 1, 0))
    d["cond"] = np.ascontiguousarray(np.stack([i["c_ctx"], i["c"][0]], 0).reshape(2, KC, P).transpose(2, 1, 0))
    d["consts"] = constants()
    d["ada_w"] = np.ascontiguousarray(i["ada_w"].reshape(2, KC, P, 12, 512).transpose(0, 3, 2, 1, 4)).reshape(24, P, KC, 512)
    d["ada_b"] = on_partitions(i["ada_b"])
    d["norm_g"] = on_partitions(i["norm_g"].reshape(4, D))
    d["final_g"] = on_partitions(i["final_norm_g"])
    w = i["mix0_w_in"][0]
    low = np.zeros((D, 2 * P), np.float32)
    low[:, 0:16], low[:, P:P + 16] = w[:, 3072:3088], w[:, 3088:3104]
    d["w_in0"] = col_tiles(np.concatenate([w[:, 0:1024], w[:, 1536:2048], w[:, 2560:3072], low], 1))
    vw = np.stack([w[:, 1024:1536], w[:, 2048:2560]])
    d["w_v"] = np.ascontiguousarray(vw.reshape(2, KC, P, 512).transpose(0, 2, 1, 3))
    d["w_out0"] = col_tiles(i["mix0_w_out"][0])
    d["da_lam"] = np.ascontiguousarray(np.broadcast_to(i["da_lam"], (P, 4, 64)))
    d["subln_g"] = i["da_subln_g"].reshape(P, 1)
    d["gla_g"] = i["gla_norm_g"].reshape(P, 1)
    d["cache_k"] = np.ascontiguousarray(i["cache_da_k"][0, 0].reshape(P, HEADS, P).transpose(2, 1, 0))
    d["cache_v"] = i["cache_da_v"][0, 0].reshape(P, 512)
    d["gate_up"] = np.ascontiguousarray(i["gla_gate_up"][0].transpose(1, 0, 2))
    d["gate_bias"] = np.ascontiguousarray(i["gla_gate_bias"][0].reshape(4, P).T)
    d["state_gla"] = np.ascontiguousarray(i["state_gla"][0, 0].reshape(4, P, P).transpose(1, 0, 2))
    d["s5_w_in"], d["s5_w_out"] = col_tiles(i["s5_w_in"][0]), col_tiles(i["s5_w_out"][0])
    dt = np.broadcast_to(i["s5_log_dt"][0][:, :, None], (2, 64, 64))
    d["s5_par"] = np.stack([by_pair(a).reshape(P, NPD) for a in (i["s5_a_re"][0], i["s5_a_im"][0], dt)], 1)
    d["state_s5"] = np.stack([by_pair(i["state_s5"][0, 0, ..., r]).reshape(P, NPD) for r in range(2)], 1)
    d["s5_d"] = on_partitions(i["s5_d"][0])
    bc = [i["s5_b_re"][0], i["s5_b_im"][0], i["s5_c_re"][0].transpose(0, 1, 3, 2), i["s5_c_im"][0].transpose(0, 1, 3, 2)]
    bc = np.stack([by_pair(a).reshape(P, KC, QP, GC) for a in bc], 2)
    d["s5_bc"] = np.ascontiguousarray(bc.transpose(1, 0, 2, 3, 4))
    step = np.arange(P) // GC
    masks = np.stack([step[:, None] <= step[None], step[:, None] >= step[None]], 1)
    d["s5_masks"] = masks.astype(np.float32)
    d["w_query"] = np.stack([col_tiles(w) for w in i["peer_w_query"]])
    d["sub_keys"] = np.ascontiguousarray(i["peer_sub_keys"].reshape(2, 2 * PH, NKEYS, P).transpose(0, 3, 1, 2))
    u = i["peer_u"].reshape(2, NKEYS, NKEYS, KC, P)
    d["peer_u"] = np.ascontiguousarray(u.transpose(0, 2, 4, 3, 1)).reshape(2, NKEYS, P, D)
    d["peer_v"] = np.ascontiguousarray(i["peer_v"].reshape(2, NKEYS, NKEYS, D).transpose(0, 2, 1, 3))
    return d


OUTS = {"y": (P, KC, T), "new_k": (P, HEADS, P), "new_v": (P, 512), "new_gla": (P, 4, P), "new_s5": (P, 2, NPD)}


def kernel(**inputs):
    import concourse.bacc as bacc
    from concourse.bass_utils import run_bass_kernel_spmd

    nc = bacc.Bacc("TRN2", target_bir_lowering=False, num_devices=1)
    arrays = layouts({k: np.asarray(v) for k, v in inputs.items()})
    d = {k: nc.dram_tensor(f"in_{k}", a.shape, F32, kind="ExternalInput").ap() for k, a in arrays.items()}
    d.update({k: nc.dram_tensor(f"out_{k}", s, F32, kind="ExternalOutput").ap() for k, s in OUTS.items()})
    build(nc, d)
    r = run_bass_kernel_spmd(nc, [{f"in_{k}": a for k, a in arrays.items()}], core_ids=[0]).results[0]
    y = r["out_y"].transpose(2, 1, 0).reshape(T, D)
    s5 = r["out_new_s5"].reshape(2, 64, 2, KC, 2, QUAD)
    return (
        y[None, :TP], y[None, TP:],
        r["out_new_k"].reshape(1, 1, P, 2 * HEADS, 64),
        r["out_new_v"].reshape(1, 1, P, HEADS, P),
        r["out_new_gla"].transpose(1, 0, 2).reshape(1, 1, 2, HEADS, 64, P),
        np.ascontiguousarray(s5.transpose(4, 3, 5, 0, 1, 2)).reshape(1, 1, 2, 64, 64, 2),
    )
```
